# Optimizing a Trainium2 kernel written in Bass

```python
import jax, jax.numpy as jnp
from jax import lax
import numpy as np

D_MODEL = 1024
BATCH = 1
SEQ = 256
DEPTH = 1

GDN_HEADS = 4
GDN_HEAD_DIM = 128
GDN_WIDTH = GDN_HEADS * GDN_HEAD_DIM
GDN_CHUNK = 64
LRU_WIDTH = D_MODEL // 2
LRU_BLOCKS = 8
LRU_BLOCK = LRU_WIDTH // LRU_BLOCKS
LRU_C = 8.0
CONV_WIDTH = 4
N_EXPERTS = 32
TOP_K = 4
D_FF = D_MODEL
SWIGLU_ALPHA = 1.702
SWIGLU_LIMIT = 7.0
MOE_BLOCK = 256
EPS = 1e-6

IN_SPLITS = (GDN_WIDTH, GDN_WIDTH, GDN_WIDTH, GDN_WIDTH, GDN_HEADS, GDN_HEADS,
             LRU_WIDTH, LRU_WIDTH, D_MODEL, D_MODEL)
D_IN = sum(IN_SPLITS)

kernel_name = 'hybrid_gdn_rglru_moe_block'

def rms_norm(x, gain):
    xf = x.astype(jnp.float32)
    y = xf * lax.rsqrt(jnp.mean(xf * xf, axis=-1, keepdims=True) + EPS)
    return (y * gain.astype(jnp.float32)).astype(x.dtype)

def causal_depthwise_conv(x, w):
    return lax.conv_general_dilated(
        x, w[:, None, :].astype(x.dtype), window_strides=(1,),
        padding=[(CONV_WIDTH - 1, 0)], dimension_numbers=('NWC', 'WIO', 'NWC'),
        feature_group_count=x.shape[-1])

def l2_normalize(t):
    return t * lax.rsqrt(jnp.sum(t * t, axis=-1, keepdims=True) + EPS)

def _to_chunks(t):
    b, s, h = t.shape[:3]
    t = t.reshape(b, s // GDN_CHUNK, GDN_CHUNK, h, *t.shape[3:])
    return jnp.moveaxis(t, 3, 1)

def gated_delta_rule(q, k, v, g, beta):
    b, s, h, dk = q.shape
    dv = v.shape[-1]
    q = _to_chunks(q * (dk ** -0.5))
    k = _to_chunks(k)
    v = _to_chunks(v)
    g = _to_chunks(g)
    beta = _to_chunks(beta)
    c = GDN_CHUNK
    incl = jnp.tril(jnp.ones((c, c), bool))
    strict = jnp.tril(jnp.ones((c, c), bool), -1)
    gc = jnp.cumsum(g, axis=-1)
    diff = gc[..., :, None] - gc[..., None, :]
    decay = jnp.where(incl, jnp.exp(jnp.where(incl, diff, 0.0)), 0.0)
    kb = k * beta[..., None]
    a_mat = jnp.where(strict, jnp.einsum('bhncd,bhnsd->bhncs', kb, k) * decay, 0.0)
    eye = jnp.eye(c, dtype=q.dtype)
    t_mat = lax.linalg.triangular_solve(eye + a_mat, jnp.broadcast_to(eye, a_mat.shape),
                                        left_side=True, lower=True, unit_diagonal=True)
    u = jnp.matmul(t_mat, v * beta[..., None])
    w = jnp.matmul(t_mat, kb * jnp.exp(gc)[..., None])
    qk = jnp.where(incl, jnp.einsum('bhncd,bhnsd->bhncs', q, k) * decay, 0.0)
    q_dec = q * jnp.exp(gc)[..., None]
    k_dec = k * jnp.exp(gc[..., -1:] - gc)[..., None]
    g_last = jnp.exp(gc[..., -1])
    xs = tuple(jnp.moveaxis(t, 2, 0) for t in (w, u, q_dec, k_dec, qk, g_last))

    def step(state, inp):
        w_c, u_c, qd_c, kd_c, qk_c, gl_c = inp
        v_new = u_c - jnp.einsum('bhcd,bhde->bhce', w_c, state)
        o_c = (jnp.einsum('bhcd,bhde->bhce', qd_c, state)
               + jnp.einsum('bhcs,bhse->bhce', qk_c, v_new))
        state = state * gl_c[..., None, None] + jnp.einsum('bhcd,bhce->bhde', kd_c, v_new)
        return state, o_c

    state0 = jnp.zeros((b, h, dk, dv), q.dtype)
    _, o = lax.scan(step, state0, xs)
    return jnp.transpose(o, (1, 0, 3, 2, 4)).reshape(b, s, h, dv)

def gdn_branch(q, k, v, z, b_in, a_in, conv_w, a_log, dt_bias, norm_w):
    bsz, s, _ = q.shape
    qkv = jax.nn.silu(causal_depthwise_conv(jnp.concatenate([q, k, v], axis=-1), conv_w))
    q, k, v = jnp.split(qkv, 3, axis=-1)
    heads = lambda t: t.reshape(bsz, s, GDN_HEADS, GDN_HEAD_DIM).astype(jnp.float32)
    q = l2_normalize(heads(q))
    k = l2_normalize(heads(k))
    v = heads(v)
    beta = jax.nn.sigmoid(b_in.astype(jnp.float32))
    g = -jnp.exp(a_log.astype(jnp.float32)) * jax.nn.softplus(
        a_in.astype(jnp.float32) + dt_bias.astype(jnp.float32))
    o = gated_delta_rule(q, k, v, g, beta)
    o = (o * lax.rsqrt(jnp.mean(o * o, axis=-1, keepdims=True) + EPS)
         * norm_w.astype(jnp.float32) * jax.nn.silu(heads(z)))
    return o.reshape(bsz, s, GDN_WIDTH).astype(q_dtype_of(z))

def q_dtype_of(t):
    return t.dtype

def rglru_branch(xb, yb, conv_w, conv_b, w_a, b_a, w_x, b_x, lam):
    bsz, s, _ = xb.shape
    xc = causal_depthwise_conv(xb, conv_w) + conv_b
    xblk = xc.reshape(bsz, s, LRU_BLOCKS, LRU_BLOCK)
    r = jax.nn.sigmoid((jnp.einsum('bsnc,ncd->bsnd', xblk, w_a).reshape(bsz, s, LRU_WIDTH)
                        + b_a).astype(jnp.float32))
    i = jax.nn.sigmoid((jnp.einsum('bsnc,ncd->bsnd', xblk, w_x).reshape(bsz, s, LRU_WIDTH)
                        + b_x).astype(jnp.float32))
    log_a = -LRU_C * r * jax.nn.softplus(-lam.astype(jnp.float32))
    a = jnp.exp(log_a)
    mult = jnp.sqrt(jnp.maximum(-jnp.expm1(2.0 * log_a), 0.0))
    bterm = mult * (i * xc.astype(jnp.float32))

    def combine(left, right):
        a_l, b_l = left
        a_r, b_r = right
        return a_l * a_r, a_r * b_l + b_r

    _, hseq = lax.associative_scan(combine, (a, bterm), axis=1)
    y = hseq * jax.nn.gelu(yb.astype(jnp.float32))
    return y.astype(xb.dtype)

def swiglu_clamped(u):
    u_glu = jnp.minimum(u[..., ::2], SWIGLU_LIMIT)
    u_lin = jnp.clip(u[..., 1::2], -SWIGLU_LIMIT, SWIGLU_LIMIT)
    return u_glu * jax.nn.sigmoid(SWIGLU_ALPHA * u_glu) * (u_lin + 1.0)

def moe_ffn(h, w_router, b_router, w1, b1, w2, b2):
    bsz, s, d = h.shape
    n_tok = bsz * s
    hf = h.reshape(n_tok, d)
    logits = hf.astype(jnp.float32) @ w_router.astype(jnp.float32) + b_router.astype(jnp.float32)
    top_val, top_idx = lax.top_k(logits, TOP_K)
    gate = jax.nn.softmax(top_val, axis=-1)
    n_assign = n_tok * TOP_K
    flat_e = top_idx.reshape(-1).astype(jnp.int32)
    flat_tok = jnp.arange(n_assign, dtype=jnp.int32) // TOP_K
    flat_w = gate.reshape(-1)
    order = jnp.argsort(flat_e)
    sorted_e = flat_e[order]
    counts = jnp.bincount(flat_e, length=N_EXPERTS)
    padded = (counts + MOE_BLOCK - 1) // MOE_BLOCK * MOE_BLOCK
    start = jnp.cumsum(counts) - counts
    pstart = jnp.cumsum(padded) - padded
    dest = pstart[sorted_e] + jnp.arange(n_assign, dtype=jnp.int32) - start[sorted_e]
    n_blocks = -(-n_assign // MOE_BLOCK) + N_EXPERTS
    n_slots = n_blocks * MOE_BLOCK
    slot_tok = jnp.full((n_slots,), n_tok, jnp.int32).at[dest].set(flat_tok[order])
    slot_w = jnp.zeros((n_slots,), h.dtype).at[dest].set(flat_w[order].astype(h.dtype))
    block_e = jnp.minimum(
        jnp.searchsorted(jnp.cumsum(padded), jnp.arange(n_blocks) * MOE_BLOCK, side='right'),
        N_EXPERTS - 1)
    h_pad = jnp.concatenate([hf, jnp.zeros((1, d), h.dtype)], axis=0)
    xs = h_pad[slot_tok].reshape(n_blocks, MOE_BLOCK, d)

    def expert_block(args):
        xblk, e = args
        u = xblk @ w1[e] + b1[e]
        return swiglu_clamped(u) @ w2[e] + b2[e]

    ys = lax.map(expert_block, (xs, block_e)).reshape(n_slots, d)
    out = jnp.zeros((n_tok + 1, d), h.dtype).at[slot_tok].add(ys * slot_w[:, None])
    return out[:n_tok].reshape(bsz, s, d)

def setup_inputs(seed: int = 0) -> dict:
    key = jax.random.key(seed)
    ks = jax.random.split(key, 32)
    f32 = jnp.float32
    nrm = lambda k, shape, scale: jax.random.normal(k, shape, f32) * scale
    L, D, E, F = DEPTH, D_MODEL, N_EXPERTS, D_FF
    a_init = jax.random.uniform(ks[8], (L, GDN_HEADS), f32, 1.0, 16.0)
    dt = jnp.exp(jax.random.uniform(ks[9], (L, GDN_HEADS), f32, float(np.log(1e-3)), float(np.log(0.1))))
    a_pow = jax.random.uniform(ks[17], (L, LRU_WIDTH), f32, 0.9, 0.999)
    a_lru = a_pow ** (1.0 / LRU_C)
    return {
        'x': nrm(ks[0], (BATCH, SEQ, D), 1.0),
        'c': nrm(ks[1], (BATCH, D), 1.0),
        'w_ada': nrm(ks[2], (L, D, 6 * D), D ** -0.5),
        'b_ada': nrm(ks[3], (L, 6 * D), 0.01),
        'norm_mix': 1.0 + nrm(ks[4], (L, D), 0.01),
        'norm_ffn': 1.0 + nrm(ks[5], (L, D), 0.01),
        'w_in': nrm(ks[6], (L, D, D_IN), D ** -0.5),
        'gdn_conv_w': nrm(ks[7], (L, CONV_WIDTH, 3 * GDN_WIDTH), CONV_WIDTH ** -0.5),
        'gdn_a_log': jnp.log(a_init),
        'gdn_dt_bias': dt + jnp.log(-jnp.expm1(-dt)),
        'gdn_norm_w': 1.0 + nrm(ks[10], (L, GDN_HEAD_DIM), 0.01),
        'lru_conv_w': nrm(ks[11], (L, CONV_WIDTH, LRU_WIDTH), CONV_WIDTH ** -0.5),
        'lru_conv_b': nrm(ks[12], (L, LRU_WIDTH), 0.01),
        'lru_w_a': nrm(ks[13], (L, LRU_BLOCKS, LRU_BLOCK, LRU_BLOCK), LRU_BLOCK ** -0.5),
        'lru_b_a': nrm(ks[14], (L, LRU_WIDTH), 0.01),
        'lru_w_x': nrm(ks[15], (L, LRU_BLOCKS, LRU_BLOCK, LRU_BLOCK), LRU_BLOCK ** -0.5),
        'lru_b_x': nrm(ks[16], (L, LRU_WIDTH), 0.01),
        'lru_lambda': jnp.log(a_lru) - jnp.log1p(-a_lru),
        'w_branch_gdn': nrm(ks[18], (L, GDN_WIDTH, D), GDN_WIDTH ** -0.5),
        'w_branch_lru': nrm(ks[19], (L, LRU_WIDTH, D), LRU_WIDTH ** -0.5),
        'w_out': nrm(ks[20], (L, D, D), D ** -0.5),
        'w_router': nrm(ks[21], (L, D, E), D ** -0.5),
        'b_router': nrm(ks[22], (L, E), 0.01),
        'w1': nrm(ks[23], (L, E, D, 2 * F), D ** -0.5),
        'b1': nrm(ks[24], (L, E, 2 * F), 0.01),
        'w2': nrm(ks[25], (L, E, F, D), F ** -0.5),
        'b2': nrm(ks[26], (L, E, D), 0.01),
        'norm_final': 1.0 + nrm(ks[27], (D,), 0.01),
    }

def reference(x, c, w_ada, b_ada, norm_mix, norm_ffn, w_in, gdn_conv_w, gdn_a_log, gdn_dt_bias,
              gdn_norm_w, lru_conv_w, lru_conv_b, lru_w_a, lru_b_a, lru_w_x, lru_b_x, lru_lambda,
              w_branch_gdn, w_branch_lru, w_out, w_router, b_router, w1, b1, w2, b2, norm_final):
    split_pts = tuple(int(p) for p in np.cumsum(IN_SPLITS)[:-1])
    c_act = jax.nn.silu(c)
    for l in range(DEPTH):
        mod = c_act @ w_ada[l] + b_ada[l]
        shift_m, scale_m, gate_m, shift_f, scale_f, gate_f = [
            m[:, None, :] for m in jnp.split(mod, 6, axis=-1)]
        h = rms_norm(x, norm_mix[l]) * (1.0 + scale_m) + shift_m
        proj = h @ w_in[l]
        q, k, v, z, b_in, a_in, xb, yb, g_gdn, g_lru = jnp.split(proj, split_pts, axis=-1)
        o_gdn = gdn_branch(q, k, v, z, b_in, a_in, gdn_conv_w[l], gdn_a_log[l], gdn_dt_bias[l],
                           gdn_norm_w[l])
        o_lru = rglru_branch(xb, yb, lru_conv_w[l], lru_conv_b[l], lru_w_a[l], lru_b_a[l],
                             lru_w_x[l], lru_b_x[l], lru_lambda[l])
        merged = (jax.nn.sigmoid(g_gdn) * (o_gdn @ w_branch_gdn[l])
                  + jax.nn.sigmoid(g_lru) * (o_lru @ w_branch_lru[l]))
        x = x + gate_m * (merged @ w_out[l])
        h = rms_norm(x, norm_ffn[l]) * (1.0 + scale_f) + shift_f
        x = x + gate_f * moe_ffn(h, w_router[l], b_router[l], w1[l], b1[l], w2[l], b2[l])
    return rms_norm(x, norm_final)


_drawn_inputs = setup_inputs


def setup_inputs(seed=0):
    import zlib

    import numpy as np

    out = dict(_drawn_inputs(seed))
    spreads = {}
    factors = {'norm_mix': 3.604,
     'norm_ffn': 56.423,
     'gdn_norm_w': 36.548,
     'lru_b_a': 200.0,
     'lru_b_x': 136.665,
     'b_router': 132.033,
     'b1': 133.446,
     'b2': 200.0,
     'norm_final': 200.0,
     'lru_conv_b': 28.138}
    for name, (base, spread) in spreads.items():
        noise = np.random.default_rng([zlib.crc32(name.encode()), seed]).standard_normal(out[name].shape)
        drawn = base * np.exp(spread * noise) if base else spread * noise
        out[name] = __import__('jax').numpy.asarray(drawn.astype(out[name].dtype))
    for name, factor in factors.items():
        out[name] = (out[name] * factor).astype(out[name].dtype)
    return out
```

```python
from contextlib import ExitStack

import numpy as np
import concourse.bass as bass
from concourse import mybir

F32 = mybir.dt.float32
I32 = mybir.dt.int32
U32 = mybir.dt.uint32
ALU = mybir.AluOpType
ACT = mybir.ActivationFunctionType
AX = mybir.AxisListType
ds = bass.ds

P = 128
SEQ, D = 256, 1024
TT = SEQ // P
KD = D // P
HEADS, HD = 4, 128
GW = HEADS * HD
LW = D // 2
LT = LW // P
CONV = 4
E, TOPK, FF = 32, 4, D
C64 = 64
ITEMS = 48
EPS = 1e-6
SW_ALPHA, SW_LIMIT = 1.702, 7.0
LRU_C = 8.0
GELU_A, GELU_B = 0.044715, 2.0 * 0.7978845608028654
BANK = 512
LEVELS = 7

C_IDENT = 0
C_TRI = C_IDENT + P
C_STRICT = C_TRI + P
C_LEVEL = C_STRICT + P
C_ONES = C_LEVEL + LEVELS * P
C_SLOT = C_ONES + P
C_EXPERT = C_SLOT + 2 * C64
C_ITEM = C_EXPERT + E
C_QUAD = C_ITEM + ITEMS
C_EPS = C_QUAD + 4
CONSTS = C_EPS + 1

R_C = 0
R_NORM_MIX = R_C + KD
R_GCONV = R_NORM_MIX + KD
R_LCONV = R_GCONV + CONV * 3 * HEADS
R_LCONV_B = R_LCONV + CONV * LT
R_BA = R_LCONV_B + LT
R_BX = R_BA + LT
R_LAM = R_BX + LT
R_NORM_W = R_LAM + LT
PARAMS = R_NORM_W + 1

HALF = 6
SLOTS = 12
IN_Z, IN_BA = 3 * GW, 4 * GW
IN_X = 4 * GW + 2 * HEADS
IN_G = IN_X + 2 * LW
STREAM = [("ada", 0, k) for k in range(KD)]
STREAM += [("in", 256 * j, 0) for j in range(6)]
STREAM += [("in", IN_X + 256 * j, 0) for j in range(4)]
STREAM += [("in", IN_Z + 256 * j, 0) for j in range(2)]
for _j in range(8):
    STREAM += [("in", IN_G + 256 * _j, 0)]
    STREAM += [("ada", 1 + (2 * _j) // KD, (2 * _j + a) % KD) for a in range(2)]
STREAM += [("branch", 256 * j, 0) for j in range(4)]
STREAM += [("out", 0, j) for j in range(4)]


def constants():
    a = np.zeros((P, CONSTS), np.float32)
    r = np.arange(P)
    s, c = r[:, None], r[None, :]
    a[:, C_IDENT:C_IDENT + P] = s == c
    a[:, C_TRI:C_TRI + P] = s <= c
    a[:, C_STRICT:C_STRICT + P] = s < c
    for level in range(LEVELS):
        b = 1 << level
        a[:, C_LEVEL + level * P:C_LEVEL + (level + 1) * P] = (
            (s // (2 * b) == c // (2 * b)) & (s % (2 * b) < b) & (c % (2 * b) >= b))
    a[:, C_ONES:C_ONES + P] = 1
    a[:, C_SLOT:C_SLOT + 2 * C64] = np.tile(np.arange(C64), 2)
    a[:, C_EXPERT:C_EXPERT + E] = np.arange(E)
    a[:, C_ITEM:C_ITEM + ITEMS] = np.arange(ITEMS)
    for q in range(4):
        a[32 * q, C_QUAD + q] = 1
    a[:, C_EPS] = EPS
    return a


def bank_plan():
    order = [("params", 0), ("xT0", 4), ("xT1", 5), ("xT2", 6), ("xT3", 7), ("ada0", 1), ("modcol", 2), ("ba", 2)]
    order += [("in0", 0), ("in1", 3), ("gc", 2), ("gcrow0", 6), ("gcrow1", 7)]
    order += [(f"in{n}", (0, 3)[n % 2]) for n in range(2, 10)]
    order += [("k0", 4), ("k1", 5), ("q0", 6), ("q1", 7), ("v0", 2), ("v1", 4)]
    order += [("in10", 0), ("lru_r0", 3), ("lru_r1", 5), ("in11", 0), ("lru_i0", 6), ("lru_i1", 7)]
    order += [("knT0", 4), ("knT1", 5), ("kbT0", 6), ("kbT1", 7), ("qnT0", 2), ("qnT1", 4), ("qdT", 5)]
    order += [("in12", 0), ("ada1", 1), ("kk0", 6), ("kk1", 7), ("qk0", 2), ("qk1", 4), ("in13", 3), ("T0", 5), ("T1", 6)]
    for level in range(1, LEVELS):
        order += [(f"X{level}_0", 4), (f"X{level}_1", 5)]
        for t in range(TT):
            if level < LEVELS - 1:
                order += [(f"PT{level}_{t}", (6, 2)[t])]
            order += [(f"PU{level}_{t}", (7, 3 if level % 2 else 0)[t])]
        order += [(f"in{13 + level}", 0 if level % 2 else 3)]
    order += [("ada2", 1)]
    order += [("vn0", 4), ("S", 5), ("kS", 6), ("vn1", 7), ("o0", 4), ("o1", 5), ("oT0", 6), ("oT1", 7)]
    order += [(f"row{n}", (0, 2, 3)[n % 3]) for n in range(8)]
    for m in range(4):
        order += [(f"bg{m}", (4, 6)[m % 2]), (f"bl{m}", (5, 7)[m % 2])]
    order += [("x00", 4), ("x01", 5), ("x10", 6), ("x11", 7)]
    order += [("h2T0", 0), ("h2T1", 1), ("h2T2", 2), ("h2T3", 3)]
    order += [("logits", 4), ("count", 5), ("pos", 6), ("end", 5), ("posT", 7), ("gateT", 0),
              ("b2_00", 1), ("b2_01", 2), ("b2_10", 3), ("b2_11", 4), ("pick", 6), ("gpick", 5), ("table", 0)]
    uses, plan = [0] * 8, {}
    for name, bank in order:
        plan[name] = (bank, uses[bank])
        uses[bank] += 1
    return plan


def hybrid_block(nc, x, c, w_ada, b_ada, norm_mix, norm_ffn, w_in, gdn_conv_w, gdn_a_log, gdn_dt_bias, gdn_norm_w,
                 lru_conv_w, lru_conv_b, lru_w_a, lru_b_a, lru_w_x, lru_b_x, lru_lambda, w_branch_gdn, w_branch_lru,
                 w_out, w_router, b_router, w1, b1, w2, b2, norm_final, consts, out):
    plan = bank_plan()
    with ExitStack() as ctx:
        def sb(name, shape, dt=F32):
            return ctx.enter_context(nc.sbuf_tensor(name, shape, dt))

        def sem(name):
            return ctx.enter_context(nc.semaphore(name))

        ring = sb("ring", [P, SLOTS, 2048])
        cst = sb("cst", [P, CONSTS])
        x_sb = sb("x_sb", [P, TT, D])
        hT = sb("hT", [P, KD, SEQ])
        mergedT = hT
        h2 = sb("h2", [P, TT, D])
        acc = sb("acc", [P, TT, D])
        area = sb("area", [P, 14 * 512])
        zT = sb("zT", [P, HEADS, SEQ])
        xcT = sb("xcT", [P, LT, SEQ])
        ybT = sb("ybT", [P, LT, SEQ])
        gatesT = sb("gatesT", [P, 2 * KD, SEQ])
        modreg = sb("modreg", [P, 3072])
        prm = sb("prm", [P, PARAMS])
        w_ba = sb("w_ba", [P, KD, 2 * HEADS])
        wr_sb = sb("wr_sb", [P, KD, E])
        small = sb("small", [P, 640])
        idx_u = sb("idx_u", [P, 2 * 8], U32)
        table_i = sb("table_i", [1, ITEMS + 1], I32)

        def view(t, at, shape):
            return t[:, at:at + shape[0] * shape[1]].rearrange("p (a b) -> p a b", b=shape[1])

        ident = cst[:, C_IDENT:C_IDENT + P]
        tri = cst[:, C_TRI:C_TRI + P]
        strict = cst[:, C_STRICT:C_STRICT + P]
        ones = cst[:, C_ONES:C_ONES + P]
        eps = cst[:, C_EPS:C_EPS + 1]

        def level_mask(level):
            return cst[:, C_LEVEL + level * P:C_LEVEL + (level + 1) * P].rearrange("p (a b) -> p a b", a=1)\
                .to_broadcast([P, HEADS, P])

        spare = ring[:, HALF:SLOTS, :].rearrange("p s n -> p (s n)")

        def work(n, tiles=TT):
            return spare[:, 512 * n:512 * (n + tiles)].rearrange("p (t n) -> p t n", t=tiles)

        k_tok, q_tok, v_tok = work(0), work(2), work(4)
        kn, kb, qn = work(6), work(8), work(10)
        qd, kd = work(12, 1), work(13, 1)
        knT, kbT, qnT, qdT = work(14), work(16), work(18), work(20, 1)
        vb = v_tok
        vn0, state, vn1 = k_tok[:, 0, :], k_tok[:, 1, :], kb[:, 0, :]
        ks_sb, r_sb, o_sqr = q_tok[:, 0, :], q_tok[:, 1, :], kn

        def conv_sg(n):
            return spare[:, 512 * (14 + n):512 * (15 + n)].rearrange("p (a n) -> p a n", a=2)

        convT = view(area, 0, (3 * HEADS, SEQ))
        U, T, X = (view(area, 1024 * n, (TT, 512)) for n in range(3))
        Bm, BM, QKT, Dm = (view(area, 3072 + 1024 * n, (TT, 512)) for n in range(4))
        sq = view(area, 3072 + 1024, (TT, 512))
        gate_m_b, shift_f_b, scale_f_b, gate_f_b, norm_ffn_b, norm_fin_b = (
            area[:, 1024 * n:1024 * (n + 1)] for n in range(6))
        g_bc = view(area, 3072, (TT * HEADS, P))

        acc_flat = acc[:, :, :].rearrange("p t n -> p (t n)")
        stage = acc_flat[0:PARAMS, 1024:1024 + P]
        wa_bd, wx_bd = view(acc_flat, 0, (LT, P)), view(acc_flat, 512, (LT, P))
        lru_a = view(acc_flat, 1024, (LT, SEQ))
        h2_flat = h2[:, :, :].rearrange("p t n -> p (t n)")
        lru_r, lru_i = view(h2_flat, 0, (LT, SEQ)), view(h2_flat, 1024, (LT, SEQ))

        mod = view(modreg, 0, (3, 512))
        mod_bias = view(modreg, 1536, (3, 512))
        b1_row = modreg[0:1, 0:2048]
        b2_sb = modreg[0:E, 2048:3072]

        g_flat = gatesT[:, :, :].rearrange("p t n -> p (t n)")
        hsel = view(g_flat, 0, (KD, C64))
        glu, sig, lin, act = (g_flat[:, 512 * n:512 * (n + 1)] for n in range(1, 5))
        actT = view(g_flat, 512 * 5, (4, P))
        y_sb = g_flat[:, 512 * 6:512 * 7]
        sgT = g_flat[:, 512 * 7:512 * 7 + SEQ]
        sel = view(g_flat, 512 * 7 + 256, (TT, C64))
        z_flat = zT[:, :, :].rearrange("p t n -> p (t n)")
        sg = view(z_flat, 0, (TT, P))
        pos_i, gate_i = view(z_flat, 256, (TT, ITEMS)), view(z_flat, 352, (TT, ITEMS))
        posT, gateT = z_flat[0:E, 448:704], z_flat[0:E, 704:960]
        xc_flat = xcT[:, :, :].rearrange("p t n -> p (t n)")
        eq, eqg = view(xc_flat, 0, (TT * TOPK, E)), view(xc_flat, 256, (TT * TOPK, E))
        M, G, pos_m = (view(xc_flat, 512 + 64 * n, (TT, E)) for n in range(3))
        cmp_end, one_hot = xc_flat[0:E, 704:704 + ITEMS], xc_flat[0:E, 752:752 + ITEMS]
        r64 = xc_flat[0:E, 800:928]
        yb_flat = ybT[:, :, :].rearrange("p t n -> p (t n)")
        quad = view(yb_flat, 0, (4, P))
        mtmp = [yb_flat[:, 0:512], yb_flat[:, 512:1024]]

        def col(n, w=1):
            return small[:, n:n + w]

        ssx, rstd = col(0, 2), col(2, 2)
        modcol = col(4, 16)
        beta, spx, gts = col(20, 8), col(28, 12), col(40, 8)
        sp_t, sp_s, sp_s2, sp_p, sp_d = col(48, 12), col(60, 12), col(72, 12), col(84, 12), col(96, 12)
        gc, egc, ekd, rs = col(108, 8), col(116, 8), col(124, 4), col(128, 16)
        ss = col(144, 16)
        a_exp, dt_b = col(160, 4), col(164, 4)
        be = col(168, 8)
        lam_c = col(176, 4)
        oss = col(184, 8)
        m8 = col(192, 16)
        idx_f = col(208, 16)
        gk, gsum, negm = col(224, 8), col(232, 2), col(234, 2)
        br_b = col(240, E)
        cnt = col(272, 8)
        sil = col(280, KD)
        logit = view(small, 288, (TT, E))
        c_bc = view(small, 352, (KD, 32))

        bank = [ctx.enter_context(nc.psum_tensor(f"bank{i}", [P, BANK], F32)) for i in range(8)]
        bU, bHS, bAT, bY, bO, bSG = (0, 1), 2, 3, 4, (5, 6), 7

        full = [sem(f"bank_full{i}") for i in range(8)]
        evac = [sem(f"bank_evacuated{i}") for i in range(8)]
        pre_loaded = [sem(f"pre_loaded{i}") for i in range(HALF)]
        pre_used = sem("pre_used")
        w_loaded = [sem(f"w_loaded{i}") for i in range(SLOTS)]
        w_used = [sem(f"w_used{i}") for i in range(SLOTS)]
        names = """const_in stage_in x_in bias_in ba_in row_in gate_w_in router_in late_in b2_in b1_in dve_chain
            act_chain pool_chain sqrt_x xn_ready sig_c cb_ready ba_read sp_in sp_exp g_ready gbc_ready
            diff_ready decay_ready conv_sig qkv_ready z_sig ss_ready rs_sqrt kn_ready U0_ready mask_ready
            r_ready o_sq oss_ready o_sqrt yb_arg yb_sig yb_done lru_exp lru_m lru_sqrt lru_b lru_out
            quad_ready merged_ready x1_ready sqrt_x1 h2_ready top_ready gates_exp M_ready count_ready
            item_ready pos_ready sel_ready gathered hsel_ready b1_used scattered y_ready sgT_ready
            acc_added u_read sg_ready sg_turned glu_ready sig_ready act_ready act_turned actT_ready
            gl_ready x2_ready sqrt_x2 out_ready out_stored""".split()
        S = {n: sem(n) for n in names}

        class Chain:
            def __init__(self, eng, name):
                self.eng, self.sem, self.n = eng, S[name], 0

            def __call__(self, ins):
                self.n += 1
                ins.then_inc(self.sem, 1)
                self.eng.wait_ge(self.sem, self.n)

        def bank_of(name):
            return bank[plan[name][0]]

        def open_bank(pe, name):
            b, n = plan[name]
            if n:
                pe.wait_ge(evac[b], n)

        def wait_full(eng, name):
            b, n = plan[name]
            eng.wait_ge(full[b], n + 1)

        def wait_evac(eng, name):
            b, n = plan[name]
            eng.wait_ge(evac[b], n + 1)

        def slot_of(c):
            return (HALF + c) % SLOTS

        block = ctx.enter_context(nc.Block())

        def release(n):
            kind, a, b = STREAM[n]
            if kind == "in":
                b, u = plan[f"in{[m for m in range(len(STREAM)) if STREAM[m][0] == 'in'].index(n)}"]
                return full[b], u + 1
            if kind == "branch":
                b, u = plan[f"bl{a // 256}"]
                return full[b], u + 1
            if kind == "ada" and b == KD - 1:
                b, u = plan[f"ada{a}"]
                return full[b], u + 1
            if kind == "out" and b == 3:
                b, u = plan["x11"]
                return full[b], u + 1
            before = [m for m in range(n + 1) if (STREAM[m][0] == "ada" and STREAM[m][2] < KD - 1)
                      or (STREAM[m][0] == "out" and STREAM[m][2] < 3)]
            return pre_used, len(before)

        @block.sync
        def _(sp):
            for t in range(TT):
                sp.dma_start(x_sb[:, t, :], x[0, t * P:(t + 1) * P, :]).then_inc(S["x_in"], 16)
            for n, (kind, a, b) in enumerate(STREAM):
                if n >= HALF:
                    sp.wait_ge(*release(n - HALF))
                dst, loaded = ring[:, n % HALF, :], pre_loaded[n % HALF]
                if kind == "ada":
                    sp.dma_start(dst, w_ada[0, b * P:(b + 1) * P, a * 2048:(a + 1) * 2048]).then_inc(loaded, 16)
                elif kind == "in":
                    sp.dma_start(dst.rearrange("p (k m) -> p k m", k=KD),
                                 w_in[0, :, a:a + 256].rearrange("(k p) m -> p k m", p=P)).then_inc(loaded, 16)
                elif kind == "branch":
                    halves = dst.rearrange("p (b k m) -> p b k m", b=2, k=4)
                    for i, w in enumerate((w_branch_gdn, w_branch_lru)):
                        sp.dma_start(halves[:, i], w[0, :, a:a + 256].rearrange("(k p) m -> p k m", p=P))\
                            .then_inc(loaded, 16)
                else:
                    sp.dma_start(dst.rearrange("p (k m) -> p k m", k=2),
                                 w_out[0, b * 256:(b + 1) * 256, :].rearrange("(k p) m -> p k m", p=P))\
                        .then_inc(loaded, 16)

            def load_expert(e, wait_free):
                wait_free(None)
                sp.dma_start(b1_row, b1[0, ds(e, 1), :]).then_inc(S["b1_in"], 16)
                for c in range(SLOTS):
                    wait_free(c)
                    dst = ring[:, slot_of(c), :]
                    if c < KD:
                        rows = w1[0, ds(e, 1), c * P:(c + 1) * P, :].rearrange("a p n -> p (a n)")
                    else:
                        k = 2 * (c - KD)
                        dst = dst.rearrange("p (k n) -> p k n", k=2)
                        rows = w2[0, ds(e, 1), k * P:(k + 2) * P, :].rearrange("a (k p) n -> p (a k) n", p=P)
                    sp.dma_start(dst, rows).then_inc(w_loaded[c], 16)

            def first_free(c):
                if c is None:
                    wait_full(sp, "row7")
                elif c == 0:
                    wait_full(sp, "oT1")
                elif c >= HALF:
                    slot = slot_of(c)
                    sp.wait_ge(*release(max(m for m in range(len(STREAM)) if m % HALF == slot)))

            load_expert(0, first_free)
            wait_evac(sp, "table")
            n_items = sp.value_load(table_i[0:1, ITEMS:ITEMS + 1], min_val=2, max_val=ITEMS - 1)
            with sp.Fori(1, n_items) as i:
                now = sp.value_load(table_i[0:1, ds(i, 1)], min_val=0, max_val=E - 1)
                before = sp.value_load(table_i[0:1, ds(i - 1, 1)], min_val=0, max_val=E - 1)
                with sp.If(now != before):
                    load_expert(now, lambda c: sp.wait_ge(S["b1_used"] if c is None else w_used[c], i))
                with sp.Else():
                    sp.wait_ge(S["b1_used"], i)
                    sp.sem_inc(S["b1_in"], 16)
                    for c in range(SLOTS):
                        sp.wait_ge(w_used[c], i)
                        sp.sem_inc(w_loaded[c], 16)
            for t in range(TT):
                sp.wait_ge(S["out_ready"], t + 1)
                sp.dma_start(out[0, t * P:(t + 1) * P, :], h2[:, t, :]).then_inc(S["out_stored"], 16)
            sp.wait_ge(S["out_stored"], 16 * TT)

        @block.tensor
        def _(pe):
            position = [0]

            def next_chunk():
                n = position[0]
                position[0] += 1
                loads = sum(2 if STREAM[m][0] == "branch" else 1 for m in range(n % HALF, n + 1, HALF))
                pe.wait_ge(pre_loaded[n % HALF], 16 * loads)
                return ring[:, n % HALF, :]

            def ended(mm, name):
                mm.then_inc(full[plan[name][0]], 1)

            def ada(part, ks):
                name = f"ada{part}"
                for k in ks:
                    if k == 0:
                        open_bank(pe, name)
                    w = next_chunk()
                    for q in range(4):
                        mm = pe.matmul(bank_of(name)[32 * q:32 * q + 32, :], c_bc[:, k, :],
                                       w[:, 512 * q:512 * q + 512], start=k == 0, stop=k == KD - 1)
                    if k < KD - 1:
                        mm.then_inc(pre_used, 1)
                    else:
                        ended(mm, name)

            def project(n):
                name = f"in{n}"
                open_bank(pe, name)
                w = next_chunk().rearrange("p (k m) -> p k m", k=KD)
                for half in range(2):
                    for k in range(KD):
                        mm = pe.matmul(bank_of(name)[:, 256 * half:256 * half + 256],
                                       w[:, k, 128 * half:128 * half + 128], hT[:, k, :],
                                       start=k == 0, stop=k == KD - 1)
                ended(mm, name)

            def heads(name, lhsT, rhs, transpose=False):
                open_bank(pe, name)
                for h in range(HEADS):
                    s = slice(P * h, P * h + P)
                    if transpose:
                        mm = pe.transpose(bank_of(name)[:, s], lhsT(h), ident)
                    else:
                        mm = pe.matmul(bank_of(name)[:, s], lhsT(h), rhs(h), start=True, stop=True)
                ended(mm, name)

            def of(tile, t=None):
                return lambda h: tile[:, P * h:P * h + P] if t is None else tile[:, t, P * h:P * h + P]

            pe.wait_ge(S["const_in"], 16)
            pe.wait_ge(S["stage_in"], 16 * 15)
            ended(pe.transpose(bank_of("params")[:, 0:PARAMS], stage, ident[0:PARAMS, 0:PARAMS]), "params")

            pe.wait_ge(S["xn_ready"], 2)
            for j in range(4):
                for k in (2 * j, 2 * j + 1):
                    for t in range(TT):
                        at = 256 * (k % 2) + P * t
                        mm = pe.transpose(bank_of(f"xT{j}")[:, at:at + P], h2[:, t, k * P:k * P + P], ident)
                ended(mm, f"xT{j}")

            pe.wait_ge(S["cb_ready"], 1)
            ada(0, range(KD))
            wait_evac(pe, "ada0")
            for m in range(2 * KD):
                mm = pe.matmul(bank_of("modcol")[:, m:m + 1], mod[:, 0, P * (m % 4):P * (m % 4) + P],
                               cst[:, C_QUAD + m // 4:C_QUAD + m // 4 + 1], start=True, stop=True)
            ended(mm, "modcol")

            for j in range(4):
                wait_evac(pe, f"xT{j}")
            pe.wait_ge(S["ba_in"], 16)
            open_bank(pe, "ba")
            for t in range(TT):
                for k in range(KD):
                    mm = pe.matmul(bank_of("ba")[:, 8 * t:8 * t + 8], hT[:, k, P * t:P * t + P], w_ba[:, k, :],
                                   start=k == 0, stop=k == KD - 1)
            ended(mm, "ba")
            project(0)
            project(1)

            pe.wait_ge(S["gbc_ready"], 1)
            open_bank(pe, "gc")
            ended(pe.matmul(bank_of("gc")[:, 0:TT * HEADS], tri, gts, start=True, stop=True), "gc")
            for t in range(TT):
                heads(f"gcrow{t}", lambda h: g_bc[:, HEADS * t + h, :], lambda h: tri)
            for n in range(2, 10):
                project(n)

            pe.wait_ge(S["qkv_ready"], 6)
            for kind, first in (("k", HEADS), ("q", 0), ("v", 2 * HEADS)):
                for t in range(TT):
                    heads(f"{kind}{t}", lambda h: convT[:, first + h, P * t:P * t + P], None, transpose=True)

            def lru_gate(kind, n, w):
                name = f"lru_{kind}{n}"
                open_bank(pe, name)
                for half in range(2):
                    j = 2 * n + half
                    mm = pe.matmul(bank_of(name)[:, 256 * half:256 * half + 256], w[:, j, :], xcT[:, j, :],
                                   start=True, stop=True)
                ended(mm, name)

            project(10)
            pe.wait_ge(S["gate_w_in"], 16 * 4)
            for n in (6, 7):
                wait_evac(pe, f"in{n}")
            for n in range(2):
                lru_gate("r", n, wa_bd)
            project(11)
            for n in range(2):
                lru_gate("i", n, wx_bd)

            for name, tile, t, value in (("knT0", kn, 0, 1), ("knT1", kn, 1, 2), ("kbT0", kb, 0, 3), ("kbT1", kb, 1, 4),
                                         ("qnT0", qn, 0, 5), ("qnT1", qn, 1, 6), ("qdT", qd, 0, 7)):
                pe.wait_ge(S["kn_ready"], value)
                heads(name, of(tile, t), None, transpose=True)
            project(12)
            ada(1, (0, 1))

            for t in range(TT):
                wait_evac(pe, f"knT{t}")
                wait_evac(pe, f"kbT{t}")
                heads(f"kk{t}", of(knT, t), of(kbT, t))
            for t in range(TT):
                wait_evac(pe, f"qnT{t}")
                heads(f"qk{t}", of(knT, t), of(qnT, t))
            project(13)
            ada(1, (2, 3))
            for t in range(TT):
                pe.wait_ge(S["U0_ready"], t + 1)
                heads(f"T{t}", of(U, t), None, transpose=True)

            for level in range(1, LEVELS):
                for t in range(TT):
                    wait_evac(pe, f"T{t}" if level == 1 else f"PT{level - 1}_{t}")
                    pe.wait_ge(S["mask_ready"], TT * (level - 1) + t + 1)
                    heads(f"X{level}_{t}", of(BM, t), of(T, t))
                for t in range(TT):
                    wait_evac(pe, f"X{level}_{t}")
                    if level > 1:
                        wait_evac(pe, f"PU{level - 1}_{t}")
                    if level < LEVELS - 1:
                        heads(f"PT{level}_{t}", of(U, t), of(X, t))
                    heads(f"PU{level}_{t}", of(X, t), of(U, t))
                project(13 + level)
                part, k = divmod(2 * (level + 1), KD)
                ada(1 + part, (k, k + 1))

            wait_evac(pe, f"PU{LEVELS - 1}_0")
            heads("vn0", of(U, 0), of(vb, 0))
            wait_evac(pe, "vn0")
            heads("S", of(kd, 0), of(vn0))
            wait_evac(pe, "S")
            heads("kS", of(knT, 1), of(state))
            pe.wait_ge(S["r_ready"], 1)
            wait_evac(pe, f"PU{LEVELS - 1}_1")
            heads("vn1", of(U, 1), of(r_sb))
            for t in range(TT):
                wait_evac(pe, f"qk{t}")
            heads("o0", of(QKT, 0), of(vn0))
            open_bank(pe, "o1")
            wait_evac(pe, "qdT")
            wait_evac(pe, "vn1")
            for h in range(HEADS):
                s = slice(P * h, P * h + P)
                pe.matmul(bank_of("o1")[:, s], qdT[:, 0, s], state[:, s], start=True, stop=False)
                mm = pe.matmul(bank_of("o1")[:, s], QKT[:, 1, s], vn1[:, s], start=False, stop=True)
            ended(mm, "o1")
            for t in range(TT):
                wait_evac(pe, f"o{t}")
                heads(f"oT{t}", of(qn, t), None, transpose=True)

            pe.wait_ge(S["quad_ready"], 1)
            wait_evac(pe, "ada1")
            wait_evac(pe, "ada2")
            for n in range(8):
                open_bank(pe, f"row{n}")
                ended(pe.matmul(bank_of(f"row{n}")[:, :], quad[:, n % 4, :], mod[:, 1 + n // 4, :],
                                start=True, stop=True), f"row{n}")

            pe.wait_ge(S["lru_out"], 1)
            for t in range(TT):
                wait_evac(pe, f"oT{t}")
            for m in range(4):
                w = next_chunk().rearrange("p (b k m) -> p b k m", b=2, k=4)
                for b, (name, src) in enumerate(((f"bg{m}", zT), (f"bl{m}", xcT))):
                    open_bank(pe, name)
                    for half in range(2):
                        for k in range(4):
                            mm = pe.matmul(bank_of(name)[:, 256 * half:256 * half + 256],
                                           w[:, b, k, 128 * half:128 * half + 128], src[:, k, :],
                                           start=k == 0, stop=k == 3)
                    ended(mm, name)

            for t in range(TT):
                for half in range(2):
                    open_bank(pe, f"x{t}{half}")
            for j in range(4):
                w = next_chunk().rearrange("p (k m) -> p k m", k=2)
                pe.wait_ge(S["merged_ready"], j + 1)
                for kk in range(2):
                    k = 2 * j + kk
                    for t in range(TT):
                        for half in range(2):
                            mm = pe.matmul(bank_of(f"x{t}{half}")[:, :], mergedT[:, k, P * t:P * t + P],
                                           w[:, kk, 512 * half:512 * half + 512], start=k == 0, stop=k == KD - 1)
                            if k == KD - 1:
                                ended(mm, f"x{t}{half}")
                if j < 3:
                    mm.then_inc(pre_used, 1)

            pe.wait_ge(S["h2_ready"], TT)
            for j in range(4):
                open_bank(pe, f"h2T{j}")
                for k in (2 * j, 2 * j + 1):
                    for t in range(TT):
                        at = 256 * (k % 2) + P * t
                        mm = pe.transpose(bank_of(f"h2T{j}")[:, at:at + P], h2[:, t, k * P:k * P + P], ident)
                ended(mm, f"h2T{j}")
            open_bank(pe, "logits")
            pe.wait_ge(S["router_in"], 16)
            for j in range(4):
                wait_evac(pe, f"h2T{j}")
            for t in range(TT):
                for k in range(KD):
                    mm = pe.matmul(bank_of("logits")[:, E * t:E * t + E], hT[:, k, P * t:P * t + P], wr_sb[:, k, :],
                                   start=k == 0, stop=k == KD - 1)
            ended(mm, "logits")

            pe.wait_ge(S["M_ready"], 1)
            open_bank(pe, "count")
            for t in range(TT):
                mm = pe.matmul(bank_of("count")[0:E, 0:1], M[:, t, :], ones[:, 0:1], start=t == 0, stop=t == TT - 1)
            ended(mm, "count")
            open_bank(pe, "pos")
            pe.matmul(bank_of("pos")[:, 0:E], strict, M[:, 0, :], start=True, stop=True)
            pe.matmul(bank_of("pos")[:, E:2 * E], strict, M[:, 1, :], start=True, stop=False)
            ended(pe.matmul(bank_of("pos")[:, E:2 * E], ones, M[:, 0, :], start=False, stop=True), "pos")
            pe.wait_ge(S["count_ready"], 1)
            open_bank(pe, "end")
            ended(pe.matmul(bank_of("end")[0:E, 0:1], tri[0:E, 0:E], cnt[0:E, 1:2], start=True, stop=True), "end")
            pe.wait_ge(S["pos_ready"], 1)
            for name, src in (("posT", pos_m), ("gateT", G)):
                open_bank(pe, name)
                for t in range(TT):
                    mm = pe.transpose(bank_of(name)[0:E, P * t:P * t + P], src[:, t, :], ident)
                ended(mm, name)
            wait_evac(pe, "posT")
            wait_evac(pe, "gateT")
            pe.wait_ge(S["item_ready"], 1)
            open_bank(pe, "pick")
            for t in range(TT):
                dst = bank_of("pick")[:, ITEMS * t:ITEMS * t + ITEMS]
                pe.matmul(dst, posT[:, P * t:P * t + P], one_hot, start=True, stop=False)
                mm = pe.matmul(dst, r64, cmp_end, start=False, stop=True)
            ended(mm, "pick")
            open_bank(pe, "gpick")
            for t in range(TT):
                mm = pe.matmul(bank_of("gpick")[:, ITEMS * t:ITEMS * t + ITEMS], gateT[:, P * t:P * t + P], one_hot,
                               start=True, stop=True)
            ended(mm, "gpick")
            open_bank(pe, "table")
            pe.matmul(bank_of("table")[0:1, 0:ITEMS], ones[0:E, 0:1], cmp_end, start=True, stop=True)
            ended(pe.matmul(bank_of("table")[0:1, ITEMS:ITEMS + 1], ones[0:E, 0:1], cnt[0:E, 1:2],
                            start=True, stop=True), "table")
            pe.wait_ge(S["b2_in"], 16)
            for t in range(TT):
                for half in range(2):
                    name = f"b2_{t}{half}"
                    open_bank(pe, name)
                    ended(pe.matmul(bank_of(name)[:, :], gateT[:, P * t:P * t + P], b2_sb[:, 512 * half:512 * half + 512],
                                    start=True, stop=True), name)

            for b in range(8):
                pe.wait_ge(evac[b], sum(1 for v in plan.values() if v[0] == b))

            def gather(ins_to):
                for k in range(KD):
                    for t in range(TT):
                        mm = pe.matmul(bank[bHS][:, C64 * k:C64 * k + C64], h2[:, t, P * k:P * k + P], sel[:, t, :],
                                       start=t == 0, stop=t == TT - 1)
                mm.then_inc(ins_to, 1)

            def scatter():
                for t in range(TT):
                    for half, b in enumerate((bO[0], bO[1]) if t == 0 else (bAT, bY)):
                        rows = slice(64 * half, 64 * half + 64)
                        mm = pe.matmul(bank[b][:, :], sgT[rows, P * t:P * t + P], y_sb[rows, :], start=True, stop=True)
                mm.then_inc(S["scattered"], 1)

            pe.wait_ge(S["sel_ready"], 1)
            gather(S["gathered"])
            wait_evac(pe, "table")
            n_items = pe.value_load(table_i[0:1, ITEMS:ITEMS + 1], min_val=2, max_val=ITEMS - 1)
            with pe.Fori(0, n_items) as i:
                pe.wait_ge(S["hsel_ready"], i + 1)
                pe.wait_ge(S["u_read"], i + 1)
                pe.wait_ge(S["b1_in"], 16 * i + 16)
                for half in range(2):
                    for group in range(2):
                        at = 1024 * group + 512 * half
                        mm = pe.matmul(bank[bU[half]][64 * group:64 * group + 64, :], ones[0:1, 0:C64],
                                       b1_row[:, at:at + 512], start=True, stop=False)
                mm.then_inc(S["b1_used"], 1)
                for k in range(KD):
                    pe.wait_ge(w_loaded[k], 16 * i + 16)
                    w = ring[:, slot_of(k), :]
                    for half in range(2):
                        for group in range(2):
                            at = 1024 * group + 512 * half
                            mm = pe.matmul(bank[bU[half]][64 * group:64 * group + 64, :], hsel[:, k, :],
                                           w[:, at:at + 512], start=False, stop=k == KD - 1)
                    mm.then_inc(w_used[k], 1)
                    if k == 3:
                        pe.wait_ge(S["y_ready"], i + 1)
                        pe.wait_ge(S["sgT_ready"], i + 1)
                        pe.wait_ge(S["acc_added"], i + 1)
                        scatter()
                pe.wait_ge(S["sg_ready"], i + 1)
                for t in range(TT):
                    mm = pe.transpose(bank[bSG][:, P * t:P * t + P], sg[:, t, :], ident)
                mm.then_inc(S["sg_turned"], 1)
                pe.wait_ge(S["sel_ready"], i + 2)
                gather(S["gathered"])
                pe.wait_ge(S["acc_added"], i + 2)
                pe.wait_ge(S["act_ready"], i + 1)
                for j in range(4):
                    mm = pe.transpose(bank[bAT][:, P * j:P * j + P], act[:, P * j:P * j + P], ident)
                mm.then_inc(S["act_turned"], 1)
                pe.wait_ge(S["actT_ready"], i + 1)
                for c in range(KD, SLOTS):
                    pe.wait_ge(w_loaded[c], 16 * i + 16)
                    w = ring[:, slot_of(c), :].rearrange("p (k n) -> p k n", k=2)
                    for kk in range(2):
                        k = 2 * (c - KD) + kk
                        for group in range(2):
                            mm = pe.matmul(bank[bY][64 * group:64 * group + 64, :],
                                           actT[:, k % 4, 64 * (k // 4):64 * (k // 4) + 64],
                                           w[:, kk, 512 * group:512 * group + 512], start=k == 0, stop=k == KD - 1)
                    mm.then_inc(w_used[c], 1)
            pe.wait_ge(S["y_ready"], n_items + 1)
            pe.wait_ge(S["sgT_ready"], n_items + 1)
            pe.wait_ge(S["acc_added"], n_items + 1)
            scatter()

        @block.vector
        def _(v):
            step = Chain(v, "dve_chain")

            def evacuated(ins, name):
                ins.then_inc(evac[plan[name][0]], 1)

            def head_scale(dst, src, scale, op=ALU.mult):
                return v.tensor_tensor(dst.rearrange("p (h d) -> p h d", h=HEADS), src.rearrange("p (h d) -> p h d", h=HEADS),
                                       scale.rearrange("p (h a) -> p h a", a=1).to_broadcast([P, HEADS, P]), op)

            wait_full(v, "params")
            evacuated(v.tensor_copy(prm[:, :], bank_of("params")[:, 0:PARAMS]), "params")
            v.wait_ge(S["sqrt_x"], 1)
            step(v.reciprocal(rstd, rstd))
            for t in range(TT):
                v.tensor_scalar(h2[:, t, :], x_sb[:, t, :], rstd[:, t:t + 1], None, ALU.mult).then_inc(S["xn_ready"], 1)
            v.wait_ge(S["sig_c"], 1)
            step(v.tensor_tensor(sil, sil, prm[:, R_C:R_C + KD], ALU.mult))
            v.tensor_copy(c_bc, sil.rearrange("p (k a) -> p k a", a=1).to_broadcast([P, KD, 32])).then_inc(S["cb_ready"], 1)
            v.wait_ge(S["bias_in"], 16 * 12)

            def ada_rows(part):
                wait_full(v, f"ada{part}")
                evacuated(v.tensor_tensor(mod[:, part, :], bank_of(f"ada{part}")[:, :], mod_bias[:, part, :], ALU.add),
                          f"ada{part}")

            ada_rows(0)
            wait_full(v, "modcol")
            step(v.tensor_copy(modcol[:, 0:KD], bank_of("modcol")[:, 0:KD]))
            evacuated(v.scalar_tensor_tensor(modcol[:, KD:2 * KD], bank_of("modcol")[:, KD:2 * KD], 1.0,
                                             prm[:, R_NORM_MIX:R_NORM_MIX + KD], ALU.add, ALU.mult), "modcol")
            wait_evac(v, "modcol")
            for k in range(4):
                name = f"xT{k // 2}"
                wait_full(v, name)
                ins = v.tensor_scalar(hT[:, k, :], bank_of(name)[:, 256 * (k % 2):256 * (k % 2) + 256],
                                      modcol[:, KD + k:KD + k + 1], modcol[:, k:k + 1], ALU.mult, ALU.add)
                if k % 2:
                    evacuated(ins, name)

            wait_full(v, "ba")
            v.wait_ge(S["row_in"], 16 * 3)
            ba = bank_of("ba")[:, 0:16].rearrange("p (t n) -> p t n", t=TT)
            v.tensor_tensor(spx[:, 0:8].rearrange("p (t h) -> p t h", t=TT), ba[:, :, HEADS:2 * HEADS],
                            dt_b.rearrange("p (a h) -> p a h", a=1).to_broadcast([P, TT, HEADS]), ALU.add)\
                .then_inc(S["ba_read"], 1)
            v.wait_ge(S["ba_read"], 1)
            step(v.tensor_scalar(spx[:, 8:12], prm[:, R_LAM:R_LAM + LT], -1.0, None, ALU.mult))
            v.scalar_tensor_tensor(sp_s, spx, -1.0, spx, ALU.mult, ALU.min).then_inc(S["sp_in"], 1)
            v.wait_ge(S["sp_exp"], 1)
            step(v.tensor_scalar(sp_d, sp_t, 2.0, None, ALU.add))
            step(v.reciprocal(sp_d, sp_d))
            step(v.tensor_tensor(sp_s, sp_t, sp_d, ALU.mult))
            step(v.tensor_tensor(sp_s2, sp_s, sp_s, ALU.mult))
            step(v.tensor_scalar(sp_p, sp_s2, 1.0 / 17, None, ALU.mult))
            for n in (15, 13, 11, 9, 7, 5, 3):
                step(v.scalar_tensor_tensor(sp_p, sp_p, 1.0 / n, sp_s2, ALU.add, ALU.mult))
            step(v.scalar_tensor_tensor(sp_p, sp_p, 1.0, sp_s, ALU.add, ALU.mult))
            step(v.tensor_scalar(sp_d, spx, 0.0, None, ALU.max))
            step(v.scalar_tensor_tensor(sp_d, sp_p, 2.0, sp_d, ALU.mult, ALU.add))
            step(v.tensor_scalar(lam_c, sp_d[:, 8:12], -LRU_C, None, ALU.mult))
            v.scalar_tensor_tensor(gts.rearrange("p (t h) -> p t h", t=TT), sp_d[:, 0:8].rearrange("p (t h) -> p t h", t=TT),
                                   -1.0, a_exp.rearrange("p (a h) -> p a h", a=1).to_broadcast([P, TT, HEADS]),
                                   ALU.mult, ALU.mult).then_inc(S["g_ready"], 1)
            v.wait_ge(S["g_ready"], 1)
            v.tensor_copy(g_bc, gts.rearrange("p (n a) -> p n a", a=1).to_broadcast([P, TT * HEADS, P]))\
                .then_inc(S["gbc_ready"], 1)

            def conv(n, dst, weight, bias, signal):
                name = f"in{n}"
                wait_full(v, name)
                for half in range(2):
                    src = bank_of(name)[:, 256 * half:256 * half + 256]
                    o, w = dst[:, half, :], weight(half)
                    if bias is None:
                        step(v.tensor_scalar(o, src, w[CONV - 1], None, ALU.mult))
                    else:
                        step(v.tensor_scalar(o, src, w[CONV - 1], bias(half), ALU.mult, ALU.add))
                    for tap in range(CONV - 1):
                        back = CONV - 1 - tap
                        ins = v.scalar_tensor_tensor(o[:, back:], src[:, :SEQ - back], w[tap], o[:, back:],
                                                     ALU.mult, ALU.add)
                        if half and tap == CONV - 2:
                            evacuated(ins, name)
                            wait_evac(v, name)
                        else:
                            step(ins)

            def qkv_conv(n):
                def weight(half):
                    return [prm[:, R_GCONV + 12 * tap + 2 * n + half:][:, 0:1] for tap in range(CONV)]
                conv(n, convT[:, 2 * n:2 * n + 2, :], weight, None, None)

            def qkv_silu(n):
                v.wait_ge(S["conv_sig"], n + 1)
                v.tensor_tensor(convT[:, 2 * n:2 * n + 2, :], convT[:, 2 * n:2 * n + 2, :], conv_sg(n), ALU.mult)\
                    .then_inc(S["qkv_ready"], 1)

            qkv_conv(0)
            qkv_conv(1)
            qkv_silu(0)
            wait_full(v, "gc")
            evacuated(v.tensor_copy(gc, bank_of("gc")[:, 0:TT * HEADS]), "gc")
            wait_evac(v, "gc")
            for t in range(TT):
                wait_full(v, f"gcrow{t}")
                evacuated(head_scale(Dm[:, t, :], bank_of(f"gcrow{t}")[:, :], gc[:, HEADS * t:HEADS * t + HEADS],
                                     ALU.subtract), f"gcrow{t}")
                wait_evac(v, f"gcrow{t}")
                v.tensor_scalar(Dm[:, t, :], Dm[:, t, :], 0.0, None, ALU.min).then_inc(S["diff_ready"], 1)
            for n in range(2, 6):
                qkv_conv(n)
                qkv_silu(n - 1)
                if n == 2:
                    v.wait_ge(S["decay_ready"], 1)
                    step(v.tensor_copy(ekd.rearrange("p (h a) -> p h a", a=1),
                                       Dm[:, 0, :].rearrange("p (h c) -> p h c", h=HEADS)[:, :, P - 1:P]))
                    for t in range(TT):
                        step(v.tensor_tensor(Dm[:, t, :].rearrange("p (h c) -> p h c", h=HEADS),
                                             Dm[:, t, :].rearrange("p (h c) -> p h c", h=HEADS),
                                             tri.rearrange("p (a c) -> p a c", a=1).to_broadcast([P, HEADS, P]), ALU.mult))
                    step(v.tensor_tensor(be, beta, egc, ALU.mult))
            qkv_silu(5)
            for n in (6, 7):
                j = 2 * (n - 6)
                conv(n, xcT[:, j:j + 2, :],
                     lambda half: [prm[:, R_LCONV + LT * tap + j + half:][:, 0:1] for tap in range(CONV)],
                     lambda half: prm[:, R_LCONV_B + j + half:][:, 0:1], None)

            for n in range(4):
                wait_evac(v, ("k0", "k1", "q0", "q1")[n])
                v.tensor_reduce(ss[:, 4 * n:4 * n + 4], sq[:, n % 2, :].rearrange("p (h d) -> p h d", h=HEADS),
                                AX.X, ALU.add).then_inc(S["ss_ready"], 1)
            for t in range(TT):
                wait_full(v, f"v{t}")
                evacuated(head_scale(vb[:, t, :], bank_of(f"v{t}")[:, :], beta[:, HEADS * t:HEADS * t + HEADS]), f"v{t}")
            v.wait_ge(S["rs_sqrt"], 1)
            step(v.reciprocal(rs, rs))
            step(v.tensor_scalar(rs[:, 8:16], rs[:, 8:16], float(HD) ** -0.5, None, ALU.mult))
            wait_evac(v, "q1")

            def scaled(dst, src, scale):
                head_scale(dst, src, scale).then_inc(S["kn_ready"], 1)

            for t in range(TT):
                scaled(kn[:, t, :], k_tok[:, t, :], rs[:, 4 * t:4 * t + 4])
            v.wait_ge(S["kn_ready"], 2)
            for t in range(TT):
                scaled(kb[:, t, :], kn[:, t, :], beta[:, 4 * t:4 * t + 4])
            for t in range(TT):
                scaled(qn[:, t, :], q_tok[:, t, :], rs[:, 8 + 4 * t:12 + 4 * t])
            v.wait_ge(S["kn_ready"], 6)
            scaled(qd[:, 0, :], qn[:, 1, :], egc[:, 4:8])
            scaled(kd[:, 0, :], kn[:, 0, :], ekd)

            def silu_z(n):
                v.wait_ge(S["z_sig"], n - 9)
                evacuated(v.tensor_tensor(zT[:, 2 * (n - 10):2 * (n - 10) + 2, :], zT[:, 2 * (n - 10):2 * (n - 10) + 2, :],
                                          bank_of(f"in{n}")[:, :].rearrange("p (a n) -> p a n", a=2), ALU.mult), f"in{n}")

            silu_z(10)
            silu_z(11)
            for name, dst in (("knT1", knT[:, 1, :]), ("kbT1", kbT[:, 1, :]), ("qnT1", qnT[:, 1, :])):
                wait_full(v, name)
                evacuated(v.tensor_copy(dst, bank_of(name)[:, :]), name)
            for t in range(TT):
                wait_full(v, f"kk{t}")
                ins = v.tensor_tensor(Bm[:, t, :], bank_of(f"kk{t}")[:, :], Dm[:, t, :], ALU.mult)
                evacuated(ins, f"kk{t}")
                wait_evac(v, f"kk{t}")
                step(v.tensor_tensor(U[:, t, :].rearrange("p (h c) -> p h c", h=HEADS),
                                     Bm[:, t, :].rearrange("p (h c) -> p h c", h=HEADS), level_mask(0), ALU.mult))
                v.tensor_tensor(U[:, t, :].rearrange("p (h c) -> p h c", h=HEADS),
                                ident.rearrange("p (a c) -> p a c", a=1).to_broadcast([P, HEADS, P]),
                                U[:, t, :].rearrange("p (h c) -> p h c", h=HEADS), ALU.subtract)\
                    .then_inc(S["U0_ready"], 1)
            for t in range(TT):
                wait_full(v, f"qk{t}")
                evacuated(v.tensor_tensor(QKT[:, t, :], bank_of(f"qk{t}")[:, :], Dm[:, t, :], ALU.mult), f"qk{t}")
            v.wait_ge(S["U0_ready"], TT)
            for level in range(1, LEVELS):
                for t in range(TT):
                    if level > 1:
                        wait_evac(v, f"PU{level - 1}_{t}")
                    if level < LEVELS - 1:
                        name = f"PT{level}_{t}"
                        wait_full(v, name)
                        wait_evac(v, f"T{t}" if level == 1 else f"PT{level - 1}_{t}")
                        evacuated(v.tensor_tensor(T[:, t, :], T[:, t, :], bank_of(name)[:, :], ALU.subtract), name)
                    name = f"PU{level}_{t}"
                    wait_full(v, name)
                    evacuated(v.tensor_tensor(U[:, t, :], U[:, t, :], bank_of(name)[:, :], ALU.subtract), name)
                if level == 2:
                    ada_rows(1)
                if level == 3:
                    v.wait_ge(S["lru_b"], 1)
                    for j in range(LT):
                        step(v.tensor_tensor_scan(xcT[:, j, :], lru_a[:, j, :], lru_i[:, j, :], 0.0, ALU.mult, ALU.add))
                    v.tensor_tensor(xcT[:, :, :], xcT[:, :, :], ybT[:, :, :], ALU.mult).then_inc(S["lru_out"], 1)
                    v.wait_ge(S["lru_out"], 1)
                    v.tensor_copy(quad, cst[:, C_QUAD:C_QUAD + 4].rearrange("p (q a) -> p q a", a=1)
                                  .to_broadcast([P, 4, P])).then_inc(S["quad_ready"], 1)
            ada_rows(2)

            wait_full(v, "kS")
            evacuated(head_scale(ks_sb, bank_of("kS")[:, :], be[:, 4:8]), "kS")
            wait_evac(v, "kS")
            wait_evac(v, "v1")
            v.tensor_tensor(r_sb, vb[:, 1, :], ks_sb, ALU.subtract).then_inc(S["r_ready"], 1)
            for t in range(TT):
                v.wait_ge(S["o_sq"], t + 1)
                v.tensor_reduce(oss[:, 4 * t:4 * t + 4], o_sqr[:, t, :].rearrange("p (h d) -> p h d", h=HEADS),
                                AX.X, ALU.add).then_inc(S["oss_ready"], 1)
            v.wait_ge(S["o_sqrt"], 1)
            step(v.reciprocal(oss, oss))
            for t in range(TT):
                evacuated(head_scale(qn[:, t, :], bank_of(f"o{t}")[:, :], oss[:, 4 * t:4 * t + 4]), f"o{t}")
            for t in range(TT):
                wait_full(v, f"oT{t}")
                zt = zT[:, :, P * t:P * t + P]
                evacuated(v.scalar_tensor_tensor(zt, bank_of(f"oT{t}")[:, :].rearrange("p (h c) -> p h c", h=HEADS),
                                                 prm[:, R_NORM_W:R_NORM_W + 1], zt, ALU.mult, ALU.mult), f"oT{t}")
            v.wait_ge(S["late_in"], 16 * 2)
            for n in range(8):
                name = f"row{n}"
                wait_full(v, name)
                s = slice(512 * (n % 2), 512 * (n % 2) + 512)
                if n // 2 == 2:
                    ins = v.scalar_tensor_tensor(norm_ffn_b[:, s], bank_of(name)[:, :], 1.0, norm_ffn_b[:, s],
                                                 ALU.add, ALU.mult)
                else:
                    ins = v.tensor_copy((gate_m_b, shift_f_b, None, gate_f_b)[n // 2][:, s], bank_of(name)[:, :])
                evacuated(ins, name)
            wait_evac(v, "row7")
            wait_evac(v, "row6")
            wait_evac(v, "row5")
            for m in range(4):
                def gate(b):
                    return gatesT[:, KD * b + 2 * m:KD * b + 2 * m + 2, :].rearrange("p a n -> p (a n)")
                dst = mergedT[:, 2 * m:2 * m + 2, :].rearrange("p a n -> p (a n)")
                wait_full(v, f"bg{m}")
                wait_evac(v, f"in{12 + m}")
                wait_evac(v, f"in{16 + m}")
                evacuated(v.tensor_tensor(mtmp[m % 2], bank_of(f"bg{m}")[:, :], gate(0), ALU.mult), f"bg{m}")
                wait_full(v, f"bl{m}")
                evacuated(v.tensor_tensor(dst, bank_of(f"bl{m}")[:, :], gate(1), ALU.mult), f"bl{m}")
                wait_evac(v, f"bg{m}")
                wait_evac(v, f"bl{m}")
                v.tensor_tensor(dst, dst, mtmp[m % 2], ALU.add).then_inc(S["merged_ready"], 1)
            v.wait_ge(S["merged_ready"], 4)
            for t in range(TT):
                for half in range(2):
                    name = f"x{t}{half}"
                    s = slice(512 * half, 512 * half + 512)
                    wait_full(v, name)
                    evacuated(v.tensor_tensor(h2[:, t, s], bank_of(name)[:, :], gate_m_b[:, s], ALU.mult), name)
                    wait_evac(v, name)
                    v.tensor_tensor(x_sb[:, t, s], x_sb[:, t, s], h2[:, t, s], ALU.add).then_inc(S["x1_ready"], 1)
            v.wait_ge(S["x1_ready"], 4)
            v.wait_ge(S["sqrt_x1"], 1)
            step(v.reciprocal(rstd, rstd))
            for t in range(TT):
                step(v.scalar_tensor_tensor(h2[:, t, :], x_sb[:, t, :], rstd[:, t:t + 1], norm_ffn_b, ALU.mult, ALU.mult))
                v.tensor_tensor(h2[:, t, :], h2[:, t, :], shift_f_b, ALU.add).then_inc(S["h2_ready"], 1)
            for j in (0, 1):
                wait_full(v, f"h2T{j}")
                evacuated(v.tensor_copy(hT[:, 2 * j:2 * j + 2, :].rearrange("p a n -> p (a n)"),
                                        bank_of(f"h2T{j}")[:, :]), f"h2T{j}")

            wait_full(v, "logits")
            evacuated(v.tensor_tensor(logit, bank_of("logits")[:, 0:TT * E].rearrange("p (t e) -> p t e", t=TT),
                                      br_b.rearrange("p (a e) -> p a e", a=1).to_broadcast([P, TT, E]), ALU.add), "logits")
            wait_evac(v, "logits")
            for t in range(TT):
                step(v.max(m8[:, 8 * t:8 * t + 8], logit[:, t, :]))
                step(v.max_index(idx_u[:, 8 * t:8 * t + 8], m8[:, 8 * t:8 * t + 8], logit[:, t, :]))
            v.tensor_scalar(negm.rearrange("p (t a) -> p t a", a=1),
                            m8.rearrange("p (t n) -> p t n", t=TT)[:, :, 0:1], -1.0, None, ALU.mult)\
                .then_inc(S["top_ready"], 1)
            step(v.tensor_copy(idx_f, idx_u[:, :]))
            for t in range(TT):
                step(v.tensor_tensor(eq[:, TOPK * t:TOPK * t + TOPK, :],
                                     cst[:, C_EXPERT:C_EXPERT + E].rearrange("p (a e) -> p a e", a=1).to_broadcast([P, TOPK, E]),
                                     idx_f[:, 8 * t:8 * t + TOPK].rearrange("p (k a) -> p k a", a=1).to_broadcast([P, TOPK, E]),
                                     ALU.is_equal))
            v.wait_ge(S["gates_exp"], 2)
            step(v.reciprocal(gsum, gsum))
            step(v.tensor_tensor(gk.rearrange("p (t k) -> p t k", t=TT), gk.rearrange("p (t k) -> p t k", t=TT),
                                 gsum.rearrange("p (t a) -> p t a", a=1).to_broadcast([P, TT, TOPK]), ALU.mult))
            step(v.tensor_tensor(eqg, eq, gk.rearrange("p (n a) -> p n a", a=1).to_broadcast([P, TT * TOPK, E]), ALU.mult))
            for t in range(TT):
                step(v.tensor_reduce(G[:, t, :], eqg[:, TOPK * t:TOPK * t + TOPK, :].rearrange("p k e -> p e k"),
                                     AX.X, ALU.add))
                ins = v.tensor_reduce(M[:, t, :], eq[:, TOPK * t:TOPK * t + TOPK, :].rearrange("p k e -> p e k"),
                                      AX.X, ALU.add)
                if t == TT - 1:
                    ins.then_inc(S["M_ready"], 1)
                    v.wait_ge(S["M_ready"], 1)
                else:
                    step(ins)
            wait_full(v, "count")
            evacuated(v.tensor_copy(cnt[0:E, 0:1], bank_of("count")[0:E, 0:1]), "count")
            wait_evac(v, "count")
            step(v.tensor_scalar(cnt[0:E, 1:2], cnt[0:E, 0:1], C64 + 0.5, 1.0, ALU.is_gt, ALU.add))
            step(v.scalar_tensor_tensor(cnt[0:E, 1:2], cnt[0:E, 0:1], 2 * C64 + 0.5, cnt[0:E, 1:2], ALU.is_gt, ALU.add))
            v.scalar_tensor_tensor(cnt[0:E, 1:2], cnt[0:E, 0:1], 3 * C64 + 0.5, cnt[0:E, 1:2], ALU.is_gt, ALU.add)\
                .then_inc(S["count_ready"], 1)
            v.wait_ge(S["count_ready"], 1)
            wait_full(v, "pos")
            Mf, posf = M.rearrange("p t e -> p (t e)"), pos_m.rearrange("p t e -> p (t e)")
            evacuated(v.scalar_tensor_tensor(posf, Mf, -4096.0, bank_of("pos")[:, 0:TT * E], ALU.mult, ALU.add), "pos")
            wait_evac(v, "pos")
            v.tensor_scalar(posf, posf, 4096.0, None, ALU.add).then_inc(S["pos_ready"], 1)
            wait_full(v, "end")
            evacuated(v.tensor_copy(cnt[0:E, 2:3], bank_of("end")[0:E, 0:1]), "end")
            wait_evac(v, "end")
            step(v.tensor_tensor(cnt[0:E, 3:4], cnt[0:E, 2:3], cnt[0:E, 1:2], ALU.subtract))
            item = cst[:, C_ITEM:C_ITEM + ITEMS]
            step(v.tensor_scalar(cmp_end, item[0:E, :], cnt[0:E, 2:3], None, ALU.is_ge))
            step(v.scalar_tensor_tensor(one_hot, item[0:E, :], cnt[0:E, 3:4], cmp_end, ALU.is_ge, ALU.subtract))
            v.tensor_scalar(r64, ones[0:E, :], cnt[0:E, 1:2], float(C64), ALU.mult, ALU.mult).then_inc(S["item_ready"], 1)
            wait_full(v, "pick")
            for t in range(TT):
                ins = v.scalar_tensor_tensor(pos_i[:, t, :], item, -float(C64), bank_of("pick")[:, ITEMS * t:ITEMS * t + ITEMS],
                                             ALU.mult, ALU.add)
                if t == TT - 1:
                    evacuated(ins, "pick")
                    wait_evac(v, "pick")
                else:
                    step(ins)
            wait_full(v, "gpick")
            evacuated(v.tensor_copy(gate_i.rearrange("p t n -> p (t n)"), bank_of("gpick")[:, 0:TT * ITEMS]), "gpick")
            wait_evac(v, "gpick")
            wait_full(v, "table")
            evacuated(v.tensor_copy(table_i[0:1, :], bank_of("table")[0:1, 0:ITEMS + 1]), "table")
            wait_evac(v, "table")

            def select(column):
                for t in range(TT):
                    ins = v.tensor_scalar(sel[:, t, :], cst[:, C_SLOT:C_SLOT + C64], column(pos_i, t), None, ALU.is_equal)
                ins.then_inc(S["sel_ready"], 1)

            wait_evac(v, "bl3")
            select(lambda tile, t: tile[:, t, 0:1])
            v.memset(y_sb, 0.0).then_inc(S["y_ready"], 1)
            v.memset(sgT, 0.0).then_inc(S["sgT_ready"], 1)
            for t in range(TT):
                for half in range(2):
                    wait_evac(v, f"b2_{t}{half}")
            v.sem_inc(S["acc_added"], 1)
            v.sem_inc(S["u_read"], 1)

            def add_scattered(n):
                v.wait_ge(S["scattered"], n)
                v.wait_ge(S["acc_added"], n)
                for t in range(TT):
                    for half, b in enumerate((bO[0], bO[1]) if t == 0 else (bAT, bY)):
                        a = acc[:, t, 512 * half:512 * half + 512]
                        ins = v.tensor_tensor(a, a, bank[b][:, :], ALU.add)
                ins.then_inc(S["acc_added"], 1)

            n_items = v.value_load(table_i[0:1, ITEMS:ITEMS + 1], min_val=2, max_val=ITEMS - 1)
            with v.Fori(0, n_items) as i:
                v.wait_ge(S["gathered"], i + 1)
                for t in range(TT):
                    ins = v.tensor_scalar(sel[:, t, :], cst[:, C_SLOT:C_SLOT + C64], pos_i[:, t, ds(i + 1, 1)], None,
                                          ALU.is_equal)
                ins.then_inc(S["sel_ready"], 1)
                add_scattered(i + 1)
                for t in range(TT):
                    ins = v.tensor_scalar(sg[:, t, :], cst[:, C_SLOT:C_SLOT + 2 * C64], pos_i[:, t, ds(i, 1)],
                                          gate_i[:, t, ds(i, 1)], ALU.is_equal, ALU.mult)
                ins.then_inc(S["sg_ready"], 1)
                v.wait_ge(w_used[KD - 1], i + 1)
                u = [bank[b][:, :].rearrange("p (f two) -> p f two", two=2) for b in bU]
                for half in range(2):
                    ins = v.tensor_scalar(glu[:, 256 * half:256 * half + 256].rearrange("p (f a) -> p f a", a=1),
                                          u[half][:, :, 0:1], SW_LIMIT, None, ALU.min)
                ins.then_inc(S["glu_ready"], 1)
                for half in range(2):
                    ins = v.tensor_scalar(lin[:, 256 * half:256 * half + 256].rearrange("p (f a) -> p f a", a=1),
                                          u[half][:, :, 1:2], SW_LIMIT, -SW_LIMIT, ALU.min, ALU.max)
                ins.then_inc(S["u_read"], 1)
                v.wait_ge(S["u_read"], i + 2)
                v.scalar_tensor_tensor(lin, lin, 1.0, glu, ALU.add, ALU.mult).then_inc(S["gl_ready"], 1)
                v.wait_ge(S["gl_ready"], i + 1)
                v.wait_ge(S["sig_ready"], i + 1)
                v.tensor_tensor(act, lin, sig, ALU.mult).then_inc(S["act_ready"], 1)
            add_scattered(n_items + 1)
            v.wait_ge(S["acc_added"], n_items + 2)
            for t in range(TT):
                step(v.tensor_tensor(acc[:, t, :], acc[:, t, :], gate_f_b, ALU.mult))
                v.tensor_tensor(x_sb[:, t, :], x_sb[:, t, :], acc[:, t, :], ALU.add).then_inc(S["x2_ready"], 1)
            for t in range(TT):
                v.wait_ge(S["sqrt_x2"], t + 1)
                step(v.reciprocal(rstd[:, t:t + 1], rstd[:, t:t + 1]))
                v.scalar_tensor_tensor(h2[:, t, :], x_sb[:, t, :], rstd[:, t:t + 1], norm_fin_b, ALU.mult, ALU.mult)\
                    .then_inc(S["out_ready"], 1)

        @block.scalar
        def _(a):
            step = Chain(a, "act_chain")

            def evacuated(ins, name):
                ins.then_inc(evac[plan[name][0]], 1)

            a.dma_start(cst[:, :], consts).then_inc(S["const_in"], 16)
            for at, src in ((R_C, c[0]), (R_NORM_MIX, norm_mix[0]), (R_LCONV_B, lru_conv_b[0]), (R_BA, lru_b_a[0]),
                            (R_BX, lru_b_x[0]), (R_LAM, lru_lambda[0])):
                n = src.shape[0] // P
                a.dma_start(stage[at:at + n, :], src.rearrange("(n p) -> n p", p=P)).then_inc(S["stage_in"], 16)
            a.dma_start(stage[R_NORM_W:R_NORM_W + 1, :], gdn_norm_w).then_inc(S["stage_in"], 16)
            for at, src in ((R_GCONV, gdn_conv_w[0]), (R_LCONV, lru_conv_w[0])):
                n = src.shape[1] // P
                for w in range(CONV):
                    a.dma_start(stage[at + n * w:at + n * w + n, :], src[w].rearrange("(n p) -> n p", p=P))\
                        .then_inc(S["stage_in"], 16)
            for b in range(3):
                for q in range(4):
                    at = 2048 * b + 512 * q
                    a.dma_start(mod_bias[32 * q:32 * q + 32, b, :], b_ada[0:1, at:at + 512].to_broadcast([32, 512]))\
                        .then_inc(S["bias_in"], 16)
            a.dma_start(w_ba[:, :, :], w_in[0, :, IN_BA:IN_X].rearrange("(k p) m -> p k m", p=P)).then_inc(S["ba_in"], 16)
            a.dma_start(a_exp, gdn_a_log.to_broadcast([P, HEADS])).then_inc(S["row_in"], 16)
            a.dma_start(dt_b, gdn_dt_bias.to_broadcast([P, HEADS])).then_inc(S["row_in"], 16)
            a.dma_start(br_b, b_router.to_broadcast([P, E])).then_inc(S["row_in"], 16)
            a.dma_start(wr_sb[:, :, :], w_router[0].rearrange("(k p) e -> p k e", p=P)).then_inc(S["router_in"], 16)

            a.wait_ge(S["x_in"], 16 * TT)
            for t in range(TT):
                step(a.activation(h2[:, t, :], x_sb[:, t, :], ACT.Square, accum_out=ssx[:, t:t + 1]))
            a.wait_ge(S["const_in"], 16)
            a.activation(rstd, ssx, ACT.Sqrt, scale=1.0 / D, bias=eps).then_inc(S["sqrt_x"], 1)
            wait_evac(a, "params")
            a.activation(sil, prm[:, R_C:R_C + KD], ACT.Sigmoid).then_inc(S["sig_c"], 1)
            wait_evac(a, "modcol")
            for k in range(4, KD):
                name = f"xT{k // 2}"
                wait_full(a, name)
                ins = a.activation(hT[:, k, :], bank_of(name)[:, 256 * (k % 2):256 * (k % 2) + 256], ACT.Identity,
                                   scale=modcol[:, KD + k:KD + k + 1], bias=modcol[:, k:k + 1])
                if k % 2:
                    evacuated(ins, name)
            a.wait_ge(S["ba_read"], 1)
            evacuated(a.activation(beta.rearrange("p (t h) -> p t h", t=TT),
                                   bank_of("ba")[:, 0:16].rearrange("p (t n) -> p t n", t=TT)[:, :, 0:HEADS],
                                   ACT.Sigmoid), "ba")
            a.wait_ge(S["row_in"], 16 * 3)
            step(a.activation(a_exp, a_exp, ACT.Exp))
            a.wait_ge(S["sp_in"], 1)
            a.activation(sp_t, sp_s, ACT.Exp).then_inc(S["sp_exp"], 1)

            def conv_sigmoid(n):
                wait_evac(a, f"in{n}")
                a.activation(conv_sg(n), convT[:, 2 * n:2 * n + 2, :], ACT.Sigmoid).then_inc(S["conv_sig"], 1)

            conv_sigmoid(0)
            conv_sigmoid(1)
            a.wait_ge(S["diff_ready"], TT)
            step(a.activation(egc, gc, ACT.Exp))
            a.activation(Dm, Dm, ACT.Exp).then_inc(S["decay_ready"], 1)
            for n in range(2, 6):
                conv_sigmoid(n)
            for n in (8, 9):
                wait_full(a, f"in{n}")
                evacuated(a.activation(ybT[:, 2 * (n - 8):2 * (n - 8) + 2, :],
                                       bank_of(f"in{n}")[:, :].rearrange("p (a n) -> p a n", a=2), ACT.Copy), f"in{n}")
            for n, name in enumerate(("k0", "k1", "q0", "q1")):
                wait_full(a, name)
                if n >= 2:
                    a.wait_ge(S["ss_ready"], n - 1)
                step(a.activation((k_tok, q_tok)[n // 2][:, n % 2, :], bank_of(name)[:, :], ACT.Copy))
                evacuated(a.activation(sq[:, n % 2, :], bank_of(name)[:, :], ACT.Square), name)
            a.wait_ge(S["ss_ready"], 4)
            a.activation(rs, ss, ACT.Sqrt, bias=eps).then_inc(S["rs_sqrt"], 1)
            def z_sigmoid(n):
                wait_full(a, f"in{n}")
                a.activation(zT[:, 2 * (n - 10):2 * (n - 10) + 2, :],
                             bank_of(f"in{n}")[:, :].rearrange("p (a n) -> p a n", a=2), ACT.Sigmoid).then_inc(S["z_sig"], 1)

            def lru_sigmoid(kind, n, dst, row):
                name = f"lru_{kind}{n}"
                wait_full(a, name)
                for half in range(2):
                    j = 2 * n + half
                    ins = a.activation(dst[:, j, :], bank_of(name)[:, 256 * half:256 * half + 256], ACT.Sigmoid,
                                       bias=prm[:, row + j:row + j + 1])
                evacuated(ins, name)

            z_sigmoid(10)
            for n in range(2):
                lru_sigmoid("r", n, lru_r, R_BA)
            z_sigmoid(11)
            for n in range(2):
                lru_sigmoid("i", n, lru_i, R_BX)
            a.wait_ge(S["yb_arg"], 1)
            a.activation(lru_a, lru_a, ACT.Sigmoid, scale=GELU_B).then_inc(S["yb_sig"], 1)
            for name, dst in (("knT0", knT[:, 0, :]), ("kbT0", kbT[:, 0, :]), ("qnT0", qnT[:, 0, :]), ("qdT", qdT[:, 0, :])):
                wait_full(a, name)
                evacuated(a.activation(dst, bank_of(name)[:, :], ACT.Copy), name)

            def gate_sigmoid(n):
                wait_full(a, f"in{n}")
                evacuated(a.activation(gatesT[:, 2 * (n - 12):2 * (n - 12) + 2, :],
                                       bank_of(f"in{n}")[:, :].rearrange("p (a n) -> p a n", a=2), ACT.Sigmoid), f"in{n}")

            gate_sigmoid(12)
            a.wait_ge(S["yb_done"], 1)
            a.wait_ge(S["g_ready"], 1)
            for n in range(2):
                wait_evac(a, f"lru_r{n}")
            for j in range(LT):
                step(a.activation(lru_a[:, j, :], lru_r[:, j, :], ACT.Exp, scale=lam_c[:, j:j + 1]))
            for j in range(LT):
                ins = a.activation(lru_r[:, j, :], lru_r[:, j, :], ACT.Tanh, scale=lam_c[:, j:j + 1])
            ins.then_inc(S["lru_exp"], 1)
            gate_sigmoid(13)
            for t in range(TT):
                wait_full(a, f"T{t}")
                evacuated(a.activation(T[:, t, :], bank_of(f"T{t}")[:, :], ACT.Copy), f"T{t}")
            for level in range(1, LEVELS):
                for t in range(TT):
                    wait_full(a, f"X{level}_{t}")
                    if level > 1:
                        wait_full(a, f"PU{level - 1}_{t}")
                    evacuated(a.activation(X[:, t, :], bank_of(f"X{level}_{t}")[:, :], ACT.Copy), f"X{level}_{t}")
                if level == 2:
                    a.wait_ge(S["lru_m"], 1)
                    a.activation(xcT[:, :, :], xcT[:, :, :], ACT.Sqrt).then_inc(S["lru_sqrt"], 1)
                gate_sigmoid(13 + level)
            for name, dst in (("vn0", vn0), ("S", state), ("vn1", vn1)):
                wait_full(a, name)
                evacuated(a.activation(dst, bank_of(name)[:, :], ACT.Copy), name)
            for t in range(TT):
                wait_full(a, f"o{t}")
                a.activation(o_sqr[:, t, :], bank_of(f"o{t}")[:, :], ACT.Square).then_inc(S["o_sq"], 1)
            a.wait_ge(S["oss_ready"], 2)
            a.activation(oss, oss, ACT.Sqrt, scale=1.0 / HD, bias=eps).then_inc(S["o_sqrt"], 1)
            for t in range(TT):
                wait_evac(a, f"o{t}")
            a.dma_start(norm_ffn_b, norm_ffn.to_broadcast([P, D])).then_inc(S["late_in"], 16)
            a.dma_start(norm_fin_b, norm_final.rearrange("(a n) -> a n", a=1).to_broadcast([P, D])).then_inc(S["late_in"], 16)
            wait_full(a, "row7")
            a.dma_start(b2_sb, b2[0]).then_inc(S["b2_in"], 16)
            a.wait_ge(S["x1_ready"], 4)
            for t in range(TT):
                step(a.activation(acc[:, t, :], x_sb[:, t, :], ACT.Square, accum_out=ssx[:, t:t + 1]))
            a.activation(rstd, ssx, ACT.Sqrt, scale=1.0 / D, bias=eps).then_inc(S["sqrt_x1"], 1)
            for j in (2, 3):
                wait_full(a, f"h2T{j}")
                evacuated(a.activation(hT[:, 2 * j:2 * j + 2, :], bank_of(f"h2T{j}")[:, :].rearrange("p (a n) -> p a n", a=2),
                                       ACT.Copy), f"h2T{j}")
            a.wait_ge(S["top_ready"], 1)
            for t in range(TT):
                a.activation(gk[:, TOPK * t:TOPK * t + TOPK], m8[:, 8 * t:8 * t + TOPK], ACT.Exp, bias=negm[:, t:t + 1],
                             accum_out=gsum[:, t:t + 1]).then_inc(S["gates_exp"], 1)
            for name, dst in (("posT", posT), ("gateT", gateT)):
                wait_full(a, name)
                evacuated(a.activation(dst, bank_of(name)[0:E, 0:SEQ], ACT.Copy), name)
            for t in range(TT):
                for half in range(2):
                    name = f"b2_{t}{half}"
                    wait_full(a, name)
                    evacuated(a.activation(acc[:, t, 512 * half:512 * half + 512], bank_of(name)[:, :], ACT.Copy), name)

            def take_gathered(n):
                a.wait_ge(S["gathered"], n)
                a.activation(hsel, bank[bHS][:, :].rearrange("p (k s) -> p k s", k=KD), ACT.Copy).then_inc(S["hsel_ready"], 1)

            take_gathered(1)
            wait_evac(a, "table")
            n_items = a.value_load(table_i[0:1, ITEMS:ITEMS + 1], min_val=2, max_val=ITEMS - 1)
            with a.Fori(0, n_items) as i:
                a.wait_ge(S["glu_ready"], i + 1)
                a.activation(sig, glu, ACT.Sigmoid, scale=SW_ALPHA).then_inc(S["sig_ready"], 1)
                a.wait_ge(S["sg_turned"], i + 1)
                a.activation(sgT, bank[bSG][:, 0:SEQ], ACT.Copy).then_inc(S["sgT_ready"], 1)
                a.wait_ge(S["gathered"], i + 2)
                a.activation(hsel, bank[bHS][:, :].rearrange("p (k s) -> p k s", k=KD), ACT.Copy).then_inc(S["hsel_ready"], 1)
                a.wait_ge(S["act_turned"], i + 1)
                a.activation(actT, bank[bAT][:, :].rearrange("p (j s) -> p j s", j=4), ACT.Copy).then_inc(S["actT_ready"], 1)
                a.wait_ge(w_used[SLOTS - 1], i + 1)
                a.activation(y_sb, bank[bY][:, :], ACT.Copy).then_inc(S["y_ready"], 1)
            for t in range(TT):
                a.wait_ge(S["x2_ready"], t + 1)
                step(a.activation(h2[:, t, :], x_sb[:, t, :], ACT.Square, accum_out=ssx[:, t:t + 1]))
                a.activation(rstd[:, t:t + 1], ssx[:, t:t + 1], ACT.Sqrt, scale=1.0 / D, bias=eps).then_inc(S["sqrt_x2"], 1)

        @block.gpsimd
        def _(g):
            step = Chain(g, "pool_chain")
            wait_full(g, "params")
            step(g.memset(acc_flat[:, 0:1024], 0.0))
            for dst, src in ((wa_bd, lru_w_a), (wx_bd, lru_w_x)):
                pairs = src[0].rearrange("(j two) c d -> two c j d", two=2)
                for i in range(2):
                    g.dma_start(dst[64 * i:64 * i + 64, :, 64 * i:64 * i + 64], pairs[i]).then_inc(S["gate_w_in"], 16)
            for n in (8, 9):
                wait_evac(g, f"in{n}")
            step(g.tensor_tensor(lru_a, ybT[:, :, :], ybT[:, :, :], ALU.mult))
            step(g.tensor_scalar(lru_a, lru_a, GELU_A, 1.0, ALU.mult, ALU.add))
            g.tensor_tensor(lru_a, lru_a, ybT[:, :, :], ALU.mult).then_inc(S["yb_arg"], 1)
            g.wait_ge(S["yb_sig"], 1)
            g.tensor_tensor(ybT[:, :, :], ybT[:, :, :], lru_a, ALU.mult).then_inc(S["yb_done"], 1)
            def mask(level):
                for t in range(TT):
                    if level == 1:
                        wait_evac(g, f"kk{t}")
                    else:
                        wait_full(g, f"X{level - 1}_{t}")
                    g.tensor_tensor(BM[:, t, :].rearrange("p (h c) -> p h c", h=HEADS),
                                    Bm[:, t, :].rearrange("p (h c) -> p h c", h=HEADS), level_mask(level), ALU.mult)\
                        .then_inc(S["mask_ready"], 1)
            for n in range(2):
                wait_evac(g, f"lru_i{n}")
            step(g.tensor_tensor(lru_i, lru_i, xcT[:, :, :], ALU.mult))
            mask(1)
            g.wait_ge(S["lru_exp"], 1)
            step(g.tensor_tensor(xcT[:, :, :], lru_a, lru_a, ALU.mult))
            step(g.tensor_scalar(xcT[:, :, :], xcT[:, :, :], 1.0, None, ALU.add))
            mask(2)
            step(g.tensor_tensor(xcT[:, :, :], xcT[:, :, :], lru_r, ALU.mult))
            g.tensor_scalar(xcT[:, :, :], xcT[:, :, :], -1.0, 0.0, ALU.mult, ALU.max).then_inc(S["lru_m"], 1)
            mask(3)
            g.wait_ge(S["lru_sqrt"], 1)
            g.tensor_tensor(lru_i, lru_i, xcT[:, :, :], ALU.mult).then_inc(S["lru_b"], 1)
            for level in range(4, LEVELS):
                mask(level)


INPUTS = ["x", "c", "w_ada", "b_ada", "norm_mix", "norm_ffn", "w_in", "gdn_conv_w", "gdn_a_log", "gdn_dt_bias",
          "gdn_norm_w", "lru_conv_w", "lru_conv_b", "lru_w_a", "lru_b_a", "lru_w_x", "lru_b_x", "lru_lambda",
          "w_branch_gdn", "w_branch_lru", "w_out", "w_router", "b_router", "w1", "b1", "w2", "b2", "norm_final"]


def kernel(**inputs):
    import concourse.bacc as bacc
    from concourse.bass_utils import run_bass_kernel_spmd

    nc = bacc.Bacc("TRN2", target_bir_lowering=False, num_devices=1)
    arrays, args = {}, []
    for name in INPUTS:
        arrays[f"in_{name}"] = np.ascontiguousarray(inputs[name])
    arrays["in_consts"] = constants()
    for name, a in arrays.items():
        args.append(nc.dram_tensor(name, a.shape, mybir.dt.from_np(a.dtype), kind="ExternalInput").ap())
    args.append(nc.dram_tensor("out_x", (1, SEQ, D), F32, kind="ExternalOutput").ap())
    hybrid_block(nc, *args)
    return run_bass_kernel_spmd(nc, [arrays], core_ids=[0]).results[0]["out_x"]
```

```python
from contextlib import ExitStack

import numpy as np
import concourse.bass as bass
from concourse import mybir

F32 = mybir.dt.float32
I32 = mybir.dt.int32
U32 = mybir.dt.uint32
ALU = mybir.AluOpType
ACT = mybir.ActivationFunctionType
AX = mybir.AxisListType
ds = bass.ds

P = 128
SEQ, D = 256, 1024
TT = SEQ // P
KD = D // P
HEADS, HD = 4, 128
GW = HEADS * HD
LW = D // 2
LT = LW // P
CONV = 4
E, TOPK, FF = 32, 4, D
C64 = 64
ITEMS = 48
EPS = 1e-6
SW_ALPHA, SW_LIMIT = 1.702, 7.0
LRU_C = 8.0
GELU_A, GELU_B = 0.044715, 2.0 * 0.7978845608028654
BANK = 512
ROWS = (2, 3, 0, 1, 4, 5, 6)
LEVELS = 7

C_IDENT = 0
C_TRI = C_IDENT + P
C_STRICT = C_TRI + P
C_LEVEL = C_STRICT + P
C_ONES = C_LEVEL + LEVELS * P
C_SLOT = C_ONES + P
C_EXPERT = C_SLOT + 2 * C64
C_ITEM = C_EXPERT + E
C_QUAD = C_ITEM + ITEMS
C_EPS = C_QUAD + 4
CONSTS = C_EPS + 1

R_C = 0
R_NORM_MIX = R_C + KD
R_GCONV = R_NORM_MIX + KD
R_LCONV = R_GCONV + CONV * 3 * HEADS
R_LCONV_B = R_LCONV + CONV * LT
R_BA = R_LCONV_B + LT
R_BX = R_BA + LT
R_LAM = R_BX + LT
R_NORM_W = R_LAM + LT
PARAMS = R_NORM_W + 1

HALF = 6
SLOTS = 12
IN_Z, IN_BA = 3 * GW, 4 * GW
IN_X = 4 * GW + 2 * HEADS
IN_G = IN_X + 2 * LW
STREAM = [("ada", 0, k) for k in range(KD)]
STREAM += [("in", 256 * j, 0) for j in range(6)]
STREAM += [("in", IN_X + 256 * j, 0) for j in range(4)]
STREAM += [("in", IN_Z + 256 * j, 0) for j in range(2)]
for _j in range(8):
    STREAM += [("in", IN_G + 256 * _j, 0)]
    STREAM += [("ada", 1 + (2 * _j) // KD, (2 * _j + a) % KD) for a in range(2)]
STREAM += [("branch", 256 * j, 0) for j in range(4)]
STREAM += [("out", 0, j) for j in range(4)]


def constants():
    a = np.zeros((P, CONSTS), np.float32)
    r = np.arange(P)
    s, c = r[:, None], r[None, :]
    a[:, C_IDENT:C_IDENT + P] = s == c
    a[:, C_TRI:C_TRI + P] = s <= c
    a[:, C_STRICT:C_STRICT + P] = s < c
    for level in range(LEVELS):
        b = 1 << level
        a[:, C_LEVEL + level * P:C_LEVEL + (level + 1) * P] = (
            (s // (2 * b) == c // (2 * b)) & (s % (2 * b) < b) & (c % (2 * b) >= b))
    a[:, C_ONES:C_ONES + P] = 1
    a[:, C_SLOT:C_SLOT + 2 * C64] = np.tile(np.arange(C64), 2)
    a[:, C_EXPERT:C_EXPERT + E] = np.arange(E)
    a[:, C_ITEM:C_ITEM + ITEMS] = np.arange(ITEMS)
    for q in range(4):
        a[32 * q, C_QUAD + q] = 1
    a[:, C_EPS] = EPS
    return a


def bank_plan():
    order = [("params", 0), ("xT0", 4), ("xT1", 5), ("xT2", 6), ("xT3", 7), ("ada0", 1), ("modcol", 2), ("ba", 2)]
    order += [("in0", 0), ("baT", 2), ("in1", 3), ("gc", 2), ("gcrow0", 6), ("gcrow1", 7)]
    order += [(f"in{n}", (0, 3)[n % 2]) for n in range(2, 10)]
    order += [("k0", 4), ("k1", 5), ("q0", 6), ("q1", 7), ("v0", 2), ("v1", 4)]
    order += [("in10", 0), ("lru_r0", 3), ("lru_r1", 5), ("in11", 0), ("lru_i0", 6), ("lru_i1", 7)]
    order += [("knT0", 4), ("knT1", 5), ("kbT0", 6), ("kbT1", 7), ("qnT0", 2), ("qnT1", 4), ("qdT", 5)]
    order += [("in12", 0), ("ada1", 1), ("kk0", 6), ("kk1", 7), ("qk0", 2), ("qk1", 4), ("in13", 3), ("T0", 5), ("T1", 6)]
    for level in range(1, LEVELS):
        order += [(f"X{level}_0", 4), (f"X{level}_1", 5)]
        for t in range(TT):
            if level < LEVELS - 1:
                order += [(f"PT{level}_{t}", (6, 2)[t])]
            order += [(f"PU{level}_{t}", (7, 3 if level % 2 else 0)[t])]
        order += [(f"in{13 + level}", 0 if level % 2 else 3)]
    order += [("ada2", 1)]
    order += [("vn0", 4), ("S", 5), ("kS", 6), ("vn1", 7), ("o0", 4), ("o1", 5)]
    order += [(f"row{n}", (0, 2, 3)[i % 3]) for i, n in enumerate(ROWS)]
    order += [("oT0", 6), ("oT1", 7)]
    for m in range(4):
        order += [(f"bg{m}", (4, 6)[m % 2]), (f"bl{m}", (5, 7)[m % 2])]
    order += [("x00", 4), ("x01", 5), ("x10", 6), ("h2T00", 0), ("h2T01", 1), ("x11", 7), ("lgT0", 2), ("lg0", 3)]
    order += [("h2T10", 0), ("h2T11", 1), ("lgT1", 2), ("lg1", 4)]
    order += [("count", 5), ("pos", 6), ("posT", 0), ("end", 5), ("gathered0", 2), ("table", 0), ("pick", 6),
              ("gateT", 7), ("gpick", 5)]
    uses, plan = [0] * 8, {}
    for name, bank in order:
        plan[name] = (bank, uses[bank])
        uses[bank] += 1
    return plan


def hybrid_block(nc, x, c, w_ada, b_ada, norm_mix, norm_ffn, w_in, gdn_conv_w, gdn_a_log, gdn_dt_bias, gdn_norm_w,
                 lru_conv_w, lru_conv_b, lru_w_a, lru_b_a, lru_w_x, lru_b_x, lru_lambda, w_branch_gdn, w_branch_lru,
                 w_out, w_router, b_router, w1, b1, w2, b2, norm_final, consts, out):
    plan = bank_plan()
    with ExitStack() as ctx:
        def sb(name, shape, dt=F32):
            return ctx.enter_context(nc.sbuf_tensor(name, shape, dt))

        def sem(name):
            return ctx.enter_context(nc.semaphore(name))

        ring = sb("ring", [P, SLOTS, 2048])
        cst = sb("cst", [P, CONSTS])
        x_sb = sb("x_sb", [P, TT, D])
        hT = sb("hT", [P, KD, SEQ])
        mergedT = hT
        h2 = sb("h2", [P, TT, D])
        lru_ws = sb("lru_ws", [P, 2048])
        area = sb("area", [P, 14 * 512])
        zT = sb("zT", [P, HEADS, SEQ])
        xcT = sb("xcT", [P, LT, SEQ])
        ybT = sb("ybT", [P, LT, SEQ])
        gatesT = sb("gatesT", [P, 2 * KD, SEQ])
        modreg = sb("modreg", [P, 3072])
        prm = sb("prm", [P, PARAMS])
        w_ba = sb("w_ba", [P, KD, 2 * HEADS])
        wr_sb = sb("wr_sb", [P, KD, E])
        small = sb("small", [P, 640])
        idx_u = sb("idx_u", [P, 2 * 8], U32)
        table_i = sb("table_i", [1, ITEMS + 1], I32)

        def view(t, at, shape):
            return t[:, at:at + shape[0] * shape[1]].rearrange("p (a b) -> p a b", b=shape[1])

        ident = cst[:, C_IDENT:C_IDENT + P]
        tri = cst[:, C_TRI:C_TRI + P]
        strict = cst[:, C_STRICT:C_STRICT + P]
        ones = cst[:, C_ONES:C_ONES + P]
        eps = cst[:, C_EPS:C_EPS + 1]

        def level_mask(level):
            return cst[:, C_LEVEL + level * P:C_LEVEL + (level + 1) * P].rearrange("p (a b) -> p a b", a=1)\
                .to_broadcast([P, HEADS, P])

        spare = ring[:, HALF:SLOTS, :].rearrange("p s n -> p (s n)")

        def work(n, tiles=TT):
            return spare[:, 512 * n:512 * (n + tiles)].rearrange("p (t n) -> p t n", t=tiles)

        k_tok, q_tok, v_tok = work(0), work(2), work(4)
        kn, kb, qn = work(6), work(8), work(10)
        qd, kd = work(12, 1), work(13, 1)
        knT, kbT, qnT, qdT = work(14), work(16), work(18), work(20, 1)
        vb = v_tok
        vn0, state, vn1 = k_tok[:, 0, :], k_tok[:, 1, :], kb[:, 0, :]
        ks_sb, r_sb, o_sqr = q_tok[:, 0, :], q_tok[:, 1, :], kn

        def conv_sg(n):
            return spare[:, 512 * (14 + n):512 * (15 + n)].rearrange("p (a n) -> p a n", a=2)

        convT = view(area, 0, (3 * HEADS, SEQ))
        U, T, X = (view(area, 1024 * n, (TT, 512)) for n in range(3))
        Bm, BM, QKT, Dm = (view(area, 3072 + 1024 * n, (TT, 512)) for n in range(4))
        sq = view(area, 3072 + 1024, (TT, 512))
        gate_m_b, shift_f_b, _, gate_f_b, norm_ffn_b, norm_fin_b = (
            area[:, 1024 * n:1024 * (n + 1)] for n in range(6))
        gate_f_h = gate_f_b[:, 0:512]
        g_bc = view(area, 3072, (TT * HEADS, P))

        stage = lru_ws[0:PARAMS, 1024:1024 + P]
        wa_bd, wx_bd = view(lru_ws, 0, (LT, P)), view(lru_ws, 512, (LT, P))
        lru_a = view(lru_ws, 1024, (LT, SEQ))
        h2_flat = h2[:, :, :].rearrange("p t n -> p (t n)")
        lru_r, lru_i = view(h2_flat, 0, (LT, SEQ)), view(h2_flat, 1024, (LT, SEQ))

        mod = view(modreg, 0, (3, 512))
        mod_bias = view(modreg, 1536, (3, 512))
        b1_row = modreg[0:1, 0:2048]

        g_flat = gatesT[:, :, :].rearrange("p t n -> p (t n)")
        hsel = view(g_flat, 0, (KD, C64))
        glu, sig, lin, act = (g_flat[:, 512 * n:512 * (n + 1)] for n in range(1, 5))
        actT = view(g_flat, 512 * 5, (4, P))
        y_sb = g_flat[:, 512 * 6:512 * 7]
        sgT = g_flat[:, 512 * 7:512 * 7 + SEQ]
        sel = view(g_flat, 512 * 7 + 256, (TT, C64))
        z_flat = zT[:, :, :].rearrange("p t n -> p (t n)")
        sg = view(z_flat, 0, (TT, P))
        pos_i, gate_i = view(z_flat, 256, (TT, ITEMS)), view(z_flat, 352, (TT, ITEMS))
        posT = z_flat[0:E, 448:704]
        xc_flat = xcT[:, :, :].rearrange("p t n -> p (t n)")
        eq, eqg = view(xc_flat, 0, (TT * TOPK, E)), view(xc_flat, 256, (TT * TOPK, E))
        M, G, pos_m = (view(xc_flat, 512 + 64 * n, (TT, E)) for n in range(3))
        cmp_end, one_hot = xc_flat[0:E, 704:704 + ITEMS], xc_flat[0:E, 752:752 + ITEMS]
        r64 = xc_flat[0:E, 800:928]
        yb_flat = ybT[:, :, :].rearrange("p t n -> p (t n)")
        quad = view(yb_flat, 0, (4, P))
        quad_f = yb_flat[:, 512:512 + P]
        mtmp = [yb_flat[:, 0:512], yb_flat[:, 512:1024]]
        squares = yb_flat[:, 0:512]
        ba_row = yb_flat[0:2 * HEADS, 0:SEQ]
        lg_row = mod_bias[0:E, 1, 0:SEQ]

        def col(n, w=1):
            return small[:, n:n + w]

        ssx, rstd = col(0, 2), col(2, 2)
        ssh, ssb = col(608, 4), col(612, 2)
        warm = col(614)
        modcol = col(4, 16)
        beta, spx, gts = col(20, 8), col(28, 12), col(40, 8)
        sp_t, sp_s, sp_s2, sp_p, sp_d = col(48, 12), col(60, 12), col(72, 12), col(84, 12), col(96, 12)
        gc, egc, ekd, rs = col(108, 8), col(116, 8), col(124, 4), col(128, 16)
        ss = col(144, 16)
        a_exp, dt_b = col(160, 4), col(164, 4)
        be = col(168, 8)
        lam_c = col(176, 4)
        oss = col(184, 8)
        m8 = col(192, 16)
        idx_f = col(208, 16)
        gk, gsum, negm = col(224, 8), col(232, 2), col(234, 2)
        br_b = col(240, E)
        cnt = col(272, 8)
        sil = col(280, KD)
        logit = view(small, 288, (TT, E))
        c_bc = view(small, 352, (KD, 32))

        bank = [ctx.enter_context(nc.psum_tensor(f"bank{i}", [P, BANK], F32)) for i in range(8)]
        bU, bHS, bAT, bY, bO, bSG = (0, 1), 2, 3, 4, (5, 6), 7

        full = [sem(f"bank_full{i}") for i in range(8)]
        evac = [sem(f"bank_evacuated{i}") for i in range(8)]
        pre_loaded = [sem(f"pre_loaded{i}") for i in range(HALF)]
        pre_used = sem("pre_used")
        w_loaded = [sem(f"w_loaded{i}") for i in range(SLOTS)]
        w_used = [sem(f"w_used{i}") for i in range(SLOTS)]
        names = """const_in stage_in x_in bias_in bias_late ba_in norm_in y_zero row_in gate_w_in router_in late_in b2_in b1_in dve_chain
            act_chain pool_chain sqrt_x xn_ready sig_c cb_ready ba_read sp_in sp_exp g_ready gbc_ready
            diff_ready decay_ready conv_sig qkv_ready z_sig ss_ready rs_sqrt kn_ready U0_ready mask_ready
            r_ready o_sq oss_ready o_sqrt yb_arg yb_sig yb_done lru_exp lru_m lru_sqrt lru_b lru_out
            quad_ready merged_ready x1_ready sqrt_x1 h2_ready top_ready gates_exp G_ready M_ready count_ready
            item_ready pos_ready sel_ready gathered hsel_ready b1_used scattered y_ready sgT_ready
            x_added u_read sg_ready sg_turned glu_ready sig_ready act_ready act_turned actT_ready
            gl_ready x2_ready sqrt_x2 tail_scattered out_ready out_stored""".split()
        S = {n: sem(n) for n in names}

        class Chain:
            def __init__(self, eng, name):
                self.eng, self.sem, self.n = eng, S[name], 0

            def __call__(self, ins):
                self.n += 1
                ins.then_inc(self.sem, 1)
                self.eng.wait_ge(self.sem, self.n)

        def bank_of(name):
            return bank[plan[name][0]]

        def open_bank(pe, name):
            b, n = plan[name]
            if n:
                pe.wait_ge(evac[b], n)

        def wait_full(eng, name):
            b, n = plan[name]
            eng.wait_ge(full[b], n + 1)

        def wait_evac(eng, name):
            b, n = plan[name]
            eng.wait_ge(evac[b], n + 1)

        def slot_of(c):
            return (HALF + c) % SLOTS

        block = ctx.enter_context(nc.Block())

        def release(n):
            kind, a, b = STREAM[n]
            if kind == "in":
                b, u = plan[f"in{[m for m in range(len(STREAM)) if STREAM[m][0] == 'in'].index(n)}"]
                return full[b], u + 1
            if kind == "branch":
                b, u = plan[f"bl{a // 256}"]
                return full[b], u + 1
            if kind == "ada" and b == KD - 1:
                b, u = plan[f"ada{a}"]
                return full[b], u + 1
            if kind == "out" and b == 3:
                b, u = plan["x11"]
                return full[b], u + 1
            before = [m for m in range(n + 1) if (STREAM[m][0] == "ada" and STREAM[m][2] < KD - 1)
                      or (STREAM[m][0] == "out" and STREAM[m][2] < 3)]
            return pre_used, len(before)

        @block.sync
        def _(sp):
            for at, src in ((R_C, c[0]), (R_NORM_MIX, norm_mix[0]), (R_LCONV_B, lru_conv_b[0]), (R_BA, lru_b_a[0]),
                            (R_BX, lru_b_x[0]), (R_LAM, lru_lambda[0])):
                n = src.shape[0] // P
                sp.dma_start(stage[at:at + n, :], src.rearrange("(n p) -> n p", p=P)).then_inc(S["stage_in"], 16)
            sp.dma_start(stage[R_NORM_W:R_NORM_W + 1, :], gdn_norm_w).then_inc(S["stage_in"], 16)
            for at, src in ((R_GCONV, gdn_conv_w[0]), (R_LCONV, lru_conv_w[0])):
                n = src.shape[1] // P
                sp.dma_start(stage[at:at + n * CONV, :], src.rearrange("w (n p) -> (w n) p", p=P))\
                    .then_inc(S["stage_in"], 16)
            for t in range(TT):
                sp.dma_start(x_sb[:, t, :], x[0, t * P:(t + 1) * P, :]).then_inc(S["x_in"], 16)
            for q in range(4):
                sp.dma_start(mod_bias[32 * q:32 * q + 32, 0, :], b_ada[0:1, 512 * q:512 * q + 512].to_broadcast([32, 512]))\
                    .then_inc(S["bias_in"], 16)
            for n, (kind, a, b) in enumerate(STREAM):
                if n >= HALF:
                    sp.wait_ge(*release(n - HALF))
                dst, loaded = ring[:, n % HALF, :], pre_loaded[n % HALF]
                if kind == "ada":
                    sp.dma_start(dst, w_ada[0, b * P:(b + 1) * P, a * 2048:(a + 1) * 2048]).then_inc(loaded, 16)
                elif kind == "in":
                    sp.dma_start(dst.rearrange("p (k m) -> p k m", k=KD),
                                 w_in[0, :, a:a + 256].rearrange("(k p) m -> p k m", p=P)).then_inc(loaded, 16)
                elif kind == "branch":
                    halves = dst.rearrange("p (b k m) -> p b k m", b=2, k=4)
                    for i, w in enumerate((w_branch_gdn, w_branch_lru)):
                        sp.dma_start(halves[:, i], w[0, :, a:a + 256].rearrange("(k p) m -> p k m", p=P))\
                            .then_inc(loaded, 16)
                else:
                    sp.dma_start(dst.rearrange("p (k m) -> p k m", k=2),
                                 w_out[0, b * 256:(b + 1) * 256, :].rearrange("(k p) m -> p k m", p=P))\
                        .then_inc(loaded, 16)

            def load_expert(e, wait_free):
                wait_free(None)
                sp.dma_start(b1_row, b1[0, ds(e, 1), :]).then_inc(S["b1_in"], 16)
                for c in range(SLOTS):
                    wait_free(c)
                    dst = ring[:, slot_of(c), :]
                    if c < KD:
                        rows = w1[0, ds(e, 1), c * P:(c + 1) * P, :].rearrange("a p n -> p (a n)")
                    else:
                        k = 2 * (c - KD)
                        dst = dst.rearrange("p (k n) -> p k n", k=2)
                        rows = w2[0, ds(e, 1), k * P:(k + 2) * P, :].rearrange("a (k p) n -> p (a k) n", p=P)
                    sp.dma_start(dst, rows).then_inc(w_loaded[c], 16)

            def first_free(c):
                if c is None:
                    wait_full(sp, "row6")
                elif c == 0:
                    wait_full(sp, "oT1")
                elif c >= HALF:
                    slot = slot_of(c)
                    sp.wait_ge(*release(max(m for m in range(len(STREAM)) if m % HALF == slot)))

            load_expert(0, first_free)
            wait_evac(sp, "table")
            n_items = sp.value_load(table_i[0:1, ITEMS:ITEMS + 1], min_val=2, max_val=ITEMS - 1)
            with sp.Fori(1, n_items) as i:
                now = sp.value_load(table_i[0:1, ds(i, 1)], min_val=0, max_val=E - 1)
                before = sp.value_load(table_i[0:1, ds(i - 1, 1)], min_val=0, max_val=E - 1)
                with sp.If(now != before):
                    load_expert(now, lambda c: sp.wait_ge(S["b1_used"] if c is None else w_used[c], i))
                with sp.Else():
                    sp.wait_ge(S["b1_used"], i)
                    sp.sem_inc(S["b1_in"], 16)
                    for chunk in range(SLOTS):
                        sp.wait_ge(w_used[chunk], i)
                        sp.sem_inc(w_loaded[chunk], 16)
            for t in range(TT):
                for half in range(2):
                    s = slice(512 * half, 512 * half + 512)
                    sp.wait_ge(S["out_ready"], 2 * t + half + 1)
                    sp.dma_start(out[0, t * P:(t + 1) * P, s], h2[:, t, s]).then_inc(S["out_stored"], 16)
            sp.wait_ge(S["out_stored"], 16 * 2 * TT)

        @block.tensor
        def _(pe):
            position = [0]

            def next_chunk():
                n = position[0]
                position[0] += 1
                loads = sum(2 if STREAM[m][0] == "branch" else 1 for m in range(n % HALF, n + 1, HALF))
                pe.wait_ge(pre_loaded[n % HALF], 16 * loads)
                return ring[:, n % HALF, :]

            def ended(mm, name):
                mm.then_inc(full[plan[name][0]], 1)

            def ada(part, ks):
                name = f"ada{part}"
                for k in ks:
                    if k == 0:
                        open_bank(pe, name)
                    w = next_chunk()
                    for q in range(4):
                        mm = pe.matmul(bank_of(name)[32 * q:32 * q + 32, :], c_bc[:, k, :],
                                       w[:, 512 * q:512 * q + 512], start=k == 0, stop=k == KD - 1)
                    if k < KD - 1:
                        mm.then_inc(pre_used, 1)
                    else:
                        ended(mm, name)

            def project_part(n, w, part):
                half, ks = part // 2, range(4 * (part % 2), 4 * (part % 2) + 4)
                for k in ks:
                    mm = pe.matmul(bank_of(f"in{n}")[:, 256 * half:256 * half + 256],
                                   w[:, k, 128 * half:128 * half + 128], hT[:, k, :],
                                   start=k == 0, stop=k == KD - 1)
                if part == 3:
                    ended(mm, f"in{n}")

            def project(n, parts=range(4)):
                open_bank(pe, f"in{n}")
                w = next_chunk().rearrange("p (k m) -> p k m", k=KD)
                for part in parts:
                    project_part(n, w, part)
                return w

            def heads(name, lhsT, rhs, transpose=False):
                open_bank(pe, name)
                for h in range(HEADS):
                    s = slice(P * h, P * h + P)
                    if transpose:
                        mm = pe.transpose(bank_of(name)[:, s], lhsT(h), ident)
                    else:
                        mm = pe.matmul(bank_of(name)[:, s], lhsT(h), rhs(h), start=True, stop=True)
                ended(mm, name)

            def of(tile, t=None):
                return lambda h: tile[:, P * h:P * h + P] if t is None else tile[:, t, P * h:P * h + P]

            pe.wait_ge(S["const_in"], 16)
            pe.wait_ge(S["stage_in"], 16 * 9)
            ended(pe.transpose(bank_of("params")[:, 0:PARAMS], stage, ident[0:PARAMS, 0:PARAMS]), "params")

            pe.wait_ge(S["xn_ready"], 2)
            for j in range(4):
                for k in (2 * j, 2 * j + 1):
                    for t in range(TT):
                        at = 256 * (k % 2) + P * t
                        mm = pe.transpose(bank_of(f"xT{j}")[:, at:at + P], h2[:, t, k * P:k * P + P], ident)
                ended(mm, f"xT{j}")

            pe.wait_ge(S["cb_ready"], 1)
            ada(0, range(KD))
            wait_evac(pe, "ada0")
            for j in range(4):
                mm = pe.transpose(bank_of("modcol")[:, P * j:P * j + P], mod[:, 0, P * j:P * j + P], ident)
            ended(mm, "modcol")

            for j in range(4):
                wait_evac(pe, f"xT{j}")
            pe.wait_ge(S["ba_in"], 16)
            open_bank(pe, "ba")
            for k in range(KD):
                mm = pe.matmul(bank_of("ba")[0:2 * HEADS, 0:SEQ], w_ba[:, k, :], hT[:, k, :],
                               start=k == 0, stop=k == KD - 1)
            ended(mm, "ba")
            project(0)
            wait_evac(pe, "ba")
            open_bank(pe, "baT")
            for t in range(TT):
                mm = pe.transpose(bank_of("baT")[:, 8 * t:8 * t + 8], ba_row[:, P * t:P * t + P],
                                  ident[0:2 * HEADS, 0:2 * HEADS])
            ended(mm, "baT")
            project(1)

            pe.wait_ge(S["gbc_ready"], 1)
            open_bank(pe, "gc")
            ended(pe.matmul(bank_of("gc")[:, 0:TT * HEADS], tri, gts, start=True, stop=True), "gc")
            for t in range(TT):
                heads(f"gcrow{t}", lambda h: g_bc[:, HEADS * t + h, :], lambda h: tri)
            for n in range(2, 10):
                project(n)

            pe.wait_ge(S["qkv_ready"], 6)
            for kind, first in (("k", HEADS), ("q", 0), ("v", 2 * HEADS)):
                for t in range(TT):
                    heads(f"{kind}{t}", lambda h: convT[:, first + h, P * t:P * t + P], None, transpose=True)

            def lru_gate(kind, n, w):
                name = f"lru_{kind}{n}"
                open_bank(pe, name)
                for half in range(2):
                    j = 2 * n + half
                    mm = pe.matmul(bank_of(name)[:, 256 * half:256 * half + 256], w[:, j, :], xcT[:, j, :],
                                   start=True, stop=True)
                ended(mm, name)

            project(10)
            pe.wait_ge(S["gate_w_in"], 16 * 4)
            for n in (6, 7):
                wait_evac(pe, f"in{n}")
            for n in range(2):
                lru_gate("r", n, wa_bd)
            project(11)
            for n in range(2):
                lru_gate("i", n, wx_bd)

            for name, tile, t, value in (("knT0", kn, 0, 1), ("knT1", kn, 1, 2), ("kbT0", kb, 0, 3), ("kbT1", kb, 1, 4),
                                         ("qnT0", qn, 0, 5), ("qnT1", qn, 1, 6), ("qdT", qd, 0, 7)):
                pe.wait_ge(S["kn_ready"], value)
                heads(name, of(tile, t), None, transpose=True)
            project(12)
            ada(1, (0, 1))

            for t in range(TT):
                wait_evac(pe, f"knT{t}")
                wait_evac(pe, f"kbT{t}")
                heads(f"kk{t}", of(knT, t), of(kbT, t))
            for t in range(TT):
                wait_evac(pe, f"qnT{t}")
                heads(f"qk{t}", of(knT, t), of(qnT, t))
            project(13)
            ada(1, (2, 3))
            for t in range(TT):
                pe.wait_ge(S["U0_ready"], t + 1)
                heads(f"T{t}", of(U, t), None, transpose=True)

            for level in range(1, LEVELS):
                for t in range(TT):
                    wait_evac(pe, f"T{t}" if level == 1 else f"PT{level - 1}_{t}")
                    pe.wait_ge(S["mask_ready"], TT * (level - 1) + t + 1)
                    heads(f"X{level}_{t}", of(BM, t), of(T, t))
                for t in range(TT):
                    wait_evac(pe, f"X{level}_{t}")
                    if level > 1:
                        wait_evac(pe, f"PU{level - 1}_{t}")
                    if level < LEVELS - 1:
                        heads(f"PT{level}_{t}", of(U, t), of(X, t))
                    heads(f"PU{level}_{t}", of(X, t), of(U, t))
                last_in = project(13 + level, range(4) if level < LEVELS - 1 else range(1))
                part, k = divmod(2 * (level + 1), KD)
                ada(1 + part, (k, k + 1))

            wait_evac(pe, f"PU{LEVELS - 1}_0")
            heads("vn0", of(U, 0), of(vb, 0))
            project_part(12 + LEVELS, last_in, 1)
            wait_evac(pe, "vn0")
            heads("S", of(kd, 0), of(vn0))
            project_part(12 + LEVELS, last_in, 2)
            wait_evac(pe, "S")
            heads("kS", of(knT, 1), of(state))
            project_part(12 + LEVELS, last_in, 3)
            pe.wait_ge(S["r_ready"], 1)
            wait_evac(pe, f"PU{LEVELS - 1}_1")
            heads("vn1", of(U, 1), of(r_sb))
            for t in range(TT):
                wait_evac(pe, f"qk{t}")
            heads("o0", of(QKT, 0), of(vn0))
            open_bank(pe, "o1")
            wait_evac(pe, "qdT")
            wait_evac(pe, "vn1")
            for h in range(HEADS):
                s = slice(P * h, P * h + P)
                pe.matmul(bank_of("o1")[:, s], qdT[:, 0, s], state[:, s], start=True, stop=False)
                mm = pe.matmul(bank_of("o1")[:, s], QKT[:, 1, s], vn1[:, s], start=False, stop=True)
            ended(mm, "o1")
            pe.wait_ge(S["quad_ready"], 1)
            wait_evac(pe, "ada1")
            wait_evac(pe, "ada2")

            def adaln_row(n):
                open_bank(pe, f"row{n}")
                ended(pe.matmul(bank_of(f"row{n}")[:, :], quad_f if n == 6 else quad[:, n % 4, :],
                                mod[:, 1 + n // 4, :], start=True, stop=True), f"row{n}")

            for n in ROWS[:4]:
                adaln_row(n)
            for t in range(TT):
                wait_evac(pe, f"o{t}")
                heads(f"oT{t}", of(qn, t), None, transpose=True)
            for n in ROWS[4:]:
                adaln_row(n)

            pe.wait_ge(S["lru_out"], 1)
            for t in range(TT):
                wait_evac(pe, f"oT{t}")
            for m in range(4):
                w = next_chunk().rearrange("p (b k m) -> p b k m", b=2, k=4)
                for b, (name, src) in enumerate(((f"bg{m}", zT), (f"bl{m}", xcT))):
                    open_bank(pe, name)
                    for half in range(2):
                        for k in range(4):
                            mm = pe.matmul(bank_of(name)[:, 256 * half:256 * half + 256],
                                           w[:, b, k, 128 * half:128 * half + 128], src[:, k, :],
                                           start=k == 0, stop=k == 3)
                    ended(mm, name)

            w_out_sb = [next_chunk().rearrange("p (k m) -> p k m", k=2) for _ in range(4)]

            def mix(t, half, ks):
                name = f"x{t}{half}"
                if ks[0] == 0:
                    open_bank(pe, name)
                for k in ks:
                    if t == 0 and half == 0 and k % 2 == 0:
                        pe.wait_ge(S["merged_ready"], k // 2 + 1)
                    mm = pe.matmul(bank_of(name)[:, :], mergedT[:, k, P * t:P * t + P],
                                   w_out_sb[k // 2][:, k % 2, 512 * half:512 * half + 512],
                                   start=k == 0, stop=k == KD - 1)
                    if k == KD - 1:
                        ended(mm, name)
                    elif (t, half) == (1, 1) and k % 2:
                        mm.then_inc(pre_used, 1)

            def turn_h2(t):
                for half in range(2):
                    pe.wait_ge(S["h2_ready"], 2 * t + half + 1)
                    open_bank(pe, f"h2T{t}{half}")
                    for k in range(4):
                        at = 512 * half + P * k
                        mm = pe.transpose(bank_of(f"h2T{t}{half}")[:, P * k:P * k + P], h2[:, t, at:at + P], ident)
                    ended(mm, f"h2T{t}{half}")

            def route(t):
                open_bank(pe, f"lgT{t}")
                for k in range(KD):
                    if k % 4 == 0:
                        wait_evac(pe, f"h2T{t}{k // 4}")
                    mm = pe.matmul(bank_of(f"lgT{t}")[0:E, 0:P], wr_sb[:, k, :], hT[:, k, P * t:P * t + P],
                                   start=k == 0, stop=k == KD - 1)
                ended(mm, f"lgT{t}")

            def turn_logits(t):
                wait_evac(pe, f"lgT{t}")
                open_bank(pe, f"lg{t}")
                ended(pe.transpose(bank_of(f"lg{t}")[:, 0:E], lg_row[:, P * t:P * t + P], ident[0:E, 0:E]), f"lg{t}")

            mix(0, 0, range(KD))
            mix(0, 1, range(KD))
            mix(1, 0, range(KD))
            turn_h2(0)
            mix(1, 1, range(3))
            pe.wait_ge(S["router_in"], 16)
            route(0)
            mix(1, 1, range(3, 6))
            turn_logits(0)
            mix(1, 1, range(6, KD))
            turn_h2(1)
            route(1)
            turn_logits(1)

            pe.wait_ge(S["M_ready"], 2)
            open_bank(pe, "count")
            for t in range(TT):
                mm = pe.matmul(bank_of("count")[0:E, 0:1], M[:, t, :], ones[:, 0:1], start=t == 0, stop=t == TT - 1)
            ended(mm, "count")
            open_bank(pe, "pos")
            pe.matmul(bank_of("pos")[:, 0:E], strict, M[:, 0, :], start=True, stop=True)
            pe.matmul(bank_of("pos")[:, E:2 * E], strict, M[:, 1, :], start=True, stop=False)
            ended(pe.matmul(bank_of("pos")[:, E:2 * E], ones, M[:, 0, :], start=False, stop=True), "pos")
            pe.wait_ge(S["pos_ready"], 1)
            open_bank(pe, "posT")
            for t in range(TT):
                mm = pe.transpose(bank_of("posT")[0:E, P * t:P * t + P], pos_m[:, t, :], ident)
            ended(mm, "posT")
            pe.wait_ge(S["count_ready"], 1)
            open_bank(pe, "end")
            ended(pe.matmul(bank_of("end")[0:E, 0:1], tri[0:E, 0:E], cnt[0:E, 1:2], start=True, stop=True), "end")

            def gather():
                for k in range(KD):
                    for t in range(TT):
                        mm = pe.matmul(bank[bHS][:, C64 * k:C64 * k + C64], h2[:, t, P * k:P * k + P], sel[:, t, :],
                                       start=t == 0, stop=t == TT - 1)
                return mm

            pe.wait_ge(S["sel_ready"], 1)
            open_bank(pe, "gathered0")
            ended(gather(), "gathered0")
            pe.wait_ge(S["item_ready"], 1)
            open_bank(pe, "table")
            pe.matmul(bank_of("table")[0:1, 0:ITEMS], ones[0:E, 0:1], cmp_end, start=True, stop=True)
            ended(pe.matmul(bank_of("table")[0:1, ITEMS:ITEMS + 1], ones[0:E, 0:1], cnt[0:E, 1:2],
                            start=True, stop=True), "table")
            wait_evac(pe, "posT")
            open_bank(pe, "pick")
            for t in range(TT):
                dst = bank_of("pick")[:, ITEMS * t:ITEMS * t + ITEMS]
                pe.matmul(dst, posT[:, P * t:P * t + P], one_hot, start=True, stop=False)
                mm = pe.matmul(dst, r64, cmp_end, start=False, stop=True)
            ended(mm, "pick")
            pe.wait_ge(S["G_ready"], 1)
            open_bank(pe, "gateT")
            for t in range(TT):
                mm = pe.transpose(bank_of("gateT")[0:E, P * t:P * t + P], G[:, t, :], ident)
            ended(mm, "gateT")
            wait_evac(pe, "gateT")
            open_bank(pe, "gpick")
            for t in range(TT):
                mm = pe.matmul(bank_of("gpick")[:, ITEMS * t:ITEMS * t + ITEMS], sgT[0:E, P * t:P * t + P], one_hot,
                               start=True, stop=True)
            ended(mm, "gpick")

            for b in range(8):
                pe.wait_ge(evac[b], sum(1 for v in plan.values() if v[0] == b))

            def scatter(signal):
                for t in range(TT):
                    for half, b in enumerate((bO[0], bO[1]) if t == 0 else (bAT, bY)):
                        rows = slice(64 * half, 64 * half + 64)
                        mm = pe.matmul(bank[b][:, :], sgT[rows, P * t:P * t + P], y_sb[rows, :], start=True, stop=True)
                    if t == TT - 1 or signal == "tail_scattered":
                        mm.then_inc(S[signal], 1)

            n_items = pe.value_load(table_i[0:1, ITEMS:ITEMS + 1], min_val=2, max_val=ITEMS - 1)
            with pe.Fori(0, n_items) as i:
                pe.wait_ge(S["hsel_ready"], i + 1)
                pe.wait_ge(S["u_read"], i + 1)
                pe.wait_ge(S["b1_in"], 16 * i + 16)
                for half in range(2):
                    for group in range(2):
                        at = 1024 * group + 512 * half
                        mm = pe.matmul(bank[bU[half]][64 * group:64 * group + 64, :], ones[0:1, 0:C64],
                                       b1_row[:, at:at + 512], start=True, stop=False)
                mm.then_inc(S["b1_used"], 1)
                for k in range(KD):
                    pe.wait_ge(w_loaded[k], 16 * i + 16)
                    w = ring[:, slot_of(k), :]
                    for half in range(2):
                        for group in range(2):
                            at = 1024 * group + 512 * half
                            mm = pe.matmul(bank[bU[half]][64 * group:64 * group + 64, :], hsel[:, k, :],
                                           w[:, at:at + 512], start=False, stop=k == KD - 1)
                    mm.then_inc(w_used[k], 1)
                    if k == 3:
                        pe.wait_ge(S["y_ready"], i + 1)
                        pe.wait_ge(S["sgT_ready"], i + 1)
                        pe.wait_ge(S["x_added"], i + 1)
                        scatter("scattered")
                pe.wait_ge(S["sg_ready"], i + 1)
                for t in range(TT):
                    mm = pe.transpose(bank[bSG][:, P * t:P * t + P], sg[:, t, :], ident)
                mm.then_inc(S["sg_turned"], 1)
                pe.wait_ge(S["sel_ready"], i + 2)
                gather().then_inc(S["gathered"], 1)
                pe.wait_ge(S["x_added"], i + 2)
                pe.wait_ge(S["act_ready"], i + 1)
                for j in range(4):
                    mm = pe.transpose(bank[bAT][:, P * j:P * j + P], act[:, P * j:P * j + P], ident)
                mm.then_inc(S["act_turned"], 1)
                pe.wait_ge(S["actT_ready"], i + 1)
                for c in range(KD, SLOTS):
                    pe.wait_ge(w_loaded[c], 16 * i + 16)
                    w = ring[:, slot_of(c), :].rearrange("p (k n) -> p k n", k=2)
                    for kk in range(2):
                        k = 2 * (c - KD) + kk
                        for group in range(2):
                            mm = pe.matmul(bank[bY][64 * group:64 * group + 64, :],
                                           actT[:, k % 4, 64 * (k // 4):64 * (k // 4) + 64],
                                           w[:, kk, 512 * group:512 * group + 512], start=k == 0, stop=k == KD - 1)
                    mm.then_inc(w_used[c], 1)
            pe.wait_ge(S["y_ready"], n_items + 1)
            pe.wait_ge(S["sgT_ready"], n_items + 1)
            pe.wait_ge(S["x_added"], n_items + 1)
            scatter("tail_scattered")

        @block.vector
        def _(v):
            step = Chain(v, "dve_chain")

            def evacuated(ins, name):
                ins.then_inc(evac[plan[name][0]], 1)

            def head_scale(dst, src, scale, op=ALU.mult):
                return v.tensor_tensor(dst.rearrange("p (h d) -> p h d", h=HEADS), src.rearrange("p (h d) -> p h d", h=HEADS),
                                       scale.rearrange("p (h a) -> p h a", a=1).to_broadcast([P, HEADS, P]), op)

            wait_full(v, "params")
            evacuated(v.tensor_copy(prm[:, :], bank_of("params")[:, 0:PARAMS]), "params")
            v.wait_ge(S["sqrt_x"], 1)
            step(v.reciprocal(rstd, rstd))
            for t in range(TT):
                v.tensor_scalar(h2[:, t, :], x_sb[:, t, :], rstd[:, t:t + 1], None, ALU.mult).then_inc(S["xn_ready"], 1)
            v.wait_ge(S["sig_c"], 1)
            step(v.tensor_tensor(sil, sil, prm[:, R_C:R_C + KD], ALU.mult))
            v.tensor_copy(c_bc, sil.rearrange("p (k a) -> p k a", a=1).to_broadcast([P, KD, 32])).then_inc(S["cb_ready"], 1)

            def ada_rows(part):
                wait_full(v, f"ada{part}")
                v.wait_ge(S["bias_late" if part else "bias_in"], 16 * (8 if part else 4))
                evacuated(v.tensor_tensor(mod[:, part, :], bank_of(f"ada{part}")[:, :], mod_bias[:, part, :], ALU.add),
                          f"ada{part}")

            ada_rows(0)
            wait_full(v, "modcol")
            turned = bank_of("modcol")[:, :].rearrange("p (j q r) -> p q j r", j=4, q=4)
            for n in range(4):
                dst = modcol[:, 4 * n:4 * n + 4].rearrange("p (j r) -> p j r", r=1)
                src = turned[:, n, :, 0:1]
                if n < 2:
                    step(v.tensor_copy(dst, src))
                else:
                    gain = prm[:, R_NORM_MIX + 4 * n - KD:R_NORM_MIX + 4 * n - KD + 4]
                    ins = v.scalar_tensor_tensor(dst, src, 1.0, gain.rearrange("p (j r) -> p j r", r=1), ALU.add, ALU.mult)
                    if n == 2:
                        step(ins)
            evacuated(ins, "modcol")
            wait_evac(v, "modcol")
            for k in range(4):
                name = f"xT{k // 2}"
                wait_full(v, name)
                ins = v.tensor_scalar(hT[:, k, :], bank_of(name)[:, 256 * (k % 2):256 * (k % 2) + 256],
                                      modcol[:, KD + k:KD + k + 1], modcol[:, k:k + 1], ALU.mult, ALU.add)
                if k % 2:
                    evacuated(ins, name)

            wait_full(v, "baT")
            v.wait_ge(S["row_in"], 16 * 3)
            ba = bank_of("baT")[:, 0:16].rearrange("p (t n) -> p t n", t=TT)
            v.tensor_tensor(spx[:, 0:8].rearrange("p (t h) -> p t h", t=TT), ba[:, :, HEADS:2 * HEADS],
                            dt_b.rearrange("p (a h) -> p a h", a=1).to_broadcast([P, TT, HEADS]), ALU.add)\
                .then_inc(S["ba_read"], 1)
            v.wait_ge(S["ba_read"], 1)
            step(v.tensor_scalar(spx[:, 8:12], prm[:, R_LAM:R_LAM + LT], -1.0, None, ALU.mult))
            v.scalar_tensor_tensor(sp_s, spx, -1.0, spx, ALU.mult, ALU.min).then_inc(S["sp_in"], 1)
            v.wait_ge(S["sp_exp"], 1)
            step(v.tensor_scalar(sp_d, sp_t, 2.0, None, ALU.add))
            step(v.reciprocal(sp_d, sp_d))
            step(v.tensor_tensor(sp_s, sp_t, sp_d, ALU.mult))
            step(v.tensor_tensor(sp_s2, sp_s, sp_s, ALU.mult))
            step(v.tensor_scalar(sp_p, sp_s2, 1.0 / 17, None, ALU.mult))
            for n in (15, 13, 11, 9, 7, 5, 3):
                step(v.scalar_tensor_tensor(sp_p, sp_p, 1.0 / n, sp_s2, ALU.add, ALU.mult))
            step(v.scalar_tensor_tensor(sp_p, sp_p, 1.0, sp_s, ALU.add, ALU.mult))
            step(v.tensor_scalar(sp_d, spx, 0.0, None, ALU.max))
            step(v.scalar_tensor_tensor(sp_d, sp_p, 2.0, sp_d, ALU.mult, ALU.add))
            step(v.tensor_scalar(lam_c, sp_d[:, 8:12], -LRU_C, None, ALU.mult))
            v.scalar_tensor_tensor(gts.rearrange("p (t h) -> p t h", t=TT), sp_d[:, 0:8].rearrange("p (t h) -> p t h", t=TT),
                                   -1.0, a_exp.rearrange("p (a h) -> p a h", a=1).to_broadcast([P, TT, HEADS]),
                                   ALU.mult, ALU.mult).then_inc(S["g_ready"], 1)
            v.wait_ge(S["g_ready"], 1)
            v.tensor_copy(g_bc, gts.rearrange("p (n a) -> p n a", a=1).to_broadcast([P, TT * HEADS, P]))\
                .then_inc(S["gbc_ready"], 1)

            def conv(n, dst, weight, bias, signal):
                name = f"in{n}"
                wait_full(v, name)
                for half in range(2):
                    src = bank_of(name)[:, 256 * half:256 * half + 256]
                    o, w = dst[:, half, :], weight(half)
                    if bias is None:
                        step(v.tensor_scalar(o, src, w[CONV - 1], None, ALU.mult))
                    else:
                        step(v.tensor_scalar(o, src, w[CONV - 1], bias(half), ALU.mult, ALU.add))
                    for tap in range(CONV - 1):
                        back = CONV - 1 - tap
                        ins = v.scalar_tensor_tensor(o[:, back:], src[:, :SEQ - back], w[tap], o[:, back:],
                                                     ALU.mult, ALU.add)
                        if half and tap == CONV - 2:
                            evacuated(ins, name)
                            wait_evac(v, name)
                        else:
                            step(ins)

            def qkv_conv(n):
                def weight(half):
                    return [prm[:, R_GCONV + 12 * tap + 2 * n + half:][:, 0:1] for tap in range(CONV)]
                conv(n, convT[:, 2 * n:2 * n + 2, :], weight, None, None)

            def qkv_silu(n):
                v.wait_ge(S["conv_sig"], n + 1)
                v.tensor_tensor(convT[:, 2 * n:2 * n + 2, :], convT[:, 2 * n:2 * n + 2, :], conv_sg(n), ALU.mult)\
                    .then_inc(S["qkv_ready"], 1)

            qkv_conv(0)
            qkv_conv(1)
            qkv_silu(0)
            wait_full(v, "gc")
            evacuated(v.tensor_copy(gc, bank_of("gc")[:, 0:TT * HEADS]), "gc")
            wait_evac(v, "gc")
            for t in range(TT):
                wait_full(v, f"gcrow{t}")
                evacuated(head_scale(Dm[:, t, :], bank_of(f"gcrow{t}")[:, :], gc[:, HEADS * t:HEADS * t + HEADS],
                                     ALU.subtract), f"gcrow{t}")
                wait_evac(v, f"gcrow{t}")
                v.tensor_scalar(Dm[:, t, :], Dm[:, t, :], 0.0, None, ALU.min).then_inc(S["diff_ready"], 1)
            for n in range(2, 6):
                qkv_conv(n)
                qkv_silu(n - 1)
                if n == 2:
                    v.wait_ge(S["decay_ready"], 1)
                    step(v.tensor_copy(ekd.rearrange("p (h a) -> p h a", a=1),
                                       Dm[:, 0, :].rearrange("p (h c) -> p h c", h=HEADS)[:, :, P - 1:P]))
                    for t in range(TT):
                        step(v.tensor_tensor(Dm[:, t, :].rearrange("p (h c) -> p h c", h=HEADS),
                                             Dm[:, t, :].rearrange("p (h c) -> p h c", h=HEADS),
                                             tri.rearrange("p (a c) -> p a c", a=1).to_broadcast([P, HEADS, P]), ALU.mult))
                    step(v.tensor_tensor(be, beta, egc, ALU.mult))
            qkv_silu(5)
            for n in (6, 7):
                j = 2 * (n - 6)
                conv(n, xcT[:, j:j + 2, :],
                     lambda half: [prm[:, R_LCONV + LT * tap + j + half:][:, 0:1] for tap in range(CONV)],
                     lambda half: prm[:, R_LCONV_B + j + half:][:, 0:1], None)

            for n in range(4):
                wait_evac(v, ("k0", "k1", "q0", "q1")[n])
                v.tensor_reduce(ss[:, 4 * n:4 * n + 4], sq[:, n % 2, :].rearrange("p (h d) -> p h d", h=HEADS),
                                AX.X, ALU.add).then_inc(S["ss_ready"], 1)
            for t in range(TT):
                wait_full(v, f"v{t}")
                evacuated(head_scale(vb[:, t, :], bank_of(f"v{t}")[:, :], beta[:, HEADS * t:HEADS * t + HEADS]), f"v{t}")
            v.wait_ge(S["rs_sqrt"], 1)
            step(v.reciprocal(rs, rs))
            step(v.tensor_scalar(rs[:, 8:16], rs[:, 8:16], float(HD) ** -0.5, None, ALU.mult))
            wait_evac(v, "q1")

            def scaled(dst, src, scale):
                head_scale(dst, src, scale).then_inc(S["kn_ready"], 1)

            for t in range(TT):
                scaled(kn[:, t, :], k_tok[:, t, :], rs[:, 4 * t:4 * t + 4])
            v.wait_ge(S["kn_ready"], 2)
            for t in range(TT):
                scaled(kb[:, t, :], kn[:, t, :], beta[:, 4 * t:4 * t + 4])
            for t in range(TT):
                scaled(qn[:, t, :], q_tok[:, t, :], rs[:, 8 + 4 * t:12 + 4 * t])
            v.wait_ge(S["kn_ready"], 6)
            scaled(qd[:, 0, :], qn[:, 1, :], egc[:, 4:8])
            scaled(kd[:, 0, :], kn[:, 0, :], ekd)

            def silu_z(n):
                v.wait_ge(S["z_sig"], n - 9)
                evacuated(v.tensor_tensor(zT[:, 2 * (n - 10):2 * (n - 10) + 2, :], zT[:, 2 * (n - 10):2 * (n - 10) + 2, :],
                                          bank_of(f"in{n}")[:, :].rearrange("p (a n) -> p a n", a=2), ALU.mult), f"in{n}")

            silu_z(10)
            silu_z(11)
            for name, dst in (("knT1", knT[:, 1, :]), ("kbT1", kbT[:, 1, :]), ("qnT1", qnT[:, 1, :])):
                wait_full(v, name)
                evacuated(v.tensor_copy(dst, bank_of(name)[:, :]), name)
            for t in range(TT):
                wait_full(v, f"kk{t}")
                ins = v.tensor_tensor(Bm[:, t, :], bank_of(f"kk{t}")[:, :], Dm[:, t, :], ALU.mult)
                evacuated(ins, f"kk{t}")
                wait_evac(v, f"kk{t}")
                step(v.tensor_tensor(U[:, t, :].rearrange("p (h c) -> p h c", h=HEADS),
                                     Bm[:, t, :].rearrange("p (h c) -> p h c", h=HEADS), level_mask(0), ALU.mult))
                v.tensor_tensor(U[:, t, :].rearrange("p (h c) -> p h c", h=HEADS),
                                ident.rearrange("p (a c) -> p a c", a=1).to_broadcast([P, HEADS, P]),
                                U[:, t, :].rearrange("p (h c) -> p h c", h=HEADS), ALU.subtract)\
                    .then_inc(S["U0_ready"], 1)
            for t in range(TT):
                wait_full(v, f"qk{t}")
                evacuated(v.tensor_tensor(QKT[:, t, :], bank_of(f"qk{t}")[:, :], Dm[:, t, :], ALU.mult), f"qk{t}")
            v.wait_ge(S["U0_ready"], TT)
            for level in range(1, LEVELS):
                for t in range(TT):
                    if level > 1:
                        wait_evac(v, f"PU{level - 1}_{t}")
                    if level < LEVELS - 1:
                        name = f"PT{level}_{t}"
                        wait_full(v, name)
                        wait_evac(v, f"T{t}" if level == 1 else f"PT{level - 1}_{t}")
                        evacuated(v.tensor_tensor(T[:, t, :], T[:, t, :], bank_of(name)[:, :], ALU.subtract), name)
                    name = f"PU{level}_{t}"
                    wait_full(v, name)
                    evacuated(v.tensor_tensor(U[:, t, :], U[:, t, :], bank_of(name)[:, :], ALU.subtract), name)
                if level == 2:
                    ada_rows(1)
                if level == 3:
                    v.wait_ge(S["lru_b"], 1)
                    for j in range(LT):
                        step(v.tensor_tensor_scan(xcT[:, j, :], lru_a[:, j, :], lru_i[:, j, :], 0.0, ALU.mult, ALU.add))
                    v.tensor_tensor(xcT[:, :, :], xcT[:, :, :], ybT[:, :, :], ALU.mult).then_inc(S["lru_out"], 1)
                    v.wait_ge(S["lru_out"], 1)
                    for q in (2, 3):
                        step(v.tensor_copy(quad_f[:, 64 * (q - 2):64 * (q - 1)],
                                           cst[:, C_QUAD + q:C_QUAD + q + 1].to_broadcast([P, 64])))
                    v.tensor_copy(quad, cst[:, C_QUAD:C_QUAD + 4].rearrange("p (q a) -> p q a", a=1)
                                  .to_broadcast([P, 4, P])).then_inc(S["quad_ready"], 1)
            ada_rows(2)

            wait_full(v, "kS")
            evacuated(head_scale(ks_sb, bank_of("kS")[:, :], be[:, 4:8]), "kS")
            wait_evac(v, "kS")
            wait_evac(v, "v1")
            v.tensor_tensor(r_sb, vb[:, 1, :], ks_sb, ALU.subtract).then_inc(S["r_ready"], 1)
            for t in range(TT):
                v.wait_ge(S["o_sq"], t + 1)
                v.tensor_reduce(oss[:, 4 * t:4 * t + 4], o_sqr[:, t, :].rearrange("p (h d) -> p h d", h=HEADS),
                                AX.X, ALU.add).then_inc(S["oss_ready"], 1)
            v.wait_ge(S["o_sqrt"], 1)
            step(v.reciprocal(oss, oss))
            for t in range(TT):
                evacuated(head_scale(qn[:, t, :], bank_of(f"o{t}")[:, :], oss[:, 4 * t:4 * t + 4]), f"o{t}")
            for t in range(TT):
                wait_full(v, f"oT{t}")
                zt = zT[:, :, P * t:P * t + P]
                evacuated(v.scalar_tensor_tensor(zt, bank_of(f"oT{t}")[:, :].rearrange("p (h c) -> p h c", h=HEADS),
                                                 prm[:, R_NORM_W:R_NORM_W + 1], zt, ALU.mult, ALU.mult), f"oT{t}")
            v.wait_ge(S["norm_in"], 16)
            for n in (4, 5):
                wait_full(v, f"row{n}")
                s = slice(512 * (n % 2), 512 * (n % 2) + 512)
                evacuated(v.scalar_tensor_tensor(norm_ffn_b[:, s], bank_of(f"row{n}")[:, :], 1.0, norm_ffn_b[:, s],
                                                 ALU.add, ALU.mult), f"row{n}")
            for n in ROWS:
                wait_evac(v, f"row{n}")
            for m in range(4):
                def gate(b):
                    return gatesT[:, KD * b + 2 * m:KD * b + 2 * m + 2, :].rearrange("p a n -> p (a n)")
                dst = mergedT[:, 2 * m:2 * m + 2, :].rearrange("p a n -> p (a n)")
                wait_full(v, f"bg{m}")
                wait_evac(v, f"in{12 + m}")
                wait_evac(v, f"in{16 + m}")
                evacuated(v.tensor_tensor(mtmp[m % 2], bank_of(f"bg{m}")[:, :], gate(0), ALU.mult), f"bg{m}")
                wait_full(v, f"bl{m}")
                evacuated(v.tensor_tensor(dst, bank_of(f"bl{m}")[:, :], gate(1), ALU.mult), f"bl{m}")
                wait_evac(v, f"bg{m}")
                wait_evac(v, f"bl{m}")
                v.tensor_tensor(dst, dst, mtmp[m % 2], ALU.add).then_inc(S["merged_ready"], 1)
            v.wait_ge(S["merged_ready"], 4)
            step(v.memset(sgT, 0.0))
            v.memset(y_sb, 0.0).then_inc(S["y_zero"], 1)
            def mixed(t, half):
                name = f"x{t}{half}"
                s = slice(512 * half, 512 * half + 512)
                wait_full(v, name)
                evacuated(v.tensor_tensor(h2[:, t, s], bank_of(name)[:, :], gate_m_b[:, s], ALU.mult), name)
                wait_evac(v, name)
                v.tensor_tensor(x_sb[:, t, s], x_sb[:, t, s], h2[:, t, s], ALU.add).then_inc(S["x1_ready"], 1)
                v.wait_ge(S["x1_ready"], 2 * t + half + 1)
                step(v.tensor_tensor(h2[:, t, s], x_sb[:, t, s], norm_ffn_b[:, s], ALU.mult))

            def ffn_norm(t):
                v.wait_ge(S["sqrt_x1"], t + 1)
                step(v.reciprocal(rstd[:, t:t + 1], rstd[:, t:t + 1]))
                for half in range(2):
                    s = slice(512 * half, 512 * half + 512)
                    v.scalar_tensor_tensor(h2[:, t, s], h2[:, t, s], rstd[:, t:t + 1], shift_f_b[:, s],
                                           ALU.mult, ALU.add).then_inc(S["h2_ready"], 1)

            def top4(t):
                wait_full(v, f"lg{t}")
                evacuated(v.tensor_tensor(logit[:, t, :], bank_of(f"lg{t}")[:, 0:E], br_b, ALU.add), f"lg{t}")
                wait_evac(v, f"lg{t}")
                best = m8[:, 8 * t:8 * t + 8]
                step(v.max(best, logit[:, t, :]))
                step(v.max_index(idx_u[:, 8 * t:8 * t + 8], best, logit[:, t, :]))
                step(v.tensor_copy(idx_f[:, 8 * t:8 * t + 8], idx_u[:, 8 * t:8 * t + 8]))
                step(v.tensor_tensor(eq[:, TOPK * t:TOPK * t + TOPK, :],
                                     cst[:, C_EXPERT:C_EXPERT + E].rearrange("p (a e) -> p a e", a=1).to_broadcast([P, TOPK, E]),
                                     idx_f[:, 8 * t:8 * t + TOPK].rearrange("p (k a) -> p k a", a=1).to_broadcast([P, TOPK, E]),
                                     ALU.is_equal))
                v.tensor_reduce(M[:, t, :], eq[:, TOPK * t:TOPK * t + TOPK, :].rearrange("p k e -> p e k"),
                                AX.X, ALU.add).then_inc(S["M_ready"], 1)
                v.tensor_scalar(negm[:, t:t + 1], best[:, 0:1], -1.0, None, ALU.mult).then_inc(S["top_ready"], 1)

            mixed(0, 0)
            mixed(0, 1)
            ffn_norm(0)
            mixed(1, 0)
            top4(0)
            mixed(1, 1)
            ffn_norm(1)
            wait_full(v, "h2T10")
            evacuated(v.tensor_copy(hT[:, 0:4, P:2 * P], bank_of("h2T10")[:, :].rearrange("p (a n) -> p a n", a=4)), "h2T10")
            top4(1)
            v.wait_ge(S["M_ready"], 2)
            wait_full(v, "count")
            evacuated(v.tensor_copy(cnt[0:E, 0:1], bank_of("count")[0:E, 0:1]), "count")
            wait_evac(v, "count")
            step(v.tensor_scalar(cnt[0:E, 1:2], cnt[0:E, 0:1], C64 + 0.5, 1.0, ALU.is_gt, ALU.add))
            step(v.scalar_tensor_tensor(cnt[0:E, 1:2], cnt[0:E, 0:1], 2 * C64 + 0.5, cnt[0:E, 1:2], ALU.is_gt, ALU.add))
            v.scalar_tensor_tensor(cnt[0:E, 1:2], cnt[0:E, 0:1], 3 * C64 + 0.5, cnt[0:E, 1:2], ALU.is_gt, ALU.add)\
                .then_inc(S["count_ready"], 1)
            v.wait_ge(S["count_ready"], 1)
            wait_full(v, "pos")
            Mf, posf = M.rearrange("p t e -> p (t e)"), pos_m.rearrange("p t e -> p (t e)")
            evacuated(v.scalar_tensor_tensor(posf, Mf, -4096.0, bank_of("pos")[:, 0:TT * E], ALU.mult, ALU.add), "pos")
            wait_evac(v, "pos")
            v.tensor_scalar(posf, posf, 4096.0, None, ALU.add).then_inc(S["pos_ready"], 1)
            v.wait_ge(S["pos_ready"], 1)

            def select(column):
                for t in range(TT):
                    ins = v.tensor_scalar(sel[:, t, :], cst[:, C_SLOT:C_SLOT + C64], column(t), None, ALU.is_equal)
                ins.then_inc(S["sel_ready"], 1)

            select(lambda t: pos_m[:, t, 0:1])
            wait_full(v, "end")
            evacuated(v.tensor_copy(cnt[0:E, 2:3], bank_of("end")[0:E, 0:1]), "end")
            wait_evac(v, "end")
            step(v.tensor_tensor(cnt[0:E, 3:4], cnt[0:E, 2:3], cnt[0:E, 1:2], ALU.subtract))
            item = cst[:, C_ITEM:C_ITEM + ITEMS]
            step(v.tensor_scalar(cmp_end, item[0:E, :], cnt[0:E, 2:3], None, ALU.is_ge))
            step(v.scalar_tensor_tensor(one_hot, item[0:E, :], cnt[0:E, 3:4], cmp_end, ALU.is_ge, ALU.subtract))
            v.tensor_scalar(r64, ones[0:E, :], cnt[0:E, 1:2], float(C64), ALU.mult, ALU.mult).then_inc(S["item_ready"], 1)
            v.wait_ge(S["gates_exp"], 2)
            step(v.reciprocal(gsum, gsum))
            step(v.tensor_tensor(gk.rearrange("p (t k) -> p t k", t=TT), gk.rearrange("p (t k) -> p t k", t=TT),
                                 gsum.rearrange("p (t a) -> p t a", a=1).to_broadcast([P, TT, TOPK]), ALU.mult))
            step(v.tensor_tensor(eqg, eq, gk.rearrange("p (n a) -> p n a", a=1).to_broadcast([P, TT * TOPK, E]), ALU.mult))
            for t in range(TT):
                ins = v.tensor_reduce(G[:, t, :], eqg[:, TOPK * t:TOPK * t + TOPK, :].rearrange("p k e -> p e k"),
                                      AX.X, ALU.add)
            ins.then_inc(S["G_ready"], 1)
            wait_full(v, "table")
            evacuated(v.tensor_copy(table_i[0:1, :], bank_of("table")[0:1, 0:ITEMS + 1]), "table")
            wait_evac(v, "table")
            wait_full(v, "pick")
            for t in range(TT):
                ins = v.scalar_tensor_tensor(pos_i[:, t, :], item, -float(C64), bank_of("pick")[:, ITEMS * t:ITEMS * t + ITEMS],
                                             ALU.mult, ALU.add)
                if t == TT - 1:
                    evacuated(ins, "pick")
                    wait_evac(v, "pick")
                else:
                    step(ins)
            wait_full(v, "gpick")
            evacuated(v.tensor_copy(gate_i.rearrange("p t n -> p (t n)"), bank_of("gpick")[:, 0:TT * ITEMS]), "gpick")
            wait_evac(v, "gpick")
            v.wait_ge(S["b2_in"], 16 * 2)
            v.tensor_tensor(y_sb, y_sb, gate_f_h, ALU.mult).then_inc(S["y_ready"], 1)
            v.sem_inc(S["x_added"], 1)
            v.sem_inc(S["u_read"], 1)

            def add_scattered(n):
                v.wait_ge(S["scattered"], n)
                v.wait_ge(S["x_added"], n)
                for t in range(TT):
                    for half, b in enumerate((bO[0], bO[1]) if t == 0 else (bAT, bY)):
                        xs = x_sb[:, t, 512 * half:512 * half + 512]
                        ins = v.tensor_tensor(xs, xs, bank[b][:, :], ALU.add)
                ins.then_inc(S["x_added"], 1)

            n_items = v.value_load(table_i[0:1, ITEMS:ITEMS + 1], min_val=2, max_val=ITEMS - 1)
            with v.Fori(0, n_items) as i:
                v.wait_ge(S["gathered"], i + 1)
                for t in range(TT):
                    ins = v.tensor_scalar(sel[:, t, :], cst[:, C_SLOT:C_SLOT + C64], pos_i[:, t, ds(i + 1, 1)], None,
                                          ALU.is_equal)
                ins.then_inc(S["sel_ready"], 1)
                add_scattered(i + 1)
                for t in range(TT):
                    ins = v.tensor_scalar(sg[:, t, :], cst[:, C_SLOT:C_SLOT + 2 * C64], pos_i[:, t, ds(i, 1)],
                                          gate_i[:, t, ds(i, 1)], ALU.is_equal, ALU.mult)
                ins.then_inc(S["sg_ready"], 1)
                v.wait_ge(w_used[KD - 1], i + 1)
                u = [bank[b][:, :].rearrange("p (f two) -> p f two", two=2) for b in bU]
                for half in range(2):
                    ins = v.tensor_scalar(glu[:, 256 * half:256 * half + 256].rearrange("p (f a) -> p f a", a=1),
                                          u[half][:, :, 0:1], SW_LIMIT, None, ALU.min)
                ins.then_inc(S["glu_ready"], 1)
                for half in range(2):
                    ins = v.tensor_scalar(lin[:, 256 * half:256 * half + 256].rearrange("p (f a) -> p f a", a=1),
                                          u[half][:, :, 1:2], SW_LIMIT, -SW_LIMIT, ALU.min, ALU.max)
                ins.then_inc(S["u_read"], 1)
                v.wait_ge(S["u_read"], i + 2)
                v.scalar_tensor_tensor(lin, lin, 1.0, glu, ALU.add, ALU.mult).then_inc(S["gl_ready"], 1)
                v.wait_ge(S["gl_ready"], i + 1)
                v.wait_ge(S["sig_ready"], i + 1)
                v.tensor_tensor(act, lin, sig, ALU.mult).then_inc(S["act_ready"], 1)
                v.wait_ge(w_used[SLOTS - 1], i + 1)
                v.tensor_tensor(y_sb, bank[bY][:, :], gate_f_h, ALU.mult).then_inc(S["y_ready"], 1)
            v.wait_ge(S["x_added"], n_items + 1)
            for t in range(TT):
                v.wait_ge(S["tail_scattered"], t + 1)
                for half, b in enumerate((bO[0], bO[1]) if t == 0 else (bAT, bY)):
                    xs = x_sb[:, t, 512 * half:512 * half + 512]
                    v.tensor_tensor(xs, xs, bank[b][:, :], ALU.add).then_inc(S["x2_ready"], 1)
            v.wait_ge(S["x2_ready"], 2 * TT)
            v.wait_ge(S["late_in"], 16)
            for t in range(TT):
                v.wait_ge(S["sqrt_x2"], t + 1)
                step(v.reciprocal(rstd[:, t:t + 1], rstd[:, t:t + 1]))
                for half in range(2):
                    s = slice(512 * half, 512 * half + 512)
                    v.scalar_tensor_tensor(h2[:, t, s], x_sb[:, t, s], rstd[:, t:t + 1], norm_fin_b[:, s],
                                           ALU.mult, ALU.mult).then_inc(S["out_ready"], 1)

        @block.scalar
        def _(a):
            step = Chain(a, "act_chain")

            def evacuated(ins, name):
                ins.then_inc(evac[plan[name][0]], 1)

            a.dma_start(cst[:, :], consts).then_inc(S["const_in"], 16)
            a.dma_start(w_ba[:, :, :], w_in[0, :, IN_BA:IN_X].rearrange("(k p) m -> p k m", p=P)).then_inc(S["ba_in"], 16)
            a.dma_start(a_exp, gdn_a_log.to_broadcast([P, HEADS])).then_inc(S["row_in"], 16)
            a.dma_start(dt_b, gdn_dt_bias.to_broadcast([P, HEADS])).then_inc(S["row_in"], 16)
            a.dma_start(br_b, b_router.to_broadcast([P, E])).then_inc(S["row_in"], 16)
            a.dma_start(wr_sb[:, :, :], w_router[0].rearrange("(k p) e -> p k e", p=P)).then_inc(S["router_in"], 16)

            for b in (1, 2):
                for q in range(4):
                    at = 2048 * b + 512 * q
                    a.dma_start(mod_bias[32 * q:32 * q + 32, b, :], b_ada[0:1, at:at + 512].to_broadcast([32, 512]))\
                        .then_inc(S["bias_late"], 16)
            a.wait_ge(S["x_in"], 16 * TT)
            for t in range(TT):
                step(a.activation(h2[:, t, :], x_sb[:, t, :], ACT.Square, accum_out=ssx[:, t:t + 1]))
            a.wait_ge(S["const_in"], 16)
            a.activation(rstd, ssx, ACT.Sqrt, scale=1.0 / D, bias=eps).then_inc(S["sqrt_x"], 1)
            wait_evac(a, "params")
            a.activation(sil, prm[:, R_C:R_C + KD], ACT.Sigmoid).then_inc(S["sig_c"], 1)
            wait_evac(a, "modcol")
            for k in range(4, KD):
                name = f"xT{k // 2}"
                wait_full(a, name)
                ins = a.activation(hT[:, k, :], bank_of(name)[:, 256 * (k % 2):256 * (k % 2) + 256], ACT.Identity,
                                   scale=modcol[:, KD + k:KD + k + 1], bias=modcol[:, k:k + 1])
                if k % 2:
                    evacuated(ins, name)
            wait_full(a, "ba")
            evacuated(a.activation(ba_row, bank_of("ba")[0:2 * HEADS, 0:SEQ], ACT.Copy), "ba")
            a.wait_ge(S["ba_read"], 1)
            evacuated(a.activation(beta.rearrange("p (t h) -> p t h", t=TT),
                                   bank_of("baT")[:, 0:16].rearrange("p (t n) -> p t n", t=TT)[:, :, 0:HEADS],
                                   ACT.Sigmoid), "baT")
            a.wait_ge(S["row_in"], 16 * 3)
            step(a.activation(a_exp, a_exp, ACT.Exp))
            a.wait_ge(S["sp_in"], 1)
            a.activation(sp_t, sp_s, ACT.Exp).then_inc(S["sp_exp"], 1)

            def conv_sigmoid(n):
                wait_evac(a, f"in{n}")
                a.activation(conv_sg(n), convT[:, 2 * n:2 * n + 2, :], ACT.Sigmoid).then_inc(S["conv_sig"], 1)

            conv_sigmoid(0)
            conv_sigmoid(1)
            a.wait_ge(S["diff_ready"], TT)
            step(a.activation(egc, gc, ACT.Exp))
            a.activation(Dm, Dm, ACT.Exp).then_inc(S["decay_ready"], 1)
            for n in range(2, 6):
                conv_sigmoid(n)
            for n in (8, 9):
                wait_full(a, f"in{n}")
                evacuated(a.activation(ybT[:, 2 * (n - 8):2 * (n - 8) + 2, :],
                                       bank_of(f"in{n}")[:, :].rearrange("p (a n) -> p a n", a=2), ACT.Copy), f"in{n}")
            for n, name in enumerate(("k0", "k1", "q0", "q1")):
                wait_full(a, name)
                if n >= 2:
                    a.wait_ge(S["ss_ready"], n - 1)
                step(a.activation((k_tok, q_tok)[n // 2][:, n % 2, :], bank_of(name)[:, :], ACT.Copy))
                evacuated(a.activation(sq[:, n % 2, :], bank_of(name)[:, :], ACT.Square), name)
            a.wait_ge(S["ss_ready"], 4)
            a.activation(rs, ss, ACT.Sqrt, bias=eps).then_inc(S["rs_sqrt"], 1)
            def z_sigmoid(n):
                wait_full(a, f"in{n}")
                a.activation(zT[:, 2 * (n - 10):2 * (n - 10) + 2, :],
                             bank_of(f"in{n}")[:, :].rearrange("p (a n) -> p a n", a=2), ACT.Sigmoid).then_inc(S["z_sig"], 1)

            def lru_sigmoid(kind, n, dst, row):
                name = f"lru_{kind}{n}"
                wait_full(a, name)
                for half in range(2):
                    j = 2 * n + half
                    ins = a.activation(dst[:, j, :], bank_of(name)[:, 256 * half:256 * half + 256], ACT.Sigmoid,
                                       bias=prm[:, row + j:row + j + 1])
                evacuated(ins, name)

            z_sigmoid(10)
            for n in range(2):
                lru_sigmoid("r", n, lru_r, R_BA)
            z_sigmoid(11)
            for n in range(2):
                lru_sigmoid("i", n, lru_i, R_BX)
            a.wait_ge(S["yb_arg"], 1)
            a.activation(lru_a, lru_a, ACT.Sigmoid, scale=GELU_B).then_inc(S["yb_sig"], 1)
            for name, dst in (("knT0", knT[:, 0, :]), ("kbT0", kbT[:, 0, :]), ("qnT0", qnT[:, 0, :]), ("qdT", qdT[:, 0, :])):
                wait_full(a, name)
                evacuated(a.activation(dst, bank_of(name)[:, :], ACT.Copy), name)

            def gate_sigmoid(n):
                wait_full(a, f"in{n}")
                evacuated(a.activation(gatesT[:, 2 * (n - 12):2 * (n - 12) + 2, :],
                                       bank_of(f"in{n}")[:, :].rearrange("p (a n) -> p a n", a=2), ACT.Sigmoid), f"in{n}")

            gate_sigmoid(12)
            a.wait_ge(S["yb_done"], 1)
            a.wait_ge(S["g_ready"], 1)
            for n in range(2):
                wait_evac(a, f"lru_r{n}")
            for j in range(LT):
                step(a.activation(lru_a[:, j, :], lru_r[:, j, :], ACT.Exp, scale=lam_c[:, j:j + 1]))
            for j in range(LT):
                ins = a.activation(lru_r[:, j, :], lru_r[:, j, :], ACT.Tanh, scale=lam_c[:, j:j + 1])
            ins.then_inc(S["lru_exp"], 1)
            gate_sigmoid(13)
            for t in range(TT):
                wait_full(a, f"T{t}")
                evacuated(a.activation(T[:, t, :], bank_of(f"T{t}")[:, :], ACT.Copy), f"T{t}")
            for level in range(1, LEVELS):
                for t in range(TT):
                    wait_full(a, f"X{level}_{t}")
                    if level > 1:
                        wait_full(a, f"PU{level - 1}_{t}")
                    evacuated(a.activation(X[:, t, :], bank_of(f"X{level}_{t}")[:, :], ACT.Copy), f"X{level}_{t}")
                if level == 2:
                    a.wait_ge(S["lru_m"], 1)
                    a.activation(xcT[:, :, :], xcT[:, :, :], ACT.Sqrt).then_inc(S["lru_sqrt"], 1)
                if level < LEVELS - 1:
                    gate_sigmoid(13 + level)
            wait_full(a, f"X{LEVELS - 1}_1")
            a.dma_start(norm_ffn_b, norm_ffn.to_broadcast([P, D])).then_inc(S["norm_in"], 16)
            for name, dst in (("vn0", vn0), ("S", state), ("vn1", vn1)):
                wait_full(a, name)
                evacuated(a.activation(dst, bank_of(name)[:, :], ACT.Copy), name)
            gate_sigmoid(12 + LEVELS)
            for t in range(TT):
                wait_full(a, f"o{t}")
                a.activation(o_sqr[:, t, :], bank_of(f"o{t}")[:, :], ACT.Square).then_inc(S["o_sq"], 1)
            a.wait_ge(S["oss_ready"], 2)
            a.activation(oss, oss, ACT.Sqrt, scale=1.0 / HD, bias=eps).then_inc(S["o_sqrt"], 1)
            for n in ROWS:
                if n in (4, 5):
                    continue
                wait_full(a, f"row{n}")
                dst = gate_f_h if n == 6 else (gate_m_b, shift_f_b)[n // 2][:, 512 * (n % 2):512 * (n % 2) + 512]
                evacuated(a.activation(dst, bank_of(f"row{n}")[:, :], ACT.Copy), f"row{n}")
            a.dma_start(norm_fin_b, norm_final.rearrange("(a n) -> a n", a=1).to_broadcast([P, D])).then_inc(S["late_in"], 16)
            a.wait_ge(S["y_zero"], 1)
            for half in range(2):
                a.dma_start(y_sb[64 * half:64 * half + E, :], b2[0, :, 512 * half:512 * half + 512])\
                    .then_inc(S["b2_in"], 16)

            def half_sums(src, scratch, t, ready, signal):
                for half in range(2):
                    a.wait_ge(S[ready], 2 * t + half + 1)
                    s = slice(512 * half, 512 * half + 512)
                    step(a.activation(scratch(t, s), src[:, t, s], ACT.Square,
                                      accum_out=ssh[:, 2 * t + half:2 * t + half + 1]))
                    if half == 0:
                        step(a.activation(ssb[:, t:t + 1], ssh[:, 2 * t:2 * t + 1], ACT.Identity, scale=1.0 / D, bias=eps))
                a.activation(rstd[:, t:t + 1], ssh[:, 2 * t + 1:2 * t + 2], ACT.Sqrt, scale=1.0 / D,
                             bias=ssb[:, t:t + 1]).then_inc(S[signal], 1)

            def take_h2T(t, half):
                name = f"h2T{t}{half}"
                wait_full(a, name)
                evacuated(a.activation(hT[:, 4 * half:4 * half + 4, P * t:P * t + P],
                                       bank_of(name)[:, :].rearrange("p (a n) -> p a n", a=4), ACT.Copy), name)

            def take_logits(t):
                wait_full(a, f"lgT{t}")
                evacuated(a.activation(lg_row[:, P * t:P * t + P], bank_of(f"lgT{t}")[0:E, 0:P], ACT.Copy), f"lgT{t}")

            half_sums(x_sb, lambda t, s: squares, 0, "x1_ready", "sqrt_x1")
            take_h2T(0, 0)
            take_h2T(0, 1)
            take_logits(0)
            half_sums(x_sb, lambda t, s: squares, 1, "x1_ready", "sqrt_x1")
            take_h2T(1, 1)
            take_logits(1)
            step(a.activation(warm, eps, ACT.Exp))
            wait_full(a, "posT")
            evacuated(a.activation(posT, bank_of("posT")[0:E, 0:SEQ], ACT.Copy), "posT")
            a.wait_ge(S["top_ready"], TT)
            for t in range(TT):
                a.activation(gk[:, TOPK * t:TOPK * t + TOPK], m8[:, 8 * t:8 * t + TOPK], ACT.Exp, bias=negm[:, t:t + 1],
                             accum_out=gsum[:, t:t + 1]).then_inc(S["gates_exp"], 1)
            wait_full(a, "gathered0")
            evacuated(a.activation(hsel, bank[bHS][:, :].rearrange("p (k s) -> p k s", k=KD), ACT.Copy), "gathered0")
            wait_evac(a, "gathered0")
            a.sem_inc(S["gathered"], 1)
            a.sem_inc(S["hsel_ready"], 1)
            wait_full(a, "gateT")
            a.activation(sgT[64:64 + E, :], bank_of("gateT")[0:E, 0:SEQ], ACT.Copy).then_inc(S["sgT_ready"], 1)
            evacuated(a.activation(sgT[0:E, :], bank_of("gateT")[0:E, 0:SEQ], ACT.Copy), "gateT")

            wait_evac(a, "table")
            n_items = a.value_load(table_i[0:1, ITEMS:ITEMS + 1], min_val=2, max_val=ITEMS - 1)
            with a.Fori(0, n_items) as i:
                a.wait_ge(S["glu_ready"], i + 1)
                a.activation(sig, glu, ACT.Sigmoid, scale=SW_ALPHA).then_inc(S["sig_ready"], 1)
                a.wait_ge(S["sg_turned"], i + 1)
                a.activation(sgT, bank[bSG][:, 0:SEQ], ACT.Copy).then_inc(S["sgT_ready"], 1)
                a.wait_ge(S["gathered"], i + 2)
                a.activation(hsel, bank[bHS][:, :].rearrange("p (k s) -> p k s", k=KD), ACT.Copy).then_inc(S["hsel_ready"], 1)
                a.wait_ge(S["act_turned"], i + 1)
                a.activation(actT, bank[bAT][:, :].rearrange("p (j s) -> p j s", j=4), ACT.Copy).then_inc(S["actT_ready"], 1)
            step(a.activation(warm, eps, ACT.Sqrt))
            for t in range(TT):
                half_sums(x_sb, lambda t, s: h2[:, t, s], t, "x2_ready", "sqrt_x2")

        @block.gpsimd
        def _(g):
            step = Chain(g, "pool_chain")
            wait_full(g, "params")
            step(g.memset(lru_ws[:, 0:1024], 0.0))
            for dst, src in ((wa_bd, lru_w_a), (wx_bd, lru_w_x)):
                pairs = src[0].rearrange("(j two) c d -> two c j d", two=2)
                for i in range(2):
                    g.dma_start(dst[64 * i:64 * i + 64, :, 64 * i:64 * i + 64], pairs[i]).then_inc(S["gate_w_in"], 16)
            for n in (8, 9):
                wait_evac(g, f"in{n}")
            step(g.tensor_tensor(lru_a, ybT[:, :, :], ybT[:, :, :], ALU.mult))
            step(g.tensor_scalar(lru_a, lru_a, GELU_A, 1.0, ALU.mult, ALU.add))
            g.tensor_tensor(lru_a, lru_a, ybT[:, :, :], ALU.mult).then_inc(S["yb_arg"], 1)
            g.wait_ge(S["yb_sig"], 1)
            g.tensor_tensor(ybT[:, :, :], ybT[:, :, :], lru_a, ALU.mult).then_inc(S["yb_done"], 1)
            def mask(level):
                for t in range(TT):
                    if level == 1:
                        wait_evac(g, f"kk{t}")
                    else:
                        wait_full(g, f"X{level - 1}_{t}")
                    g.tensor_tensor(BM[:, t, :].rearrange("p (h c) -> p h c", h=HEADS),
                                    Bm[:, t, :].rearrange("p (h c) -> p h c", h=HEADS), level_mask(level), ALU.mult)\
                        .then_inc(S["mask_ready"], 1)
            for n in range(2):
                wait_evac(g, f"lru_i{n}")
            step(g.tensor_tensor(lru_i, lru_i, xcT[:, :, :], ALU.mult))
            mask(1)
            g.wait_ge(S["lru_exp"], 1)
            step(g.tensor_tensor(xcT[:, :, :], lru_a, lru_a, ALU.mult))
            step(g.tensor_scalar(xcT[:, :, :], xcT[:, :, :], 1.0, None, ALU.add))
            mask(2)
            step(g.tensor_tensor(xcT[:, :, :], xcT[:, :, :], lru_r, ALU.mult))
            g.tensor_scalar(xcT[:, :, :], xcT[:, :, :], -1.0, 0.0, ALU.mult, ALU.max).then_inc(S["lru_m"], 1)
            mask(3)
            g.wait_ge(S["lru_sqrt"], 1)
            g.tensor_tensor(lru_i, lru_i, xcT[:, :, :], ALU.mult).then_inc(S["lru_b"], 1)
            for level in range(4, LEVELS):
                mask(level)


INPUTS = ["x", "c", "w_ada", "b_ada", "norm_mix", "norm_ffn", "w_in", "gdn_conv_w", "gdn_a_log", "gdn_dt_bias",
          "gdn_norm_w", "lru_conv_w", "lru_conv_b", "lru_w_a", "lru_b_a", "lru_w_x", "lru_b_x", "lru_lambda",
          "w_branch_gdn", "w_branch_lru", "w_out", "w_router", "b_router", "w1", "b1", "w2", "b2", "norm_final"]


def kernel(**inputs):
    import concourse.bacc as bacc
    from concourse.bass_utils import run_bass_kernel_spmd

    nc = bacc.Bacc("TRN2", target_bir_lowering=False, num_devices=1)
    arrays, args = {}, []
    for name in INPUTS:
        arrays[f"in_{name}"] = np.ascontiguousarray(inputs[name])
    arrays["in_consts"] = constants()
    for name, a in arrays.items():
        args.append(nc.dram_tensor(name, a.shape, mybir.dt.from_np(a.dtype), kind="ExternalInput").ap())
    args.append(nc.dram_tensor("out_x", (1, SEQ, D), F32, kind="ExternalOutput").ap())
    hybrid_block(nc, *args)
    return run_bass_kernel_spmd(nc, [arrays], core_ids=[0]).results[0]["out_x"]
```

```python
from contextlib import ExitStack

import numpy as np
import concourse.bass as bass
from concourse import mybir

F32 = mybir.dt.float32
I32 = mybir.dt.int32
U32 = mybir.dt.uint32
ALU = mybir.AluOpType
ACT = mybir.ActivationFunctionType
AX = mybir.AxisListType
ds = bass.ds

P = 128
SEQ, D = 256, 1024
TT = SEQ // P
KD = D // P
HEADS, HD = 4, 128
GW = HEADS * HD
LW = D // 2
LT = LW // P
CONV = 4
E, TOPK, FF = 32, 4, D
C64 = 64
ROW_LOADS = 4 * 7
XT_AT = 4
SCATTER_AT = 2
BIAS_AT = 5
ITEMS = 48
EPS = 1e-6
SW_ALPHA, SW_LIMIT = 1.702, 7.0
LRU_C = 8.0
GELU_A, GELU_B = 0.044715, 2.0 * 0.7978845608028654
BANK = 512
LEVELS = 7

C_IDENT = 0
C_TRI = C_IDENT + P
C_STRICT = C_TRI + P
C_ONES = C_STRICT + P
C_SLOT = C_ONES + P
C_EXPERT = C_SLOT + 2 * C64
C_ITEM = C_EXPERT + E
C_EPS = C_ITEM + ITEMS
C_INDEX = C_EPS + 1
C_REST = C_INDEX + 1
C_KEY = C_REST + 1
C_FOLD = C_KEY + 1
C_LEVEL = C_FOLD + 32
CONSTS = C_LEVEL + LEVELS * P
TIE = 2.0 ** -16
FIRST = 0

R_C = 0
R_NORM_MIX = R_C + KD
R_GCONV = R_NORM_MIX + KD
R_LCONV = R_GCONV + CONV * 3 * HEADS
R_LCONV_B = R_LCONV + CONV * LT
R_BA = R_LCONV_B + LT
R_BX = R_BA + LT
R_LAM = R_BX + LT
R_NORM_W = R_LAM + LT
PARAMS = R_NORM_W + 1

HALF = 6
SLOTS = 12
IN_Z, IN_BA = 3 * GW, 4 * GW
IN_X = 4 * GW + 2 * HEADS
IN_G = IN_X + 2 * LW
STREAM = [("ada", 0, k) for k in range(KD)]
STREAM += [("in", 256 * j, 0) for j in range(6)]
STREAM += [("in", IN_X + 256 * j, 0) for j in range(4)]
STREAM += [("in", IN_Z + 256 * j, 0) for j in range(2)]
for _j in range(8):
    STREAM += [("in", IN_G + 256 * _j, 0)]
    STREAM += [("ada", 1 + (2 * _j) // KD, (2 * _j + a) % KD) for a in range(2)]
STREAM += [("branch", 256 * j, 0) for j in range(4)]
STREAM += [("out", 0, j) for j in range(4)]


def constants():
    a = np.zeros((P, CONSTS), np.float32)
    r = np.arange(P)
    s, c = r[:, None], r[None, :]
    a[:, C_IDENT:C_IDENT + P] = s == c
    a[:, C_TRI:C_TRI + P] = s <= c
    a[:, C_STRICT:C_STRICT + P] = s < c
    for level in range(LEVELS):
        b = 1 << level
        a[:, C_LEVEL + level * P:C_LEVEL + (level + 1) * P] = (
            (s // (2 * b) == c // (2 * b)) & (s % (2 * b) < b) & (c % (2 * b) >= b))
    a[:, C_ONES:C_ONES + P] = 1
    a[:, C_SLOT:C_SLOT + 2 * C64] = np.tile(np.arange(C64), 2)
    a[:, C_EXPERT:C_EXPERT + E] = np.arange(E)
    a[:, C_ITEM:C_ITEM + ITEMS] = np.arange(ITEMS)
    a[:, C_EPS] = EPS
    a[:, C_FOLD:C_FOLD + 32] = s % 32 == c[:, :32]
    a[:, C_INDEX] = r
    a[:, C_REST] = r != FIRST
    a[:, C_KEY] = np.where(r == FIRST, -1, r * TIE)
    return a


def bank_plan():
    order = [("params", 0), ("xT0", 4), ("xT1", 5), ("xT2", 6), ("xT3", 7), ("ada0", 1), ("modcol", 2), ("ba", 2)]
    order += [("in0", 0), ("baT", 2), ("in1", 3), ("gc", 2), ("gcrow0", 6), ("gcrow1", 7)]
    order += [(f"in{n}", 4 if n == 2 else (0, 3)[n % 2]) for n in range(2, 10)]
    order += [("k0", 4), ("k1", 5), ("q0", 6), ("q1", 7), ("v0", 2), ("v1", 4)]
    order += [("in10", 0), ("in11", 3), ("lru_r0", 6), ("lru_r1", 5), ("lru_i0", 7), ("lru_i1", 6)]
    order += [("knT0", 4), ("knT1", 5), ("kbT0", 6), ("kbT1", 7), ("qnT0", 2), ("qnT1", 4), ("qdT", 5)]
    order += [("in12", 0), ("ada1", 1), ("kk0", 6), ("kk1", 7), ("qk0", 2), ("qk1", 4), ("in13", 3), ("T0", 5), ("T1", 6)]
    for level in range(1, LEVELS):
        order += [(f"X{level}_0", 4), (f"X{level}_1", 5)]
        for t in range(TT):
            if level < LEVELS - 1:
                order += [(f"PT{level}_{t}", (6, 2)[t])]
            order += [(f"PU{level}_{t}", (7, 3 if level % 2 else 0)[t])]
        order += [(f"in{13 + level}", 0 if level % 2 else 3)]
    order += [("ada2", 1)]
    order += [("vn0", 4), ("S", 5), ("kS", 6), ("vn1", 7), ("o0", 4), ("o1", 5)]
    order += [("oT0", 6), ("oT1", 7)]
    for m in range(4):
        order += [(f"bl{m}", (0, 2)[m % 2]), (f"bg{m}", (4, 6)[m % 2])]
    order += [("x00", 4), ("x01", 5), ("x10", 6), ("h2T00", 0), ("h2T01", 1), ("x11", 7), ("lgT0", 2), ("lg0", 3)]
    order += [("h2T10", 0), ("h2T11", 1), ("lgT1", 2), ("lg1", 4)]
    order += [("count", 5), ("pos", 6), ("posT", 0), ("gathered0", 2), ("rank", 7), ("keys", 3), ("end", 5),
              ("table", 1), ("gateT", 7), ("pick", 6), ("gpick", 5)]
    uses, plan = [0] * 8, {}
    for name, bank in order:
        plan[name] = (bank, uses[bank])
        uses[bank] += 1
    return plan


def hybrid_block(nc, x, cond, w_ada, b_ada, norm_mix, norm_ffn, w_in, gdn_conv_w, gdn_a_log, gdn_dt_bias, gdn_norm_w,
                 lru_conv_w, lru_conv_b, lru_w_a, lru_b_a, lru_w_x, lru_b_x, lru_lambda, w_branch_gdn, w_branch_lru,
                 w_out, w_router, b_router, w1, b1, w2, b2, norm_final, consts, out):
    plan = bank_plan()
    with ExitStack() as ctx:
        def sb(name, shape, dt=F32):
            return ctx.enter_context(nc.sbuf_tensor(name, shape, dt))

        def sem(name):
            return ctx.enter_context(nc.semaphore(name))

        ring = sb("ring", [P, SLOTS, 2048])
        cst = sb("cst", [P, CONSTS])
        x_sb = sb("x_sb", [P, TT, D])
        hT = sb("hT", [P, KD, SEQ])
        mergedT = hT
        h2 = sb("h2", [P, TT, D])
        lru_ws = sb("lru_ws", [P, 2048])
        area = sb("area", [P, 14 * 512])
        zT = sb("zT", [P, HEADS, SEQ])
        xcT = sb("xcT", [P, LT, SEQ])
        ybT = sb("ybT", [P, LT, SEQ])
        gatesT = sb("gatesT", [P, 2 * KD, SEQ])
        modreg = sb("modreg", [P, 3072])
        prm = sb("prm", [P, PARAMS])
        w_ba = sb("w_ba", [P, KD, 32])
        wr_sb = sb("wr_sb", [P, KD, E])
        small = sb("small", [P, 640])
        idx_u = sb("idx_u", [P, 2 * 8], U32)
        table_i = sb("table_i", [1, ITEMS + 1], I32)

        def view(t, at, shape):
            return t[:, at:at + shape[0] * shape[1]].rearrange("p (a b) -> p a b", b=shape[1])

        ident = cst[:, C_IDENT:C_IDENT + P]
        tri = cst[:, C_TRI:C_TRI + P]
        strict = cst[:, C_STRICT:C_STRICT + P]
        ones = cst[:, C_ONES:C_ONES + P]
        eps = cst[:, C_EPS:C_EPS + 1]

        def level_mask(level):
            return cst[:, C_LEVEL + level * P:C_LEVEL + (level + 1) * P].rearrange("p (a b) -> p a b", a=1)\
                .to_broadcast([P, HEADS, P])

        spare = ring[:, HALF:SLOTS, :].rearrange("p s n -> p (s n)")

        def work(n, tiles=TT):
            return spare[:, 512 * n:512 * (n + tiles)].rearrange("p (t n) -> p t n", t=tiles)

        k_tok, q_tok, v_tok = work(0), work(2), work(4)
        kn, kb, qn = work(6), work(8), work(10)
        qd, kd = work(12, 1), work(13, 1)
        knT, kbT, qnT, qdT = work(14), work(16), work(18), work(20, 1)
        vb = v_tok
        vn0, state, vn1 = k_tok[:, 0, :], k_tok[:, 1, :], kb[:, 0, :]
        ks_sb, r_sb, o_sqr = q_tok[:, 0, :], q_tok[:, 1, :], kn

        def conv_sg(n):
            return spare[:, 512 * (14 + n):512 * (15 + n)].rearrange("p (a n) -> p a n", a=2)

        convT = view(area, 0, (3 * HEADS, SEQ))
        U, T, X = (view(area, 1024 * n, (TT, 512)) for n in range(3))
        Bm, BM, QKT, Dm = (view(area, 3072 + 1024 * n, (TT, 512)) for n in range(4))
        sq = view(area, 3072 + 1024, (TT, 512))
        gate_m_b, shift_f_b, scale_f_b, gate_f_b, norm_ffn_b, norm_fin_b = (
            area[:, 1024 * n:1024 * (n + 1)] for n in range(6))
        gate_f_h = gate_f_b[:, 0:512]
        g_bc = view(area, 3072, (TT * HEADS, P))

        stage = lru_ws[0:PARAMS, 1024:1024 + P]
        wa_bd, wx_bd = view(lru_ws, 0, (LT, P)), view(lru_ws, 512, (LT, P))
        lru_a = view(lru_ws, 1024, (LT, SEQ))
        h2_flat = h2[:, :, :].rearrange("p t n -> p (t n)")
        lru_r, lru_i = view(h2_flat, 0, (LT, SEQ)), view(h2_flat, 1024, (LT, SEQ))

        mod = view(modreg, 0, (3, 512))
        mod_bias = view(modreg, 1536, (3, 512))
        b1_row = modreg[0:1, 0:2048]

        g_flat = gatesT[:, :, :].rearrange("p t n -> p (t n)")
        hsel = view(g_flat, 0, (KD, C64))
        glu, sig, lin, act = (g_flat[:, 512 * n:512 * (n + 1)] for n in range(1, 5))
        actT = view(g_flat, 512 * 5, (4, P))
        y_sb = g_flat[:, 512 * 6:512 * 7]
        sgT = g_flat[:, 512 * 7:512 * 7 + SEQ]
        sel = view(g_flat, 512 * 7 + 256, (TT, C64))
        z_flat = zT[:, :, :].rearrange("p t n -> p (t n)")
        sg = view(z_flat, 0, (TT, P))
        pos_i, gate_i = view(z_flat, 256, (TT, ITEMS)), view(z_flat, 352, (TT, ITEMS))
        posT = z_flat[0:E, 448:704]
        xc_flat = xcT[:, :, :].rearrange("p t n -> p (t n)")
        eq, eqg = view(xc_flat, 0, (TT * TOPK, E)), view(xc_flat, 256, (TT * TOPK, E))
        M, G, pos_m = (view(xc_flat, 512 + 64 * n, (TT, E)) for n in range(3))
        cmp_end, one_hot = xc_flat[0:E, 704:704 + ITEMS], xc_flat[0:E, 752:752 + ITEMS]
        key_diag, before = xc_flat[0:E, 800:800 + E], xc_flat[0:E, 832:832 + E]
        yb_flat = ybT[:, :, :].rearrange("p t n -> p (t n)")
        mtmp = [yb_flat[:, 0:512], yb_flat[:, 512:1024]]
        squares = yb_flat[:, 0:512]
        ba_row = yb_flat[:, 0:SEQ]
        lg_row = mod_bias[:, 1, 0:SEQ]
        fold = cst[:, C_FOLD:C_FOLD + 32]

        def col(n, w=1):
            return small[:, n:n + w]

        ssx, rstd = col(0, 2), col(2, 2)
        ssh, ssb = col(608, 4), col(612, 2)
        warm = col(614)
        modcol = col(4, 16)
        beta, spx, gts = col(20, 8), col(28, 12), col(40, 8)
        sp_t, sp_s, sp_s2, sp_p, sp_d = col(48, 12), col(60, 12), col(72, 12), col(84, 12), col(96, 12)
        gc, egc, ekd, rs = col(108, 8), col(116, 8), col(124, 4), col(128, 16)
        ss = col(144, 16)
        a_exp, dt_b = col(160, 4), col(164, 4)
        be = col(168, 8)
        lam_c = col(176, 4)
        oss = col(184, 8)
        m8 = col(192, 16)
        idx_f = col(208, 16)
        gk, gsum, negm = col(224, 8), col(232, 2), col(234, 2)
        br_b = col(240, E)
        cnt = col(272, 8)
        n_tok, n_item, key, end, start, start64 = (cnt[0:E, n:n + 1] for n in range(6))
        kinds, rank, total = (col(615 + 2 * n, 2)[0:E, :] for n in range(3))
        sil = col(280, KD)
        logit = view(small, 288, (TT, E))
        c_bc = view(small, 352, (KD, 32))

        bank = [ctx.enter_context(nc.psum_tensor(f"bank{i}", [P, BANK], F32)) for i in range(8)]
        bU, bHS, bAT, bY, bO, bSG = (0, 1), 2, 3, 4, (5, 6), 7

        full = [sem(f"bank_full{i}") for i in range(8)]
        evac = [sem(f"bank_evacuated{i}") for i in range(8)]
        pre_loaded = [sem(f"pre_loaded{i}") for i in range(HALF)]
        pre_used = sem("pre_used")
        w_loaded = [sem(f"w_loaded{i}") for i in range(SLOTS)]
        w_used = [sem(f"w_used{i}") for i in range(SLOTS)]
        names = """const_in stage_in x_in bias_in bias_late masks_in ba_zero ba_in norm_in y_zero row_in gate_w_in
            router_in late_in b2_in b1_in dve_chain act_chain pool_chain sqrt_x xn_ready sig_c cb_ready ba_read sp_in sp_exp g_ready gbc_ready
            diff_ready decay_ready conv_sig qkv_ready z_sig ss_ready rs_sqrt kn_ready U0_ready mask_ready
            r_ready o_sq oss_ready o_sqrt yb_arg yb_sig yb_done lru_exp lru_m lru_sqrt lru_b lru_out
            rows_in merged_ready x1_ready sqrt_x1 h2_ready top_ready gates_exp G_ready M_ready kinds_ready
            key_ready start_ready item_ready pos_ready sel_ready gathered hsel_ready b1_used scattered y_ready sgT_ready
            x_added u_read sg_ready sg_turned glu_ready sig_ready act_ready act_turned actT_ready
            gl_ready x2_ready sqrt_x2 tail_scattered out_ready out_stored""".split()
        S = {n: sem(n) for n in names}

        class Chain:
            def __init__(self, eng, name):
                self.eng, self.sem, self.n = eng, S[name], 0

            def __call__(self, ins):
                self.n += 1
                ins.then_inc(self.sem, 1)
                self.eng.wait_ge(self.sem, self.n)

        def bank_of(name):
            return bank[plan[name][0]]

        def open_bank(pe, name):
            b, n = plan[name]
            if n:
                pe.wait_ge(evac[b], n)

        def wait_full(eng, name):
            b, n = plan[name]
            eng.wait_ge(full[b], n + 1)

        def wait_evac(eng, name):
            b, n = plan[name]
            eng.wait_ge(evac[b], n + 1)

        def slot_of(c):
            return (HALF + c) % SLOTS

        block = ctx.enter_context(nc.Block())

        def release(n):
            kind, a, b = STREAM[n]
            if kind == "in":
                b, u = plan[f"in{[m for m in range(len(STREAM)) if STREAM[m][0] == 'in'].index(n)}"]
                return full[b], u + 1
            if kind == "branch":
                b, u = plan[f"bg{a // 256}"]
                return full[b], u + 1
            if kind == "ada" and b == KD - 1:
                b, u = plan[f"ada{a}"]
                return full[b], u + 1
            if kind == "out" and b == 3:
                b, u = plan["x11"]
                return full[b], u + 1
            before = [m for m in range(n + 1) if (STREAM[m][0] == "ada" and STREAM[m][2] < KD - 1)
                      or (STREAM[m][0] == "out" and STREAM[m][2] < 3)]
            return pre_used, len(before)

        def load_rows(eng, at, src):
            n = src.shape[0] // P
            eng.dma_start(stage[at:at + n, :], src.rearrange("(n p) -> n p", p=P)).then_inc(S["stage_in"], 16)

        @block.sync
        def _(sp):
            sp.dma_start(cst[:, 0:C_LEVEL], consts[:, 0:C_LEVEL]).then_inc(S["const_in"], 16)
            load_rows(sp, R_LCONV_B, lru_conv_b[0])
            sp.dma_start(x_sb[:, 0, :], x[0, 0:P, :]).then_inc(S["x_in"], 16)
            load_rows(sp, R_BA, lru_b_a[0])
            load_rows(sp, R_BX, lru_b_x[0])
            sp.dma_start(x_sb[:, 1, :], x[0, P:2 * P, :]).then_inc(S["x_in"], 16)
            load_rows(sp, R_LAM, lru_lambda[0])
            for n, (kind, a, b) in enumerate(STREAM):
                if n >= HALF:
                    sp.wait_ge(*release(n - HALF))
                dst, loaded = ring[:, n % HALF, :], pre_loaded[n % HALF]
                if kind == "ada":
                    sp.dma_start(dst, w_ada[0, b * P:(b + 1) * P, a * 2048:(a + 1) * 2048]).then_inc(loaded, 16)
                elif kind == "in":
                    sp.dma_start(dst.rearrange("p (k m) -> p k m", k=KD),
                                 w_in[0, :, a:a + 256].rearrange("(k p) m -> p k m", p=P)).then_inc(loaded, 16)
                elif kind == "branch":
                    halves = dst.rearrange("p (b k m) -> p b k m", b=2, k=4)
                    for i, w in enumerate((w_branch_gdn, w_branch_lru)):
                        sp.dma_start(halves[:, i], w[0, :, a:a + 256].rearrange("(k p) m -> p k m", p=P))\
                            .then_inc(loaded, 16)
                else:
                    sp.dma_start(dst.rearrange("p (k m) -> p k m", k=2),
                                 w_out[0, b * 256:(b + 1) * 256, :].rearrange("(k p) m -> p k m", p=P))\
                        .then_inc(loaded, 16)

            def load_expert(e, wait_free):
                for c in range(SLOTS):
                    if c == BIAS_AT:
                        wait_free(None)
                        sp.dma_start(b1_row, b1[0, ds(e, 1), :]).then_inc(S["b1_in"], 16)
                    wait_free(c)
                    dst = ring[:, slot_of(c), :]
                    if c < KD:
                        rows = w1[0, ds(e, 1), c * P:(c + 1) * P, :].rearrange("a p n -> p (a n)")
                    else:
                        k = 2 * (c - KD)
                        dst = dst.rearrange("p (k n) -> p k n", k=2)
                        rows = w2[0, ds(e, 1), k * P:(k + 2) * P, :].rearrange("a (k p) n -> p (a k) n", p=P)
                    sp.dma_start(dst, rows).then_inc(w_loaded[c], 16)

            def first_free(c):
                if c is None:
                    sp.wait_ge(S["rows_in"], 16 * ROW_LOADS)
                elif c == 0:
                    wait_full(sp, "oT1")
                elif c >= HALF:
                    slot = slot_of(c)
                    sp.wait_ge(*release(max(m for m in range(len(STREAM)) if m % HALF == slot)))

            load_expert(FIRST, first_free)
            wait_evac(sp, "table")
            n_items = sp.value_load(table_i[0:1, ITEMS:ITEMS + 1], min_val=2, max_val=ITEMS - 1)
            with sp.Fori(1, n_items) as i:
                now = sp.value_load(table_i[0:1, ds(i, 1)], min_val=0, max_val=E - 1)
                before = sp.value_load(table_i[0:1, ds(i - 1, 1)], min_val=0, max_val=E - 1)
                with sp.If(now != before):
                    load_expert(now, lambda c: sp.wait_ge(S["b1_used"] if c is None else w_used[c], i))
                with sp.Else():
                    for chunk in range(SLOTS):
                        if chunk == BIAS_AT:
                            sp.wait_ge(S["b1_used"], i)
                            sp.sem_inc(S["b1_in"], 16)
                        sp.wait_ge(w_used[chunk], i)
                        sp.sem_inc(w_loaded[chunk], 16)
            for t in range(TT):
                for half in range(2):
                    s = slice(512 * half, 512 * half + 512)
                    sp.wait_ge(S["out_ready"], 2 * t + half + 1)
                    sp.dma_start(out[0, t * P:(t + 1) * P, s], h2[:, t, s]).then_inc(S["out_stored"], 16)
            sp.wait_ge(S["out_stored"], 16 * 2 * TT)

        @block.tensor
        def _(pe):
            position = [0]

            def next_chunk():
                n = position[0]
                position[0] += 1
                loads = sum(2 if STREAM[m][0] == "branch" else 1 for m in range(n % HALF, n + 1, HALF))
                pe.wait_ge(pre_loaded[n % HALF], 16 * loads)
                return ring[:, n % HALF, :]

            def ended(mm, name):
                mm.then_inc(full[plan[name][0]], 1)

            def ada(part, ks):
                name = f"ada{part}"
                for k in ks:
                    if k == 0:
                        open_bank(pe, name)
                    w = next_chunk()
                    for q in range(4):
                        mm = pe.matmul(bank_of(name)[32 * q:32 * q + 32, :], c_bc[:, k, :],
                                       w[:, 512 * q:512 * q + 512], start=k == 0, stop=k == KD - 1)
                    if k < KD - 1:
                        mm.then_inc(pre_used, 1)
                    else:
                        ended(mm, name)

            def project_part(n, w, part):
                half, ks = part // 2, range(4 * (part % 2), 4 * (part % 2) + 4)
                for k in ks:
                    mm = pe.matmul(bank_of(f"in{n}")[:, 256 * half:256 * half + 256],
                                   w[:, k, 128 * half:128 * half + 128], hT[:, k, :],
                                   start=k == 0, stop=k == KD - 1)
                if part == 3:
                    ended(mm, f"in{n}")

            def project(n, parts=range(4)):
                open_bank(pe, f"in{n}")
                w = next_chunk().rearrange("p (k m) -> p k m", k=KD)
                for part in parts:
                    project_part(n, w, part)
                return w

            def heads(name, lhsT, rhs, transpose=False):
                open_bank(pe, name)
                for h in range(HEADS):
                    s = slice(P * h, P * h + P)
                    if transpose:
                        mm = pe.transpose(bank_of(name)[:, s], lhsT(h), ident)
                    else:
                        mm = pe.matmul(bank_of(name)[:, s], lhsT(h), rhs(h), start=True, stop=True)
                ended(mm, name)

            def of(tile, t=None):
                return lambda h: tile[:, P * h:P * h + P] if t is None else tile[:, t, P * h:P * h + P]

            def keep_warm(name, n):
                open_bank(pe, name)
                for _ in range(n):
                    pe.matmul(bank_of(name)[:, 0:P], ident, tri, start=True, stop=True)

            def narrow(name, n, w, src):
                for k in range(KD // 4):
                    for q in range(4):
                        mm = pe.matmul(bank_of(name)[32 * q:32 * q + 32, 0:n], w[:, 2 * q + k, :], src[:, 2 * q + k, :],
                                       start=k == 0, stop=k == KD // 4 - 1)
                ended(mm, name)

            pe.wait_ge(S["const_in"], 16)
            pe.wait_ge(S["stage_in"], 16 * 9)
            ended(pe.transpose(bank_of("params")[:, 0:PARAMS], stage, ident[0:PARAMS, 0:PARAMS]), "params")

            pe.wait_ge(S["cb_ready"], 1)
            ada(0, range(XT_AT))
            pe.wait_ge(S["xn_ready"], 2)
            for j in range(4):
                for k in (2 * j, 2 * j + 1):
                    for t in range(TT):
                        at = 256 * (k % 2) + P * t
                        mm = pe.transpose(bank_of(f"xT{j}")[:, at:at + P], h2[:, t, k * P:k * P + P], ident)
                ended(mm, f"xT{j}")
            for k in range(XT_AT, KD):
                ada(0, (k,))
                keep_warm("modcol", 4)
            wait_evac(pe, "ada0")
            for j in range(4):
                mm = pe.transpose(bank_of("modcol")[:, P * j:P * j + P], mod[:, 0, P * j:P * j + P], ident)
            ended(mm, "modcol")

            wait_evac(pe, "modcol")
            keep_warm("ba", 5)
            for j in range(4):
                wait_evac(pe, f"xT{j}")
            pe.wait_ge(S["ba_in"], 16)
            open_bank(pe, "ba")
            narrow("ba", SEQ, w_ba, hT[:, :, :])
            project(0)
            wait_evac(pe, "ba")
            open_bank(pe, "baT")
            for t in range(TT):
                mm = pe.matmul(bank_of("baT")[:, 8 * t:8 * t + 8], ba_row[:, P * t:P * t + P], fold[:, 0:2 * HEADS],
                               start=True, stop=True)
            ended(mm, "baT")
            project(1)
            project(2)

            pe.wait_ge(S["gbc_ready"], 1)
            open_bank(pe, "gc")
            ended(pe.matmul(bank_of("gc")[:, 0:TT * HEADS], tri, gts, start=True, stop=True), "gc")
            for t in range(TT):
                heads(f"gcrow{t}", lambda h: g_bc[:, HEADS * t + h, :], lambda h: tri)
            for n in range(3, 10):
                project(n)

            pe.wait_ge(S["qkv_ready"], 6)
            for kind, first in (("k", HEADS), ("q", 0), ("v", 2 * HEADS)):
                for t in range(TT):
                    heads(f"{kind}{t}", lambda h: convT[:, first + h, P * t:P * t + P], None, transpose=True)

            def lru_gate(kind, n, w):
                name = f"lru_{kind}{n}"
                open_bank(pe, name)
                for half in range(2):
                    j = 2 * n + half
                    mm = pe.matmul(bank_of(name)[:, 256 * half:256 * half + 256], w[:, j, :], xcT[:, j, :],
                                   start=True, stop=True)
                ended(mm, name)

            project(10)
            project(11)
            pe.wait_ge(S["gate_w_in"], 16 * 4)
            for n in (6, 7):
                wait_evac(pe, f"in{n}")
            for n in range(2):
                lru_gate("r", n, wa_bd)
            for n in range(2):
                lru_gate("i", n, wx_bd)

            for name, tile, t, value in (("knT0", kn, 0, 1), ("knT1", kn, 1, 2), ("kbT0", kb, 0, 3), ("kbT1", kb, 1, 4),
                                         ("qnT0", qn, 0, 5), ("qnT1", qn, 1, 6), ("qdT", qd, 0, 7)):
                pe.wait_ge(S["kn_ready"], value)
                heads(name, of(tile, t), None, transpose=True)
            project(12)
            ada(1, (0, 1))

            for t in range(TT):
                wait_evac(pe, f"knT{t}")
                wait_evac(pe, f"kbT{t}")
                heads(f"kk{t}", of(knT, t), of(kbT, t))
            for t in range(TT):
                wait_evac(pe, f"qnT{t}")
                heads(f"qk{t}", of(knT, t), of(qnT, t))
            project(13)
            ada(1, (2, 3))
            for t in range(TT):
                pe.wait_ge(S["U0_ready"], t + 1)
                heads(f"T{t}", of(U, t), None, transpose=True)

            for level in range(1, LEVELS):
                for t in range(TT):
                    wait_evac(pe, f"T{t}" if level == 1 else f"PT{level - 1}_{t}")
                    pe.wait_ge(S["mask_ready"], TT * (level - 1) + t + 1)
                    heads(f"X{level}_{t}", of(BM, t), of(T, t))
                for t in range(TT):
                    wait_evac(pe, f"X{level}_{t}")
                    if level > 1:
                        wait_evac(pe, f"PU{level - 1}_{t}")
                    if level < LEVELS - 1:
                        heads(f"PT{level}_{t}", of(U, t), of(X, t))
                    heads(f"PU{level}_{t}", of(X, t), of(U, t))
                last_in = project(13 + level, range(4) if level < LEVELS - 1 else range(1))
                part, k = divmod(2 * (level + 1), KD)
                if level < LEVELS - 1:
                    ada(1 + part, (k, k + 1))

            wait_evac(pe, f"PU{LEVELS - 1}_0")
            heads("vn0", of(U, 0), of(vb, 0))
            project_part(12 + LEVELS, last_in, 1)
            wait_evac(pe, "vn0")
            heads("S", of(kd, 0), of(vn0))
            project_part(12 + LEVELS, last_in, 2)
            wait_evac(pe, "S")
            heads("kS", of(knT, 1), of(state))
            ada(2, (KD - 2,))
            pe.wait_ge(S["r_ready"], 1)
            wait_evac(pe, f"PU{LEVELS - 1}_1")
            heads("vn1", of(U, 1), of(r_sb))
            for t in range(TT):
                wait_evac(pe, f"qk{t}")
            heads("o0", of(QKT, 0), of(vn0))
            open_bank(pe, "o1")
            wait_evac(pe, "qdT")
            wait_evac(pe, "vn1")
            for h in range(HEADS):
                s = slice(P * h, P * h + P)
                pe.matmul(bank_of("o1")[:, s], qdT[:, 0, s], state[:, s], start=True, stop=False)
                mm = pe.matmul(bank_of("o1")[:, s], QKT[:, 1, s], vn1[:, s], start=False, stop=True)
            ended(mm, "o1")
            project_part(12 + LEVELS, last_in, 3)
            ada(2, (KD - 1,))
            def branch(kind, m, w, halves=range(2)):
                name, src = f"b{kind}{m}", (zT, xcT)[kind == "l"]
                if halves[0] == 0:
                    open_bank(pe, name)
                for half in halves:
                    for k in range(4):
                        mm = pe.matmul(bank_of(name)[:, 256 * half:256 * half + 256],
                                       w[:, int(kind == "l"), k, 128 * half:128 * half + 128], src[:, k, :],
                                       start=k == 0, stop=k == 3)
                if halves[-1] == 1:
                    ended(mm, name)

            pe.wait_ge(S["lru_out"], 1)
            for m in range(4):
                w = next_chunk().rearrange("p (b k m) -> p b k m", b=2, k=4)
                branch("l", m, w, range(1))
                if m == 0:
                    for t in range(TT):
                        wait_evac(pe, f"o{t}")
                        heads(f"oT{t}", of(qn, t), None, transpose=True)
                branch("l", m, w, range(1, 2))
                if m == 0:
                    for t in range(TT):
                        wait_evac(pe, f"oT{t}")
                branch("g", m, w)

            w_out_sb = [next_chunk().rearrange("p (k m) -> p k m", k=2) for _ in range(4)]

            def mix(t, half, ks):
                name = f"x{t}{half}"
                if ks[0] == 0:
                    open_bank(pe, name)
                for k in ks:
                    if t == 0 and half == 0 and k % 2 == 0:
                        pe.wait_ge(S["merged_ready"], k // 2 + 1)
                    mm = pe.matmul(bank_of(name)[:, :], mergedT[:, k, P * t:P * t + P],
                                   w_out_sb[k // 2][:, k % 2, 512 * half:512 * half + 512],
                                   start=k == 0, stop=k == KD - 1)
                    if k == KD - 1:
                        ended(mm, name)
                    elif (t, half) == (1, 1) and k % 2:
                        mm.then_inc(pre_used, 1)

            def turn_h2(t):
                for half in range(2):
                    pe.wait_ge(S["h2_ready"], 2 * t + half + 1)
                    open_bank(pe, f"h2T{t}{half}")
                    for k in range(4):
                        at = 512 * half + P * k
                        mm = pe.transpose(bank_of(f"h2T{t}{half}")[:, P * k:P * k + P], h2[:, t, at:at + P], ident)
                    ended(mm, f"h2T{t}{half}")

            def route(t):
                open_bank(pe, f"lgT{t}")
                for half in range(2):
                    wait_evac(pe, f"h2T{t}{half}")
                narrow(f"lgT{t}", P, wr_sb, hT[:, :, P * t:P * t + P])

            def turn_logits(t):
                wait_evac(pe, f"lgT{t}")
                open_bank(pe, f"lg{t}")
                ended(pe.matmul(bank_of(f"lg{t}")[:, 0:E], lg_row[:, P * t:P * t + P], fold, start=True, stop=True),
                      f"lg{t}")

            mix(0, 0, range(KD))
            mix(0, 1, range(KD))
            mix(1, 0, range(KD))
            turn_h2(0)
            mix(1, 1, range(3))
            pe.wait_ge(S["router_in"], 16 * 2)
            route(0)
            mix(1, 1, range(3, 6))
            turn_logits(0)
            mix(1, 1, range(6, KD))
            keep_warm("lg1", 16)
            turn_h2(1)
            route(1)
            turn_logits(1)

            keep_warm("count", 8)
            pe.wait_ge(S["M_ready"], 2)
            open_bank(pe, "count")
            for t in range(TT):
                mm = pe.matmul(bank_of("count")[0:E, 0:1], M[:, t, :], ones[:, 0:1], start=t == 0, stop=t == TT - 1)
            ended(mm, "count")
            open_bank(pe, "pos")
            pe.matmul(bank_of("pos")[:, 0:E], strict, M[:, 0, :], start=True, stop=True)
            pe.matmul(bank_of("pos")[:, E:2 * E], strict, M[:, 1, :], start=True, stop=False)
            ended(pe.matmul(bank_of("pos")[:, E:2 * E], ones, M[:, 0, :], start=False, stop=True), "pos")
            keep_warm("posT", 4)
            pe.wait_ge(S["pos_ready"], 1)
            for t in range(TT):
                mm = pe.transpose(bank_of("posT")[0:E, P * t:P * t + P], pos_m[:, t, :], ident)
            ended(mm, "posT")
            def gather(ks=range(KD)):
                for k in ks:
                    for t in range(TT):
                        mm = pe.matmul(bank[bHS][:, C64 * k:C64 * k + C64], h2[:, t, P * k:P * k + P], sel[:, t, :],
                                       start=t == 0, stop=t == TT - 1)
                return mm

            pe.wait_ge(S["kinds_ready"], 1)
            open_bank(pe, "rank")
            pe.matmul(bank_of("rank")[0:E, 0:2], tri[0:E, 0:E], kinds, start=True, stop=True)
            ended(pe.matmul(bank_of("rank")[0:E, 2:4], ones[0:E, 0:E], kinds, start=True, stop=True), "rank")
            pe.wait_ge(S["sel_ready"], 1)
            open_bank(pe, "gathered0")
            gather(range(2))
            pe.wait_ge(S["key_ready"], 1)
            open_bank(pe, "keys")
            ended(pe.matmul(bank_of("keys")[0:E, 0:E], ones[0:E, 0:E], key_diag, start=True, stop=True), "keys")
            gather(range(2, 4))
            wait_evac(pe, "keys")
            open_bank(pe, "end")
            ended(pe.matmul(bank_of("end")[0:E, 0:1], before, n_item, start=True, stop=True), "end")
            gather(range(4, 6))
            pe.wait_ge(S["item_ready"], 1)
            open_bank(pe, "table")
            pe.matmul(bank_of("table")[0:1, 0:ITEMS], cst[0:E, C_INDEX:C_INDEX + 1], one_hot, start=True, stop=True)
            ended(pe.matmul(bank_of("table")[0:1, ITEMS:ITEMS + 1], ones[0:E, 0:1], n_item,
                            start=True, stop=True), "table")
            ended(gather(range(6, KD)), "gathered0")
            pe.wait_ge(S["G_ready"], 1)
            open_bank(pe, "gateT")
            for t in range(TT):
                mm = pe.transpose(bank_of("gateT")[0:E, P * t:P * t + P], G[:, t, :], ident)
            ended(mm, "gateT")
            wait_evac(pe, "posT")
            open_bank(pe, "pick")
            for t in range(TT):
                mm = pe.matmul(bank_of("pick")[:, ITEMS * t:ITEMS * t + ITEMS], posT[:, P * t:P * t + P], one_hot,
                               start=True, stop=True)
            ended(mm, "pick")
            wait_evac(pe, "gateT")
            open_bank(pe, "gpick")
            for t in range(TT):
                mm = pe.matmul(bank_of("gpick")[:, ITEMS * t:ITEMS * t + ITEMS], sgT[0:E, P * t:P * t + P], one_hot,
                               start=True, stop=True)
            ended(mm, "gpick")

            for b in (*bU, bHS, bAT, bY):
                pe.wait_ge(evac[b], sum(1 for v in plan.values() if v[0] == b))

            def scatter(signal):
                for t in range(TT):
                    for half, b in enumerate((bO[0], bO[1]) if t == 0 else (bAT, bY)):
                        rows = slice(64 * half, 64 * half + 64)
                        mm = pe.matmul(bank[b][:, :], sgT[rows, P * t:P * t + P], y_sb[rows, :], start=True, stop=True)
                        if signal == "tail_scattered" or (t, half) == (TT - 1, 1):
                            mm.then_inc(S[signal], 1)

            n_items = pe.value_load(table_i[0:1, ITEMS:ITEMS + 1], min_val=2, max_val=ITEMS - 1)
            with pe.Fori(0, n_items) as i:
                pe.wait_ge(S["hsel_ready"], i + 1)
                pe.wait_ge(S["u_read"], i + 1)
                for k in range(KD):
                    pe.wait_ge(w_loaded[k], 16 * i + 16)
                    w = ring[:, slot_of(k), :]
                    for half in range(2):
                        for group in range(2):
                            at = 1024 * group + 512 * half
                            mm = pe.matmul(bank[bU[half]][64 * group:64 * group + 64, :], hsel[:, k, :],
                                           w[:, at:at + 512], start=k == 0, stop=k == KD - 1)
                    mm.then_inc(w_used[k], 1)
                    if k == SCATTER_AT:
                        pe.wait_ge(S["y_ready"], i + 1)
                        pe.wait_ge(S["sgT_ready"], i + 1)
                        pe.wait_ge(S["x_added"], i + 1)
                        scatter("scattered")
                    if k == BIAS_AT - 1:
                        pe.wait_ge(S["b1_in"], 16 * i + 16)
                        for half in range(2):
                            for group in range(2):
                                at = 1024 * group + 512 * half
                                mm = pe.matmul(bank[bU[half]][64 * group:64 * group + 64, :], ones[0:1, 0:C64],
                                               b1_row[:, at:at + 512], start=False, stop=False)
                        mm.then_inc(S["b1_used"], 1)
                pe.wait_ge(S["sg_ready"], i + 1)
                for t in range(TT):
                    mm = pe.transpose(bank[bSG][:, P * t:P * t + P], sg[:, t, :], ident)
                mm.then_inc(S["sg_turned"], 1)
                pe.wait_ge(S["sel_ready"], i + 2)
                gather().then_inc(S["gathered"], 1)
                pe.wait_ge(S["x_added"], i + 2)
                pe.wait_ge(S["act_ready"], i + 1)
                for j in range(4):
                    mm = pe.transpose(bank[bAT][:, P * j:P * j + P], act[:, P * j:P * j + P], ident)
                mm.then_inc(S["act_turned"], 1)
                pe.wait_ge(S["actT_ready"], i + 1)
                for c in range(KD, SLOTS):
                    pe.wait_ge(w_loaded[c], 16 * i + 16)
                    w = ring[:, slot_of(c), :].rearrange("p (k n) -> p k n", k=2)
                    for kk in range(2):
                        k = 2 * (c - KD) + kk
                        for group in range(2):
                            mm = pe.matmul(bank[bY][64 * group:64 * group + 64, :],
                                           actT[:, k % 4, 64 * (k // 4):64 * (k // 4) + 64],
                                           w[:, kk, 512 * group:512 * group + 512], start=k == 0, stop=k == KD - 1)
                    mm.then_inc(w_used[c], 1)
            pe.wait_ge(S["y_ready"], n_items + 1)
            pe.wait_ge(S["sgT_ready"], n_items + 1)
            pe.wait_ge(S["x_added"], n_items + 1)
            scatter("tail_scattered")

        @block.vector
        def _(v):
            step = Chain(v, "dve_chain")

            def evacuated(ins, name):
                ins.then_inc(evac[plan[name][0]], 1)

            def head_scale(dst, src, scale, op=ALU.mult):
                return v.tensor_tensor(dst.rearrange("p (h d) -> p h d", h=HEADS), src.rearrange("p (h d) -> p h d", h=HEADS),
                                       scale.rearrange("p (h a) -> p h a", a=1).to_broadcast([P, HEADS, P]), op)

            wait_full(v, "params")
            evacuated(v.tensor_copy(prm[:, :], bank_of("params")[:, 0:PARAMS]), "params")
            v.wait_ge(S["sig_c"], 1)
            step(v.tensor_tensor(sil, sil, prm[:, R_C:R_C + KD], ALU.mult))
            v.tensor_copy(c_bc, sil.rearrange("p (k a) -> p k a", a=1).to_broadcast([P, KD, 32])).then_inc(S["cb_ready"], 1)
            v.wait_ge(S["sqrt_x"], 1)
            step(v.reciprocal(rstd, rstd))
            for t in range(TT):
                v.tensor_scalar(h2[:, t, :], x_sb[:, t, :], rstd[:, t:t + 1], None, ALU.mult).then_inc(S["xn_ready"], 1)

            def ada_rows(part):
                wait_full(v, f"ada{part}")
                v.wait_ge(S["bias_late" if part else "bias_in"], 16 * (8 if part else 4))
                evacuated(v.tensor_tensor(mod[:, part, :], bank_of(f"ada{part}")[:, :], mod_bias[:, part, :], ALU.add),
                          f"ada{part}")

            ada_rows(0)
            wait_full(v, "modcol")
            turned = bank_of("modcol")[:, :].rearrange("p (j q r) -> p q j r", j=4, q=4)
            for n in range(4):
                dst = modcol[:, 4 * n:4 * n + 4].rearrange("p (j r) -> p j r", r=1)
                src = turned[:, n, :, 0:1]
                if n < 2:
                    step(v.tensor_copy(dst, src))
                else:
                    gain = prm[:, R_NORM_MIX + 4 * n - KD:R_NORM_MIX + 4 * n - KD + 4]
                    ins = v.scalar_tensor_tensor(dst, src, 1.0, gain.rearrange("p (j r) -> p j r", r=1), ALU.add, ALU.mult)
                    if n == 2:
                        step(ins)
            evacuated(ins, "modcol")
            wait_evac(v, "modcol")
            for k in range(4):
                name = f"xT{k // 2}"
                wait_full(v, name)
                ins = v.tensor_scalar(hT[:, k, :], bank_of(name)[:, 256 * (k % 2):256 * (k % 2) + 256],
                                      modcol[:, KD + k:KD + k + 1], modcol[:, k:k + 1], ALU.mult, ALU.add)
                if k % 2:
                    evacuated(ins, name)

            wait_full(v, "baT")
            v.wait_ge(S["row_in"], 16 * 2)
            ba = bank_of("baT")[:, 0:16].rearrange("p (t n) -> p t n", t=TT)
            v.tensor_tensor(spx[:, 0:8].rearrange("p (t h) -> p t h", t=TT), ba[:, :, HEADS:2 * HEADS],
                            dt_b.rearrange("p (a h) -> p a h", a=1).to_broadcast([P, TT, HEADS]), ALU.add)\
                .then_inc(S["ba_read"], 1)
            v.wait_ge(S["ba_read"], 1)
            step(v.tensor_scalar(spx[:, 8:12], prm[:, R_LAM:R_LAM + LT], -1.0, None, ALU.mult))
            v.scalar_tensor_tensor(sp_s, spx, -1.0, spx, ALU.mult, ALU.min).then_inc(S["sp_in"], 1)
            v.wait_ge(S["sp_exp"], 1)
            step(v.tensor_scalar(sp_d, sp_t, 2.0, None, ALU.add))
            step(v.reciprocal(sp_d, sp_d))
            step(v.tensor_tensor(sp_s, sp_t, sp_d, ALU.mult))
            step(v.tensor_tensor(sp_s2, sp_s, sp_s, ALU.mult))
            step(v.tensor_scalar(sp_p, sp_s2, 1.0 / 17, None, ALU.mult))
            for n in (15, 13, 11, 9, 7, 5, 3):
                step(v.scalar_tensor_tensor(sp_p, sp_p, 1.0 / n, sp_s2, ALU.add, ALU.mult))
            step(v.scalar_tensor_tensor(sp_p, sp_p, 1.0, sp_s, ALU.add, ALU.mult))
            step(v.tensor_scalar(sp_d, spx, 0.0, None, ALU.max))
            step(v.scalar_tensor_tensor(sp_d, sp_p, 2.0, sp_d, ALU.mult, ALU.add))
            step(v.tensor_scalar(lam_c, sp_d[:, 8:12], -LRU_C, None, ALU.mult))
            v.scalar_tensor_tensor(gts.rearrange("p (t h) -> p t h", t=TT), sp_d[:, 0:8].rearrange("p (t h) -> p t h", t=TT),
                                   -1.0, a_exp.rearrange("p (a h) -> p a h", a=1).to_broadcast([P, TT, HEADS]),
                                   ALU.mult, ALU.mult).then_inc(S["g_ready"], 1)
            v.wait_ge(S["g_ready"], 1)
            v.tensor_copy(g_bc, gts.rearrange("p (n a) -> p n a", a=1).to_broadcast([P, TT * HEADS, P]))\
                .then_inc(S["gbc_ready"], 1)

            def conv(n, dst, weight, bias, signal):
                name = f"in{n}"
                wait_full(v, name)
                for half in range(2):
                    src = bank_of(name)[:, 256 * half:256 * half + 256]
                    o, w = dst[:, half, :], weight(half)
                    if bias is None:
                        step(v.tensor_scalar(o, src, w[CONV - 1], None, ALU.mult))
                    else:
                        step(v.tensor_scalar(o, src, w[CONV - 1], bias(half), ALU.mult, ALU.add))
                    for tap in range(CONV - 1):
                        back = CONV - 1 - tap
                        ins = v.scalar_tensor_tensor(o[:, back:], src[:, :SEQ - back], w[tap], o[:, back:],
                                                     ALU.mult, ALU.add)
                        if half and tap == CONV - 2:
                            evacuated(ins, name)
                            wait_evac(v, name)
                        else:
                            step(ins)

            def qkv_conv(n):
                def weight(half):
                    return [prm[:, R_GCONV + 12 * tap + 2 * n + half:][:, 0:1] for tap in range(CONV)]
                conv(n, convT[:, 2 * n:2 * n + 2, :], weight, None, None)

            def qkv_silu(n):
                v.wait_ge(S["conv_sig"], n + 1)
                v.tensor_tensor(convT[:, 2 * n:2 * n + 2, :], convT[:, 2 * n:2 * n + 2, :], conv_sg(n), ALU.mult)\
                    .then_inc(S["qkv_ready"], 1)

            qkv_conv(0)
            qkv_conv(1)
            qkv_silu(0)
            wait_full(v, "gc")
            evacuated(v.tensor_copy(gc, bank_of("gc")[:, 0:TT * HEADS]), "gc")
            wait_evac(v, "gc")
            for t in range(TT):
                wait_full(v, f"gcrow{t}")
                evacuated(head_scale(Dm[:, t, :], bank_of(f"gcrow{t}")[:, :], gc[:, HEADS * t:HEADS * t + HEADS],
                                     ALU.subtract), f"gcrow{t}")
                wait_evac(v, f"gcrow{t}")
                v.tensor_scalar(Dm[:, t, :], Dm[:, t, :], 0.0, None, ALU.min).then_inc(S["diff_ready"], 1)
            for n in range(2, 6):
                qkv_conv(n)
                qkv_silu(n - 1)
                if n == 2:
                    v.wait_ge(S["decay_ready"], 1)
                    step(v.tensor_copy(ekd.rearrange("p (h a) -> p h a", a=1),
                                       Dm[:, 0, :].rearrange("p (h c) -> p h c", h=HEADS)[:, :, P - 1:P]))
                    for t in range(TT):
                        step(v.tensor_tensor(Dm[:, t, :].rearrange("p (h c) -> p h c", h=HEADS),
                                             Dm[:, t, :].rearrange("p (h c) -> p h c", h=HEADS),
                                             tri.rearrange("p (a c) -> p a c", a=1).to_broadcast([P, HEADS, P]), ALU.mult))
                    step(v.tensor_tensor(be, beta, egc, ALU.mult))
            qkv_silu(5)
            for n in (6, 7):
                j = 2 * (n - 6)
                conv(n, xcT[:, j:j + 2, :],
                     lambda half: [prm[:, R_LCONV + LT * tap + j + half:][:, 0:1] for tap in range(CONV)],
                     lambda half: prm[:, R_LCONV_B + j + half:][:, 0:1], None)

            for n in range(4):
                wait_evac(v, ("k0", "k1", "q0", "q1")[n])
                v.tensor_reduce(ss[:, 4 * n:4 * n + 4], sq[:, n % 2, :].rearrange("p (h d) -> p h d", h=HEADS),
                                AX.X, ALU.add).then_inc(S["ss_ready"], 1)
            for t in range(TT):
                wait_full(v, f"v{t}")
                evacuated(head_scale(vb[:, t, :], bank_of(f"v{t}")[:, :], beta[:, HEADS * t:HEADS * t + HEADS]), f"v{t}")
            v.wait_ge(S["rs_sqrt"], 1)
            step(v.reciprocal(rs, rs))
            step(v.tensor_scalar(rs[:, 8:16], rs[:, 8:16], float(HD) ** -0.5, None, ALU.mult))
            wait_evac(v, "q1")

            def scaled(dst, src, scale):
                head_scale(dst, src, scale).then_inc(S["kn_ready"], 1)

            for t in range(TT):
                scaled(kn[:, t, :], k_tok[:, t, :], rs[:, 4 * t:4 * t + 4])
            v.wait_ge(S["kn_ready"], 2)
            for t in range(TT):
                scaled(kb[:, t, :], kn[:, t, :], beta[:, 4 * t:4 * t + 4])
            for t in range(TT):
                scaled(qn[:, t, :], q_tok[:, t, :], rs[:, 8 + 4 * t:12 + 4 * t])
            v.wait_ge(S["kn_ready"], 6)
            scaled(qd[:, 0, :], qn[:, 1, :], egc[:, 4:8])
            scaled(kd[:, 0, :], kn[:, 0, :], ekd)

            def silu_z(n):
                v.wait_ge(S["z_sig"], n - 9)
                evacuated(v.tensor_tensor(zT[:, 2 * (n - 10):2 * (n - 10) + 2, :], zT[:, 2 * (n - 10):2 * (n - 10) + 2, :],
                                          bank_of(f"in{n}")[:, :].rearrange("p (a n) -> p a n", a=2), ALU.mult), f"in{n}")

            silu_z(10)
            silu_z(11)
            for name, dst in (("knT1", knT[:, 1, :]), ("kbT1", kbT[:, 1, :]), ("qnT1", qnT[:, 1, :])):
                wait_full(v, name)
                evacuated(v.tensor_copy(dst, bank_of(name)[:, :]), name)
            v.wait_ge(S["masks_in"], 16)
            for t in range(TT):
                wait_full(v, f"kk{t}")
                ins = v.tensor_tensor(Bm[:, t, :], bank_of(f"kk{t}")[:, :], Dm[:, t, :], ALU.mult)
                evacuated(ins, f"kk{t}")
                wait_evac(v, f"kk{t}")
                step(v.tensor_tensor(U[:, t, :].rearrange("p (h c) -> p h c", h=HEADS),
                                     Bm[:, t, :].rearrange("p (h c) -> p h c", h=HEADS), level_mask(0), ALU.mult))
                v.tensor_tensor(U[:, t, :].rearrange("p (h c) -> p h c", h=HEADS),
                                ident.rearrange("p (a c) -> p a c", a=1).to_broadcast([P, HEADS, P]),
                                U[:, t, :].rearrange("p (h c) -> p h c", h=HEADS), ALU.subtract)\
                    .then_inc(S["U0_ready"], 1)
            for t in range(TT):
                wait_full(v, f"qk{t}")
                evacuated(v.tensor_tensor(QKT[:, t, :], bank_of(f"qk{t}")[:, :], Dm[:, t, :], ALU.mult), f"qk{t}")
            v.wait_ge(S["U0_ready"], TT)
            for level in range(1, LEVELS):
                for t in range(TT):
                    if level > 1:
                        wait_evac(v, f"PU{level - 1}_{t}")
                    if level < LEVELS - 1:
                        name = f"PT{level}_{t}"
                        wait_full(v, name)
                        wait_evac(v, f"T{t}" if level == 1 else f"PT{level - 1}_{t}")
                        evacuated(v.tensor_tensor(T[:, t, :], T[:, t, :], bank_of(name)[:, :], ALU.subtract), name)
                    name = f"PU{level}_{t}"
                    wait_full(v, name)
                    evacuated(v.tensor_tensor(U[:, t, :], U[:, t, :], bank_of(name)[:, :], ALU.subtract), name)
                if level == 2:
                    ada_rows(1)
                if level == 3:
                    v.wait_ge(S["lru_b"], 1)
                    for j in range(LT):
                        step(v.tensor_tensor_scan(xcT[:, j, :], lru_a[:, j, :], lru_i[:, j, :], 0.0, ALU.mult, ALU.add))
                    v.tensor_tensor(xcT[:, :, :], xcT[:, :, :], ybT[:, :, :], ALU.mult).then_inc(S["lru_out"], 1)
                    v.wait_ge(S["lru_out"], 1)

            wait_full(v, "kS")
            evacuated(head_scale(ks_sb, bank_of("kS")[:, :], be[:, 4:8]), "kS")
            wait_evac(v, "kS")
            wait_evac(v, "v1")
            v.tensor_tensor(r_sb, vb[:, 1, :], ks_sb, ALU.subtract).then_inc(S["r_ready"], 1)
            for t in range(TT):
                v.wait_ge(S["o_sq"], t + 1)
                v.tensor_reduce(oss[:, 4 * t:4 * t + 4], o_sqr[:, t, :].rearrange("p (h d) -> p h d", h=HEADS),
                                AX.X, ALU.add).then_inc(S["oss_ready"], 1)
            v.wait_ge(S["o_sqrt"], 1)
            step(v.reciprocal(oss, oss))
            for t in range(TT):
                evacuated(head_scale(qn[:, t, :], bank_of(f"o{t}")[:, :], oss[:, 4 * t:4 * t + 4]), f"o{t}")
            for t in range(TT):
                wait_full(v, f"oT{t}")
                zt = zT[:, :, P * t:P * t + P]
                evacuated(v.scalar_tensor_tensor(zt, bank_of(f"oT{t}")[:, :].rearrange("p (h c) -> p h c", h=HEADS),
                                                 prm[:, R_NORM_W:R_NORM_W + 1], zt, ALU.mult, ALU.mult), f"oT{t}")
            ada_rows(2)
            for m in range(4):
                def gate(b):
                    return gatesT[:, KD * b + 2 * m:KD * b + 2 * m + 2, :].rearrange("p a n -> p (a n)")
                dst = mergedT[:, 2 * m:2 * m + 2, :].rearrange("p a n -> p (a n)")
                wait_full(v, f"bl{m}")
                wait_evac(v, f"in{12 + m}")
                wait_evac(v, f"in{16 + m}")
                evacuated(v.tensor_tensor(mtmp[m % 2], bank_of(f"bl{m}")[:, :], gate(1), ALU.mult), f"bl{m}")
                wait_full(v, f"bg{m}")
                evacuated(v.tensor_tensor(dst, bank_of(f"bg{m}")[:, :], gate(0), ALU.mult), f"bg{m}")
                wait_evac(v, f"bg{m}")
                wait_evac(v, f"bl{m}")
                v.tensor_tensor(dst, dst, mtmp[m % 2], ALU.add).then_inc(S["merged_ready"], 1)
            v.wait_ge(S["merged_ready"], 4)
            v.wait_ge(S["norm_in"], 16)
            v.wait_ge(S["rows_in"], 16 * ROW_LOADS)
            step(v.scalar_tensor_tensor(norm_ffn_b, scale_f_b, 1.0, norm_ffn_b, ALU.add, ALU.mult))
            step(v.memset(sgT, 0.0))
            v.memset(y_sb, 0.0).then_inc(S["y_zero"], 1)
            def mixed(t, half):
                name = f"x{t}{half}"
                s = slice(512 * half, 512 * half + 512)
                wait_full(v, name)
                evacuated(v.tensor_tensor(h2[:, t, s], bank_of(name)[:, :], gate_m_b[:, s], ALU.mult), name)
                wait_evac(v, name)
                v.tensor_tensor(x_sb[:, t, s], x_sb[:, t, s], h2[:, t, s], ALU.add).then_inc(S["x1_ready"], 1)
                v.wait_ge(S["x1_ready"], 2 * t + half + 1)
                step(v.tensor_tensor(h2[:, t, s], x_sb[:, t, s], norm_ffn_b[:, s], ALU.mult))

            def ffn_norm(t):
                v.wait_ge(S["sqrt_x1"], t + 1)
                step(v.reciprocal(rstd[:, t:t + 1], rstd[:, t:t + 1]))
                for half in range(2):
                    s = slice(512 * half, 512 * half + 512)
                    v.scalar_tensor_tensor(h2[:, t, s], h2[:, t, s], rstd[:, t:t + 1], shift_f_b[:, s],
                                           ALU.mult, ALU.add).then_inc(S["h2_ready"], 1)

            v.wait_ge(S["router_in"], 16 * 2)

            def top4(t):
                wait_full(v, f"lg{t}")
                evacuated(v.tensor_tensor(logit[:, t, :], bank_of(f"lg{t}")[:, 0:E], br_b, ALU.add), f"lg{t}")
                wait_evac(v, f"lg{t}")
                best = m8[:, 8 * t:8 * t + 8]
                step(v.max(best, logit[:, t, :]))
                step(v.max_index(idx_u[:, 8 * t:8 * t + 8], best, logit[:, t, :]))
                step(v.tensor_copy(idx_f[:, 8 * t:8 * t + 8], idx_u[:, 8 * t:8 * t + 8]))
                step(v.tensor_tensor(eq[:, TOPK * t:TOPK * t + TOPK, :],
                                     cst[:, C_EXPERT:C_EXPERT + E].rearrange("p (a e) -> p a e", a=1).to_broadcast([P, TOPK, E]),
                                     idx_f[:, 8 * t:8 * t + TOPK].rearrange("p (k a) -> p k a", a=1).to_broadcast([P, TOPK, E]),
                                     ALU.is_equal))
                v.tensor_reduce(M[:, t, :], eq[:, TOPK * t:TOPK * t + TOPK, :].rearrange("p k e -> p e k"),
                                AX.X, ALU.add).then_inc(S["M_ready"], 1)
                v.tensor_scalar(negm[:, t:t + 1], best[:, 0:1], -1.0, None, ALU.mult).then_inc(S["top_ready"], 1)

            mixed(0, 0)
            mixed(0, 1)
            ffn_norm(0)
            mixed(1, 0)
            top4(0)
            mixed(1, 1)
            ffn_norm(1)
            wait_full(v, "h2T10")
            evacuated(v.tensor_copy(hT[:, 0:4, P:2 * P], bank_of("h2T10")[:, :].rearrange("p (a n) -> p a n", a=4)), "h2T10")
            top4(1)
            v.wait_ge(S["M_ready"], 2)
            wait_full(v, "count")
            evacuated(v.tensor_copy(n_tok, bank_of("count")[0:E, 0:1]), "count")
            wait_evac(v, "count")
            step(v.tensor_scalar(n_item, n_tok, C64 + 0.5, 1.0, ALU.is_gt, ALU.add))
            step(v.scalar_tensor_tensor(n_item, n_tok, 2 * C64 + 0.5, n_item, ALU.is_gt, ALU.add))
            step(v.scalar_tensor_tensor(n_item, n_tok, 3 * C64 + 0.5, n_item, ALU.is_gt, ALU.add))
            step(v.scalar_tensor_tensor(kinds[:, 0:1], n_item, 1.5, cst[0:E, C_REST:C_REST + 1], ALU.is_lt, ALU.mult))
            v.tensor_tensor(kinds[:, 1:2], cst[0:E, C_REST:C_REST + 1], kinds[:, 0:1], ALU.subtract)\
                .then_inc(S["kinds_ready"], 1)
            wait_full(v, "pos")
            Mf, posf = M.rearrange("p t e -> p (t e)"), pos_m.rearrange("p t e -> p (t e)")
            evacuated(v.scalar_tensor_tensor(posf, Mf, -4096.0, bank_of("pos")[:, 0:TT * E], ALU.mult, ALU.add), "pos")
            wait_evac(v, "pos")
            v.tensor_scalar(posf, posf, 4096.0, None, ALU.add).then_inc(S["pos_ready"], 1)
            v.wait_ge(S["pos_ready"], 1)
            for t in range(TT):
                ins = v.tensor_scalar(sel[:, t, :], cst[:, C_SLOT:C_SLOT + C64], pos_m[:, t, FIRST:FIRST + 1], None,
                                      ALU.is_equal)
            ins.then_inc(S["sel_ready"], 1)
            wait_full(v, "rank")
            step(v.tensor_scalar(total, bank_of("rank")[0:E, 2:4], 1.0, None, ALU.add))
            step(v.reciprocal(total, total))
            evacuated(v.tensor_tensor(rank, bank_of("rank")[0:E, 0:2], total, ALU.mult), "rank")
            wait_evac(v, "rank")
            step(v.tensor_tensor(rank, rank, kinds, ALU.mult))
            step(v.scalar_tensor_tensor(key, rank[:, 0:1], rank[:, 1:2], cst[0:E, C_KEY:C_KEY + 1], ALU.add, ALU.add))
            v.tensor_scalar(key_diag, ident[0:E, 0:E], key, None, ALU.mult).then_inc(S["key_ready"], 1)
            v.wait_ge(S["key_ready"], 1)
            step(v.tensor_scalar(key, key, -TIE / 4, None, ALU.add))
            wait_full(v, "keys")
            evacuated(v.tensor_scalar(before, bank_of("keys")[0:E, 0:E], key, None, ALU.is_ge), "keys")
            wait_full(v, "end")
            evacuated(v.tensor_copy(end, bank_of("end")[0:E, 0:1]), "end")
            wait_evac(v, "end")
            step(v.tensor_tensor(start, end, n_item, ALU.subtract))
            v.tensor_scalar(start64, start, float(C64), None, ALU.mult).then_inc(S["start_ready"], 1)
            item = cst[:, C_ITEM:C_ITEM + ITEMS]
            step(v.tensor_scalar(cmp_end, item[0:E, :], end, None, ALU.is_ge))
            v.scalar_tensor_tensor(one_hot, item[0:E, :], start, cmp_end, ALU.is_ge, ALU.subtract)\
                .then_inc(S["item_ready"], 1)
            v.wait_ge(S["gates_exp"], 2)
            step(v.reciprocal(gsum, gsum))
            step(v.tensor_tensor(gk.rearrange("p (t k) -> p t k", t=TT), gk.rearrange("p (t k) -> p t k", t=TT),
                                 gsum.rearrange("p (t a) -> p t a", a=1).to_broadcast([P, TT, TOPK]), ALU.mult))
            step(v.tensor_tensor(eqg, eq, gk.rearrange("p (n a) -> p n a", a=1).to_broadcast([P, TT * TOPK, E]), ALU.mult))
            for t in range(TT):
                ins = v.tensor_reduce(G[:, t, :], eqg[:, TOPK * t:TOPK * t + TOPK, :].rearrange("p k e -> p e k"),
                                      AX.X, ALU.add)
            ins.then_inc(S["G_ready"], 1)
            wait_full(v, "table")
            evacuated(v.tensor_copy(table_i[0:1, :], bank_of("table")[0:1, 0:ITEMS + 1]), "table")
            wait_evac(v, "table")
            v.sem_inc(S["u_read"], 1)
            wait_full(v, "pick")
            for t in range(TT):
                ins = v.scalar_tensor_tensor(pos_i[:, t, :], item, -float(C64), bank_of("pick")[:, ITEMS * t:ITEMS * t + ITEMS],
                                             ALU.mult, ALU.add)
                if t == TT - 1:
                    evacuated(ins, "pick")
                    wait_evac(v, "pick")
                else:
                    step(ins)
            wait_full(v, "gpick")
            evacuated(v.tensor_copy(gate_i.rearrange("p t n -> p (t n)"), bank_of("gpick")[:, 0:TT * ITEMS]), "gpick")
            wait_evac(v, "gpick")
            v.wait_ge(S["b2_in"], 16 * 2)
            v.tensor_tensor(y_sb, y_sb, gate_f_h, ALU.mult).then_inc(S["y_ready"], 1)
            v.sem_inc(S["x_added"], 1)

            def add_scattered(n):
                v.wait_ge(S["scattered"], n)
                v.wait_ge(S["x_added"], n)
                for t in range(TT):
                    for half, b in enumerate((bO[0], bO[1]) if t == 0 else (bAT, bY)):
                        xs = x_sb[:, t, 512 * half:512 * half + 512]
                        ins = v.tensor_tensor(xs, xs, bank[b][:, :], ALU.add)
                ins.then_inc(S["x_added"], 1)

            n_items = v.value_load(table_i[0:1, ITEMS:ITEMS + 1], min_val=2, max_val=ITEMS - 1)
            with v.Fori(0, n_items) as i:
                v.wait_ge(S["gathered"], i + 1)
                for t in range(TT):
                    ins = v.tensor_scalar(sel[:, t, :], cst[:, C_SLOT:C_SLOT + C64], pos_i[:, t, ds(i + 1, 1)], None,
                                          ALU.is_equal)
                ins.then_inc(S["sel_ready"], 1)
                add_scattered(i + 1)
                for t in range(TT):
                    ins = v.tensor_scalar(sg[:, t, :], cst[:, C_SLOT:C_SLOT + 2 * C64], pos_i[:, t, ds(i, 1)],
                                          gate_i[:, t, ds(i, 1)], ALU.is_equal, ALU.mult)
                ins.then_inc(S["sg_ready"], 1)
                v.wait_ge(w_used[KD - 1], i + 1)
                u = [bank[b][:, :].rearrange("p (f two) -> p f two", two=2) for b in bU]
                for half in range(2):
                    ins = v.tensor_scalar(glu[:, 256 * half:256 * half + 256].rearrange("p (f a) -> p f a", a=1),
                                          u[half][:, :, 0:1], SW_LIMIT, None, ALU.min)
                ins.then_inc(S["glu_ready"], 1)
                for half in range(2):
                    ins = v.tensor_scalar(lin[:, 256 * half:256 * half + 256].rearrange("p (f a) -> p f a", a=1),
                                          u[half][:, :, 1:2], SW_LIMIT, -SW_LIMIT, ALU.min, ALU.max)
                ins.then_inc(S["u_read"], 1)
                v.wait_ge(S["u_read"], i + 2)
                v.scalar_tensor_tensor(lin, lin, 1.0, glu, ALU.add, ALU.mult).then_inc(S["gl_ready"], 1)
                v.wait_ge(S["gl_ready"], i + 1)
                v.wait_ge(S["sig_ready"], i + 1)
                v.tensor_tensor(act, lin, sig, ALU.mult).then_inc(S["act_ready"], 1)
                v.wait_ge(w_used[SLOTS - 1], i + 1)
                v.tensor_tensor(y_sb, bank[bY][:, :], gate_f_h, ALU.mult).then_inc(S["y_ready"], 1)
            v.wait_ge(S["x_added"], n_items + 1)
            for t in range(TT):
                for half, b in enumerate((bO[0], bO[1]) if t == 0 else (bAT, bY)):
                    v.wait_ge(S["tail_scattered"], 2 * t + half + 1)
                    xs = x_sb[:, t, 512 * half:512 * half + 512]
                    v.tensor_tensor(xs, xs, bank[b][:, :], ALU.add).then_inc(S["x2_ready"], 1)
            v.wait_ge(S["x2_ready"], 2 * TT)
            v.wait_ge(S["late_in"], 16)
            for t in range(TT):
                v.wait_ge(S["sqrt_x2"], t + 1)
                step(v.reciprocal(rstd[:, t:t + 1], rstd[:, t:t + 1]))
                for half in range(2):
                    s = slice(512 * half, 512 * half + 512)
                    v.scalar_tensor_tensor(h2[:, t, s], x_sb[:, t, s], rstd[:, t:t + 1], norm_fin_b[:, s],
                                           ALU.mult, ALU.mult).then_inc(S["out_ready"], 1)

        @block.scalar
        def _(a):
            step = Chain(a, "act_chain")

            def evacuated(ins, name):
                ins.then_inc(evac[plan[name][0]], 1)

            load_rows(a, R_C, cond[0])
            load_rows(a, R_NORM_MIX, norm_mix[0])
            a.dma_start(stage[R_NORM_W:R_NORM_W + 1, :], gdn_norm_w).then_inc(S["stage_in"], 16)
            for at, src in ((R_GCONV, gdn_conv_w[0]), (R_LCONV, lru_conv_w[0])):
                n = CONV * src.shape[1] // P
                a.dma_start(stage[at:at + n, :], src.rearrange("w (n p) -> (w n) p", p=P)).then_inc(S["stage_in"], 16)

            def load_bias_rows(b, signal):
                for q in range(4):
                    at = 2048 * b + 512 * q
                    a.dma_start(mod_bias[32 * q:32 * q + 32, b, :], b_ada[0:1, at:at + 512].to_broadcast([32, 512]))\
                        .then_inc(S[signal], 16)

            load_bias_rows(0, "bias_in")
            a.wait_ge(S["ba_zero"], 1)
            a.dma_start(w_ba[:, :, 0:2 * HEADS], w_in[0, :, IN_BA:IN_X].rearrange("(k p) m -> p k m", p=P)).then_inc(S["ba_in"], 16)
            a.dma_start(a_exp, gdn_a_log.to_broadcast([P, HEADS])).then_inc(S["row_in"], 16)
            a.dma_start(dt_b, gdn_dt_bias.to_broadcast([P, HEADS])).then_inc(S["row_in"], 16)
            wait_evac(a, "params")
            a.activation(sil, prm[:, R_C:R_C + KD], ACT.Sigmoid).then_inc(S["sig_c"], 1)
            a.wait_ge(S["x_in"], 16 * TT)
            for t in range(TT):
                step(a.activation(h2[:, t, :], x_sb[:, t, :], ACT.Square, accum_out=ssx[:, t:t + 1]))
            a.wait_ge(S["const_in"], 16)
            a.activation(rstd, ssx, ACT.Sqrt, scale=1.0 / D, bias=eps).then_inc(S["sqrt_x"], 1)
            wait_evac(a, "modcol")
            for k in range(4, KD):
                name = f"xT{k // 2}"
                wait_full(a, name)
                ins = a.activation(hT[:, k, :], bank_of(name)[:, 256 * (k % 2):256 * (k % 2) + 256], ACT.Identity,
                                   scale=modcol[:, KD + k:KD + k + 1], bias=modcol[:, k:k + 1])
                if k % 2:
                    evacuated(ins, name)
            a.dma_start(br_b, b_router.to_broadcast([P, E])).then_inc(S["router_in"], 16)
            a.dma_start(wr_sb[:, :, :], w_router[0].rearrange("(k p) e -> p k e", p=P)).then_inc(S["router_in"], 16)
            load_bias_rows(1, "bias_late")
            load_bias_rows(2, "bias_late")
            a.dma_start(cst[:, C_LEVEL:], consts[:, C_LEVEL:]).then_inc(S["masks_in"], 16)
            wait_full(a, "ba")
            evacuated(a.activation(ba_row, bank_of("ba")[:, 0:SEQ], ACT.Copy), "ba")
            a.wait_ge(S["ba_read"], 1)
            evacuated(a.activation(beta.rearrange("p (t h) -> p t h", t=TT),
                                   bank_of("baT")[:, 0:16].rearrange("p (t n) -> p t n", t=TT)[:, :, 0:HEADS],
                                   ACT.Sigmoid), "baT")
            a.wait_ge(S["row_in"], 16 * 2)
            step(a.activation(a_exp, a_exp, ACT.Exp))
            a.wait_ge(S["sp_in"], 1)
            a.activation(sp_t, sp_s, ACT.Exp).then_inc(S["sp_exp"], 1)

            def conv_sigmoid(n):
                wait_evac(a, f"in{n}")
                a.activation(conv_sg(n), convT[:, 2 * n:2 * n + 2, :], ACT.Sigmoid).then_inc(S["conv_sig"], 1)

            conv_sigmoid(0)
            conv_sigmoid(1)
            a.wait_ge(S["diff_ready"], TT)
            step(a.activation(egc, gc, ACT.Exp))
            a.activation(Dm, Dm, ACT.Exp).then_inc(S["decay_ready"], 1)
            for n in range(2, 6):
                conv_sigmoid(n)
            for n in (8, 9):
                wait_full(a, f"in{n}")
                evacuated(a.activation(ybT[:, 2 * (n - 8):2 * (n - 8) + 2, :],
                                       bank_of(f"in{n}")[:, :].rearrange("p (a n) -> p a n", a=2), ACT.Copy), f"in{n}")
            for n, name in enumerate(("k0", "k1", "q0", "q1")):
                wait_full(a, name)
                if n >= 2:
                    a.wait_ge(S["ss_ready"], n - 1)
                step(a.activation((k_tok, q_tok)[n // 2][:, n % 2, :], bank_of(name)[:, :], ACT.Copy))
                evacuated(a.activation(sq[:, n % 2, :], bank_of(name)[:, :], ACT.Square), name)
            a.wait_ge(S["ss_ready"], 4)
            a.activation(rs, ss, ACT.Sqrt, bias=eps).then_inc(S["rs_sqrt"], 1)
            def z_sigmoid(n):
                wait_full(a, f"in{n}")
                a.activation(zT[:, 2 * (n - 10):2 * (n - 10) + 2, :],
                             bank_of(f"in{n}")[:, :].rearrange("p (a n) -> p a n", a=2), ACT.Sigmoid).then_inc(S["z_sig"], 1)

            def lru_sigmoid(kind, n, dst, row):
                name = f"lru_{kind}{n}"
                wait_full(a, name)
                for half in range(2):
                    j = 2 * n + half
                    ins = a.activation(dst[:, j, :], bank_of(name)[:, 256 * half:256 * half + 256], ACT.Sigmoid,
                                       bias=prm[:, row + j:row + j + 1])
                evacuated(ins, name)

            z_sigmoid(10)
            z_sigmoid(11)
            for n in range(2):
                lru_sigmoid("r", n, lru_r, R_BA)
            for n in range(2):
                lru_sigmoid("i", n, lru_i, R_BX)
            a.wait_ge(S["yb_arg"], 1)
            a.activation(lru_a, lru_a, ACT.Sigmoid, scale=GELU_B).then_inc(S["yb_sig"], 1)
            for name, dst in (("knT0", knT[:, 0, :]), ("kbT0", kbT[:, 0, :]), ("qnT0", qnT[:, 0, :]), ("qdT", qdT[:, 0, :])):
                wait_full(a, name)
                evacuated(a.activation(dst, bank_of(name)[:, :], ACT.Copy), name)

            def gate_sigmoid(n):
                wait_full(a, f"in{n}")
                evacuated(a.activation(gatesT[:, 2 * (n - 12):2 * (n - 12) + 2, :],
                                       bank_of(f"in{n}")[:, :].rearrange("p (a n) -> p a n", a=2), ACT.Sigmoid), f"in{n}")

            gate_sigmoid(12)
            a.wait_ge(S["yb_done"], 1)
            a.wait_ge(S["g_ready"], 1)
            for n in range(2):
                wait_evac(a, f"lru_r{n}")
            for j in range(LT):
                step(a.activation(lru_a[:, j, :], lru_r[:, j, :], ACT.Exp, scale=lam_c[:, j:j + 1]))
            for j in range(LT):
                ins = a.activation(lru_r[:, j, :], lru_r[:, j, :], ACT.Tanh, scale=lam_c[:, j:j + 1])
            ins.then_inc(S["lru_exp"], 1)
            gate_sigmoid(13)
            for t in range(TT):
                wait_full(a, f"T{t}")
                evacuated(a.activation(T[:, t, :], bank_of(f"T{t}")[:, :], ACT.Copy), f"T{t}")
            for level in range(1, LEVELS):
                for t in range(TT):
                    wait_full(a, f"X{level}_{t}")
                    if level > 1:
                        wait_full(a, f"PU{level - 1}_{t}")
                    evacuated(a.activation(X[:, t, :], bank_of(f"X{level}_{t}")[:, :], ACT.Copy), f"X{level}_{t}")
                if level == 2:
                    a.wait_ge(S["lru_m"], 1)
                    a.activation(xcT[:, :, :], xcT[:, :, :], ACT.Sqrt).then_inc(S["lru_sqrt"], 1)
                if level < LEVELS - 1:
                    gate_sigmoid(13 + level)
            wait_full(a, f"X{LEVELS - 1}_1")
            a.dma_start(norm_ffn_b, norm_ffn.to_broadcast([P, D])).then_inc(S["norm_in"], 16)
            for name, dst in (("vn0", vn0), ("S", state), ("vn1", vn1)):
                wait_full(a, name)
                evacuated(a.activation(dst, bank_of(name)[:, :], ACT.Copy), name)
            for t in range(TT):
                wait_full(a, f"o{t}")
                a.activation(o_sqr[:, t, :], bank_of(f"o{t}")[:, :], ACT.Square).then_inc(S["o_sq"], 1)
            a.wait_ge(S["oss_ready"], 2)
            a.activation(oss, oss, ACT.Sqrt, scale=1.0 / HD, bias=eps).then_inc(S["o_sqrt"], 1)
            gate_sigmoid(12 + LEVELS)
            for part in (1, 2):
                wait_evac(a, f"ada{part}")
            for j in range(4):
                dst_rows = slice(32 * j, 32 * j + 32)
                for part, q, dst in ((1, 0, gate_m_b), (1, 1, gate_m_b), (1, 2, shift_f_b), (1, 3, shift_f_b),
                                     (2, 0, scale_f_b), (2, 1, scale_f_b)):
                    at = 512 * (q % 2)
                    a.dma_start(dst[dst_rows, at:at + 512], mod[32 * q:32 * q + 32, part, :]).then_inc(S["rows_in"], 16)
                q = 2 + j // 2
                a.dma_start(gate_f_h[dst_rows, :], mod[32 * q:32 * q + 32, 2, :]).then_inc(S["rows_in"], 16)
            a.dma_start(norm_fin_b, norm_final.rearrange("(a n) -> a n", a=1).to_broadcast([P, D])).then_inc(S["late_in"], 16)
            a.wait_ge(S["y_zero"], 1)
            for half in range(2):
                a.dma_start(y_sb[64 * half:64 * half + E, :], b2[0, :, 512 * half:512 * half + 512])\
                    .then_inc(S["b2_in"], 16)

            def half_sums(src, scratch, t, ready, signal):
                for half in range(2):
                    a.wait_ge(S[ready], 2 * t + half + 1)
                    s = slice(512 * half, 512 * half + 512)
                    step(a.activation(scratch(t, s), src[:, t, s], ACT.Square,
                                      accum_out=ssh[:, 2 * t + half:2 * t + half + 1]))
                    if half == 0:
                        step(a.activation(ssb[:, t:t + 1], ssh[:, 2 * t:2 * t + 1], ACT.Identity, scale=1.0 / D, bias=eps))
                a.activation(rstd[:, t:t + 1], ssh[:, 2 * t + 1:2 * t + 2], ACT.Sqrt, scale=1.0 / D,
                             bias=ssb[:, t:t + 1]).then_inc(S[signal], 1)

            def take_h2T(t, half):
                name = f"h2T{t}{half}"
                wait_full(a, name)
                evacuated(a.activation(hT[:, 4 * half:4 * half + 4, P * t:P * t + P],
                                       bank_of(name)[:, :].rearrange("p (a n) -> p a n", a=4), ACT.Copy), name)

            def take_logits(t):
                wait_full(a, f"lgT{t}")
                evacuated(a.activation(lg_row[:, P * t:P * t + P], bank_of(f"lgT{t}")[:, 0:P], ACT.Copy), f"lgT{t}")

            half_sums(x_sb, lambda t, s: squares, 0, "x1_ready", "sqrt_x1")
            take_h2T(0, 0)
            take_h2T(0, 1)
            take_logits(0)
            half_sums(x_sb, lambda t, s: squares, 1, "x1_ready", "sqrt_x1")
            take_h2T(1, 1)
            take_logits(1)
            step(a.activation(warm, eps, ACT.Exp))
            a.wait_ge(S["top_ready"], TT)
            for t in range(TT):
                a.activation(gk[:, TOPK * t:TOPK * t + TOPK], m8[:, 8 * t:8 * t + TOPK], ACT.Exp, bias=negm[:, t:t + 1],
                             accum_out=gsum[:, t:t + 1]).then_inc(S["gates_exp"], 1)
            wait_full(a, "posT")
            a.wait_ge(S["start_ready"], 1)
            evacuated(a.activation(posT, bank_of("posT")[0:E, 0:SEQ], ACT.Identity, bias=start64), "posT")
            wait_full(a, "gathered0")
            evacuated(a.activation(hsel, bank[bHS][:, :].rearrange("p (k s) -> p k s", k=KD), ACT.Copy), "gathered0")
            wait_evac(a, "gathered0")
            a.sem_inc(S["gathered"], 1)
            a.sem_inc(S["hsel_ready"], 1)
            wait_full(a, "gateT")
            evacuated(a.activation(sgT[0:E, :], bank_of("gateT")[0:E, 0:SEQ], ACT.Copy), "gateT")
            a.activation(sgT[64:64 + E, :], bank_of("gateT")[0:E, 0:SEQ], ACT.Copy).then_inc(S["sgT_ready"], 1)

            wait_evac(a, "table")
            n_items = a.value_load(table_i[0:1, ITEMS:ITEMS + 1], min_val=2, max_val=ITEMS - 1)
            with a.Fori(0, n_items) as i:
                a.wait_ge(S["glu_ready"], i + 1)
                a.activation(sig, glu, ACT.Sigmoid, scale=SW_ALPHA).then_inc(S["sig_ready"], 1)
                a.wait_ge(S["sg_turned"], i + 1)
                a.activation(sgT, bank[bSG][:, 0:SEQ], ACT.Copy).then_inc(S["sgT_ready"], 1)
                a.wait_ge(S["gathered"], i + 2)
                a.activation(hsel, bank[bHS][:, :].rearrange("p (k s) -> p k s", k=KD), ACT.Copy).then_inc(S["hsel_ready"], 1)
                a.wait_ge(S["act_turned"], i + 1)
                a.activation(actT, bank[bAT][:, :].rearrange("p (j s) -> p j s", j=4), ACT.Copy).then_inc(S["actT_ready"], 1)
            step(a.activation(warm, eps, ACT.Sqrt))
            for t in range(TT):
                half_sums(x_sb, lambda t, s: h2[:, t, s], t, "x2_ready", "sqrt_x2")

        @block.gpsimd
        def _(g):
            step = Chain(g, "pool_chain")
            g.memset(w_ba[:, :, :], 0.0).then_inc(S["ba_zero"], 1)
            wait_full(g, "params")
            step(g.memset(lru_ws[:, 0:1024], 0.0))
            wait_evac(g, "modcol")
            for dst, src in ((wa_bd, lru_w_a), (wx_bd, lru_w_x)):
                pairs = src[0].rearrange("(j two) c d -> two c j d", two=2)
                for i in range(2):
                    g.dma_start(dst[64 * i:64 * i + 64, :, 64 * i:64 * i + 64], pairs[i]).then_inc(S["gate_w_in"], 16)
            for n in (8, 9):
                wait_evac(g, f"in{n}")
            step(g.tensor_tensor(lru_a, ybT[:, :, :], ybT[:, :, :], ALU.mult))
            step(g.tensor_scalar(lru_a, lru_a, GELU_A, 1.0, ALU.mult, ALU.add))
            g.tensor_tensor(lru_a, lru_a, ybT[:, :, :], ALU.mult).then_inc(S["yb_arg"], 1)
            g.wait_ge(S["yb_sig"], 1)
            g.tensor_tensor(ybT[:, :, :], ybT[:, :, :], lru_a, ALU.mult).then_inc(S["yb_done"], 1)
            g.wait_ge(S["masks_in"], 16)
            def mask(level):
                for t in range(TT):
                    if level == 1:
                        wait_evac(g, f"kk{t}")
                    else:
                        wait_full(g, f"X{level - 1}_{t}")
                    g.tensor_tensor(BM[:, t, :].rearrange("p (h c) -> p h c", h=HEADS),
                                    Bm[:, t, :].rearrange("p (h c) -> p h c", h=HEADS), level_mask(level), ALU.mult)\
                        .then_inc(S["mask_ready"], 1)
            for n in range(2):
                wait_evac(g, f"lru_i{n}")
            step(g.tensor_tensor(lru_i, lru_i, xcT[:, :, :], ALU.mult))
            mask(1)
            g.wait_ge(S["lru_exp"], 1)
            step(g.tensor_tensor(xcT[:, :, :], lru_a, lru_a, ALU.mult))
            step(g.tensor_scalar(xcT[:, :, :], xcT[:, :, :], 1.0, None, ALU.add))
            mask(2)
            step(g.tensor_tensor(xcT[:, :, :], xcT[:, :, :], lru_r, ALU.mult))
            g.tensor_scalar(xcT[:, :, :], xcT[:, :, :], -1.0, 0.0, ALU.mult, ALU.max).then_inc(S["lru_m"], 1)
            mask(3)
            g.wait_ge(S["lru_sqrt"], 1)
            g.tensor_tensor(lru_i, lru_i, xcT[:, :, :], ALU.mult).then_inc(S["lru_b"], 1)
            for level in range(4, LEVELS):
                mask(level)


INPUTS = ["x", "c", "w_ada", "b_ada", "norm_mix", "norm_ffn", "w_in", "gdn_conv_w", "gdn_a_log", "gdn_dt_bias",
          "gdn_norm_w", "lru_conv_w", "lru_conv_b", "lru_w_a", "lru_b_a", "lru_w_x", "lru_b_x", "lru_lambda",
          "w_branch_gdn", "w_branch_lru", "w_out", "w_router", "b_router", "w1", "b1", "w2", "b2", "norm_final"]


def kernel(**inputs):
    import concourse.bacc as bacc
    from concourse.bass_utils import run_bass_kernel_spmd

    nc = bacc.Bacc("TRN2", target_bir_lowering=False, num_devices=1)
    arrays, args = {}, []
    for name in INPUTS:
        arrays[f"in_{name}"] = np.ascontiguousarray(inputs[name])
    arrays["in_consts"] = constants()
    for name, a in arrays.items():
        args.append(nc.dram_tensor(name, a.shape, mybir.dt.from_np(a.dtype), kind="ExternalInput").ap())
    args.append(nc.dram_tensor("out_x", (1, SEQ, D), F32, kind="ExternalOutput").ap())
    hybrid_block(nc, *args)
    return run_bass_kernel_spmd(nc, [arrays], core_ids=[0]).results[0]["out_x"]
```
